# Optimizing a Trainium2 kernel written in Bass

```python
import jax, jax.numpy as jnp
from jax import lax
import numpy as np

D_MODEL = 1024
BATCH = 1
SEQ = 512
DEPTH = 1
DEC_BATCH = 8
DEC_SEQ = 8
PAST_LEN = 2048
PAGE_SIZE = 128

HEAD_DIM = 64
N_HEADS_A = 8
N_HEADS_B = 8
D_A = N_HEADS_A * HEAD_DIM
D_B = N_HEADS_B * HEAD_DIM
DECAY_LORA = 64
AAA_LORA = 64
GATE_LORA = 128
D_FF = 2816
Q_BLOCK = 128
NORM_EPS = 1e-6
LNX_EPS = 64e-5
N_SHIFT = 3 * D_A + DECAY_LORA + AAA_LORA + GATE_LORA
N_IN = N_SHIFT + 3 * D_B + N_HEADS_B + 2 * D_MODEL

kernel_name = "rwkv7_fox_gated_hybrid_step"

def rms_norm(x, g, eps=NORM_EPS):
    xf = x.astype(jnp.float32)
    y = xf * lax.rsqrt(jnp.mean(xf * xf, axis=-1, keepdims=True) + eps)
    return (y * g.astype(jnp.float32)).astype(x.dtype)

def swiglu_ffn(x, g, wg, wu, wd):
    h = rms_norm(x, g)
    return (jax.nn.silu(h @ wg) * (h @ wu)) @ wd

def rwkv7_branch(p_a, prev, S0, mu, w0, w2, a0, a2, g2, k_k, k_a, r_k, lnx_w, lnx_b):
    B, T, _ = p_a.shape
    H, Dh = N_HEADS_A, HEAD_DIM
    f32 = jnp.float32
    p_prev = jnp.concatenate([prev[:, None, :].astype(p_a.dtype), p_a[:, :-1]], axis=1)
    xm = p_a + (p_prev - p_a) * mu
    o1, o2, o3 = D_A, 2 * D_A, 3 * D_A
    o4 = o3 + DECAY_LORA
    o5 = o4 + AAA_LORA
    r, k, v, xw, xa, xg = jnp.split(xm, [o1, o2, o3, o4, o5], axis=-1)
    w_log = -jax.nn.softplus(-(w0 + jnp.tanh(xw) @ w2).astype(f32)) - 0.5
    decay = jnp.exp(-jnp.exp(w_log))
    a = jax.nn.sigmoid((a0 + xa @ a2).astype(f32))
    g = jax.nn.sigmoid(xg) @ g2
    heads = lambda t: t.reshape(B, T, H, Dh).astype(f32)
    r, k, v, decay, a = heads(r), heads(k), heads(v), heads(decay), heads(a)
    kk = k * k_k.reshape(H, Dh).astype(f32)
    kk = kk / jnp.maximum(jnp.sqrt(jnp.sum(kk * kk, axis=-1, keepdims=True)), 1e-12)
    k = k * (1.0 + (a - 1.0) * k_a.reshape(H, Dh).astype(f32))

    def step(S, inp):
        r_t, w_t, k_t, v_t, kk_t, a_t = inp
        sa = jnp.einsum('bhvk,bhk->bhv', S, -kk_t)
        S = (S * w_t[:, :, None, :] + sa[..., None] * (kk_t * a_t)[:, :, None, :]
             + v_t[..., None] * k_t[:, :, None, :])
        return S, jnp.einsum('bhvk,bhk->bhv', S, r_t)

    tm = lambda t: jnp.moveaxis(t, 1, 0)
    S_fin, y = lax.scan(step, S0.astype(f32), (tm(r), tm(decay), tm(k), tm(v), tm(kk), tm(a)))
    y = jnp.moveaxis(y, 0, 1)
    mean = jnp.mean(y, axis=-1, keepdims=True)
    var = jnp.mean(jnp.square(y - mean), axis=-1, keepdims=True)
    y = ((y - mean) * lax.rsqrt(var + LNX_EPS) * lnx_w.reshape(H, Dh).astype(f32)
         + lnx_b.reshape(H, Dh).astype(f32))
    y = y + jnp.sum(r * k * r_k.astype(f32), axis=-1, keepdims=True) * v
    y = y.reshape(B, T, D_A).astype(p_a.dtype) * g
    return y, p_a[:, -1], S_fin.astype(S0.dtype)

def fox_prompt(q, k, v, logf):
    B, S, H, Dh = q.shape
    scale = 1.0 / float(np.sqrt(HEAD_DIM))
    C = jnp.cumsum(logf.astype(jnp.float32), axis=1).transpose(0, 2, 1)
    kpos = jnp.arange(S)

    def block(i):
        start = i * Q_BLOCK
        qb = lax.dynamic_slice_in_dim(q, start, Q_BLOCK, axis=1)
        cb = lax.dynamic_slice_in_dim(C, start, Q_BLOCK, axis=2)
        s = (jnp.einsum('bqhd,bkhd->bhqk', qb, k).astype(jnp.float32) * scale
             + cb[..., None] - C[:, :, None, :])
        qpos = start + jnp.arange(Q_BLOCK)
        s = jnp.where(qpos[:, None] >= kpos[None, :], s, -jnp.inf)
        p = jax.nn.softmax(s, axis=-1).astype(v.dtype)
        return jnp.einsum('bhqk,bkhd->bqhd', p, v)

    o = lax.map(block, jnp.arange(S // Q_BLOCK))
    return o.transpose(1, 0, 2, 3, 4).reshape(B, S, H * Dh)

def fox_sample(q, k, v, logf, pk, pv, plogf):
    B, T, H, Dh = q.shape
    f32 = jnp.float32
    scale = 1.0 / float(np.sqrt(HEAD_DIM))
    Cn = jnp.cumsum(logf.astype(f32), axis=1).transpose(0, 2, 1)
    plf = plogf.astype(f32)
    suffix = (lax.cumsum(plf, axis=1, reverse=True) - plf).transpose(0, 2, 1)
    s_past = (jnp.einsum('bqhd,bkhd->bhqk', q, pk).astype(f32) * scale
              + Cn[..., None] + suffix[:, :, None, :])
    s_new = (jnp.einsum('bqhd,bkhd->bhqk', q, k).astype(f32) * scale
             + Cn[..., None] - Cn[:, :, None, :])
    tpos = jnp.arange(T)
    s_new = jnp.where(tpos[:, None] >= tpos[None, :], s_new, -jnp.inf)
    P = pk.shape[1]
    p = jax.nn.softmax(jnp.concatenate([s_past, s_new], axis=-1), axis=-1).astype(v.dtype)
    o = jnp.einsum('bhqk,bkhd->bqhd', p[..., :P], pv) + jnp.einsum('bhqk,bkhd->bqhd', p[..., P:], v)
    return o.reshape(B, T, H * Dh)

def layer(x, prev_shift, S0, past, lw):
    (ffn1_norm, ffn1_wg, ffn1_wu, ffn1_wd, mix_norm, w_in, shift_mu,
     rwkv_w0, rwkv_w2, rwkv_a0, rwkv_a2, rwkv_g2, rwkv_k_k, rwkv_k_a, rwkv_r_k, rwkv_lnx_w, rwkv_lnx_b,
     fox_b_f, fox_q_norm, fox_k_norm, w_o_a, w_o_b, w_out,
     ffn2_norm, ffn2_wg, ffn2_wu, ffn2_wd) = lw
    B, T, _ = x.shape
    x = x + 0.5 * swiglu_ffn(x, ffn1_norm, ffn1_wg, ffn1_wu, ffn1_wd)
    h = rms_norm(x, mix_norm)
    p = h @ w_in
    c1 = N_SHIFT
    c2 = c1 + D_B
    c3 = c2 + D_B
    c4 = c3 + D_B
    c5 = c4 + N_HEADS_B
    c6 = c5 + D_MODEL
    p_a, q, k, v, f_logit, g_a, g_b = jnp.split(p, [c1, c2, c3, c4, c5, c6], axis=-1)
    y_a, new_shift, new_S = rwkv7_branch(p_a, prev_shift, S0, shift_mu, rwkv_w0, rwkv_w2, rwkv_a0, rwkv_a2,
                                         rwkv_g2, rwkv_k_k, rwkv_k_a, rwkv_r_k, rwkv_lnx_w, rwkv_lnx_b)
    q = rms_norm(q.reshape(B, T, N_HEADS_B, HEAD_DIM), fox_q_norm)
    k = rms_norm(k.reshape(B, T, N_HEADS_B, HEAD_DIM), fox_k_norm)
    v = v.reshape(B, T, N_HEADS_B, HEAD_DIM)
    logf = jax.nn.log_sigmoid(f_logit.astype(jnp.float32) + fox_b_f.astype(jnp.float32))
    if past is None:
        y_b = fox_prompt(q, k, v, logf)
    else:
        pk, pv, plogf = past
        y_b = fox_sample(q, k, v, logf, pk, pv, plogf)
    merged = jax.nn.sigmoid(g_a) * (y_a @ w_o_a) + jax.nn.sigmoid(g_b) * (y_b @ w_o_b)
    x = x + merged @ w_out
    x = x + 0.5 * swiglu_ffn(x, ffn2_norm, ffn2_wg, ffn2_wu, ffn2_wd)
    return x, (k, v, logf.astype(x.dtype), new_S, new_shift)

def setup_inputs(seed: int = 0) -> dict:
    key = jax.random.key(seed)
    ks = iter(jax.random.split(key, 64))
    f32 = jnp.float32
    nrm = lambda shape, scale: scale * jax.random.normal(next(ks), shape, f32)
    L = DEPTH
    n_pages = PAST_LEN // PAGE_SIZE
    n_pool = (DEC_BATCH * n_pages * 5) // 4
    d_in = D_MODEL ** -0.5
    inp = {}
    inp["x_prompt"] = nrm((BATCH, SEQ, D_MODEL), 1.0)
    inp["x_sample"] = nrm((DEC_BATCH, DEC_SEQ, D_MODEL), 1.0)
    inp["cache_k"] = nrm((L, n_pool, PAGE_SIZE, N_HEADS_B, HEAD_DIM), 1.0)
    inp["cache_v"] = nrm((L, n_pool, PAGE_SIZE, N_HEADS_B, HEAD_DIM), 1.0)
    inp["cache_logf"] = jax.nn.log_sigmoid(3.0 + nrm((L, n_pool, PAGE_SIZE, N_HEADS_B), 0.5))
    inp["state_wkv"] = nrm((L, DEC_BATCH, N_HEADS_A, HEAD_DIM, HEAD_DIM), 0.1)
    inp["state_shift"] = nrm((L, DEC_BATCH, N_SHIFT), 1.0)
    perm = jax.random.permutation(next(ks), n_pool)
    inp["page_table"] = perm[:DEC_BATCH * n_pages].reshape(DEC_BATCH, n_pages).astype(jnp.int32)
    gain = lambda n: 1.0 + nrm((L, n), 0.05)
    inp["ffn1_norm"] = gain(D_MODEL)
    inp["ffn1_wg"] = nrm((L, D_MODEL, D_FF), d_in)
    inp["ffn1_wu"] = nrm((L, D_MODEL, D_FF), d_in)
    inp["ffn1_wd"] = nrm((L, D_FF, D_MODEL), D_FF ** -0.5)
    inp["mix_norm"] = gain(D_MODEL)
    inp["w_in"] = nrm((L, D_MODEL, N_IN), d_in)
    inp["shift_mu"] = jax.random.uniform(next(ks), (L, N_SHIFT), f32)
    inp["rwkv_w0"] = -2.0 + nrm((L, D_A), 1.0)
    inp["rwkv_w2"] = nrm((L, DECAY_LORA, D_A), 0.5 * DECAY_LORA ** -0.5)
    inp["rwkv_a0"] = nrm((L, D_A), 0.1)
    inp["rwkv_a2"] = nrm((L, AAA_LORA, D_A), 0.5 * AAA_LORA ** -0.5)
    inp["rwkv_g2"] = nrm((L, GATE_LORA, D_A), GATE_LORA ** -0.5)
    inp["rwkv_k_k"] = 0.85 + nrm((L, D_A), 0.05)
    inp["rwkv_k_a"] = 1.0 + nrm((L, D_A), 0.05)
    inp["rwkv_r_k"] = nrm((L, N_HEADS_A, HEAD_DIM), 0.1)
    inp["rwkv_lnx_w"] = gain(D_A)
    inp["rwkv_lnx_b"] = nrm((L, D_A), 0.02)
    inp["fox_b_f"] = 3.0 + nrm((L, N_HEADS_B), 0.5)
    inp["fox_q_norm"] = gain(HEAD_DIM)
    inp["fox_k_norm"] = gain(HEAD_DIM)
    inp["w_o_a"] = nrm((L, D_A, D_MODEL), D_A ** -0.5)
    inp["w_o_b"] = nrm((L, D_B, D_MODEL), D_B ** -0.5)
    inp["w_out"] = nrm((L, D_MODEL, D_MODEL), d_in)
    inp["ffn2_norm"] = gain(D_MODEL)
    inp["ffn2_wg"] = nrm((L, D_MODEL, D_FF), d_in)
    inp["ffn2_wu"] = nrm((L, D_MODEL, D_FF), d_in)
    inp["ffn2_wd"] = nrm((L, D_FF, D_MODEL), D_FF ** -0.5)
    return inp

def reference(x_prompt, x_sample, cache_k, cache_v, cache_logf, state_wkv, state_shift, page_table,
              ffn1_norm, ffn1_wg, ffn1_wu, ffn1_wd, mix_norm, w_in, shift_mu,
              rwkv_w0, rwkv_w2, rwkv_a0, rwkv_a2, rwkv_g2, rwkv_k_k, rwkv_k_a, rwkv_r_k, rwkv_lnx_w, rwkv_lnx_b,
              fox_b_f, fox_q_norm, fox_k_norm, w_o_a, w_o_b, w_out,
              ffn2_norm, ffn2_wg, ffn2_wu, ffn2_wd):
    Bp = x_prompt.shape[0]
    Bd = x_sample.shape[0]
    n_pages = page_table.shape[1]
    past_len = n_pages * PAGE_SIZE
    xp, xs = x_prompt, x_sample
    pk_l, pv_l, pf_l, pS_l, psh_l = [], [], [], [], []
    sk_l, sv_l, sf_l, sS_l, ssh_l = [], [], [], [], []
    for l in range(DEPTH):
        lw = (ffn1_norm[l], ffn1_wg[l], ffn1_wu[l], ffn1_wd[l], mix_norm[l], w_in[l], shift_mu[l],
              rwkv_w0[l], rwkv_w2[l], rwkv_a0[l], rwkv_a2[l], rwkv_g2[l], rwkv_k_k[l], rwkv_k_a[l], rwkv_r_k[l],
              rwkv_lnx_w[l], rwkv_lnx_b[l], fox_b_f[l], fox_q_norm[l], fox_k_norm[l], w_o_a[l], w_o_b[l], w_out[l],
              ffn2_norm[l], ffn2_wg[l], ffn2_wu[l], ffn2_wd[l])
        prev0 = jnp.zeros((Bp, N_SHIFT), xp.dtype)
        S00 = jnp.zeros((Bp, N_HEADS_A, HEAD_DIM, HEAD_DIM), xp.dtype)
        xp, (k_p, v_p, f_p, S_p, sh_p) = layer(xp, prev0, S00, None, lw)
        pk = cache_k[l][page_table].reshape(Bd, past_len, N_HEADS_B, HEAD_DIM)
        pv = cache_v[l][page_table].reshape(Bd, past_len, N_HEADS_B, HEAD_DIM)
        plf = cache_logf[l][page_table].reshape(Bd, past_len, N_HEADS_B)
        xs, (k_s, v_s, f_s, S_s, sh_s) = layer(xs, state_shift[l], state_wkv[l], (pk, pv, plf), lw)
        pk_l.append(k_p); pv_l.append(v_p); pf_l.append(f_p); pS_l.append(S_p); psh_l.append(sh_p)
        sk_l.append(k_s); sv_l.append(v_s); sf_l.append(f_s); sS_l.append(S_s); ssh_l.append(sh_s)
    prompt_k = jnp.stack(pk_l, 0)
    prompt_v = jnp.stack(pv_l, 0)
    prompt_logf = jnp.stack(pf_l, 0)
    prompt_wkv = jnp.stack(pS_l, 0)
    prompt_shift = jnp.stack(psh_l, 0)
    sample_k = jnp.stack(sk_l, 0)
    sample_v = jnp.stack(sv_l, 0)
    sample_logf = jnp.stack(sf_l, 0)
    sample_wkv = jnp.stack(sS_l, 0)
    sample_shift = jnp.stack(ssh_l, 0)
    return (xp, xs, prompt_k, prompt_v, prompt_logf, prompt_wkv, prompt_shift,
            sample_k, sample_v, sample_logf, sample_wkv, sample_shift)


_drawn_inputs = setup_inputs


def setup_inputs(seed=0):
    import zlib

    import numpy as np

    out = dict(_drawn_inputs(seed))
    spreads = {}
    factors = {'cache_logf': 7.542,
     'rwkv_lnx_w': 4.458,
     'rwkv_lnx_b': 8.0,
     'fox_q_norm': 8.0,
     'ffn2_norm': 3.044}
    for name, (base, spread) in spreads.items():
        noise = np.random.default_rng([zlib.crc32(name.encode()), seed]).standard_normal(out[name].shape)
        drawn = base * np.exp(spread * noise) if base else spread * noise
        out[name] = __import__('jax').numpy.asarray(drawn.astype(out[name].dtype))
    for name, factor in factors.items():
        out[name] = (out[name] * factor).astype(out[name].dtype)
    return out
```

```python
from contextlib import ExitStack

import numpy as np

import concourse.bass as bass
from concourse import mybir

F32 = mybir.dt.float32
F32R = mybir.dt.float32r
I32 = mybir.dt.int32
ACT = mybir.ActivationFunctionType
ALU = mybir.AluOpType
AX = mybir.AxisListType

P = 128
D = 1024
DK = D // P
SEQ = 512
NB, NT = 8, 8
TOK = SEQ + NB * NT
HALF = TOK // 2
DH = 64
NH = 8
FT = NH * DH // P
D_FF = 2816
UP = (12, 10)
N_SH = 14
N_P = 27
N_GATE = 16
CH = 128
NCH = SEQ // CH
PAGES = 16
PAGE = 128
NPOOL = 160
KAPPA = float(np.exp(-0.5))
NORM_EPS, LNX_EPS = 1e-6, 64e-5
NEG = -1e30
KROW = FT * PAGE + NH
SLOTK = 12

PC_COLS = dict(n1=8, n2=8, n3=8, mu=14, w0=4, a0=4, kk=4, ka=4, rk=4, lnw=4, lnb=4, qn=1, kn=1, bf=1, sc=1, ad=1)
CC_COLS = dict(ident=P, low=2 * P, lows=P, lev=7 * P, tri=P, causal=P, mnew=64, bmask=NB, sel8=FT * NH, selt8=FT * P)
CC2_COLS = dict(sel24=12 * 24, selt=12 * P, reset=TOK, fresh=TOK)


def columns(widths):
    at, out = 0, {}
    for name, n in widths.items():
        out[name] = at
        at += n
    return out, at


CCOL, N_CCOL = columns(CC_COLS)
CCOL2, N_CCOL2 = columns(CC2_COLS)
PCOL, N_PCOL = columns(PC_COLS)


class Tile:

    def __init__(self, first, i, j):
        self.n = 4 * i + j
        self.t = first + self.n
        self.slot = (first + j) % 4
        self.pair = (first + j) % 2
        self.use = i + (first + j) // 4
        self.couple = 2 * i + j // 2
        self.twin = j // 2 % 2
        self.odd = j % 2
        self.turn = i


def tiles(eng, first, count):
    turns = count // 4
    if turns > 1:
        with eng.Fori(0, turns) as i:
            for j in range(4):
                yield Tile(first, i, j)
    elif turns:
        for j in range(4):
            yield Tile(first, 0, j)
    for j in range(count % 4):
        yield Tile(first, turns, j)


class Chain:

    def __init__(self, eng, sem):
        self.eng, self.sem, self.n, self.turn, self.inside = eng, sem, 0, None, 0

    def __call__(self, ins):
        self.n += 1
        ins.then_inc(self.sem, 1)
        self.eng.wait_ge(self.sem, self.n if self.turn is None else self.turn + self.n)

    def loop(self, i, per):
        self.before, self.per, self.n, self.turn = self.n, per, 0, i * per + self.n

    def end(self, turns):
        assert self.n == self.per, (self.sem, self.n, self.per)
        self.n, self.turn = self.before + turns * self.per, None


class Semaphores:

    def __init__(self, nc):
        self.nc, self.held = nc, []

    def __call__(self, name):
        self.held.append(self.nc.alloc_semaphore(name=name))
        return self.held[-1]

    def __enter__(self):
        return self

    def __exit__(self, kind, error, trace):
        if kind is None:
            self.nc.clear_and_free_semaphores(self.held)
            self.nc.all_engine_barrier()


class Dense:

    def __init__(self, sems, nc):
        self.nc = nc
        sem = sems
        self.landed = [sem(f"w_landed{s}") for s in range(4)]
        self.rounded = sem("w_rounded")
        self.split_done = sem("w_split")
        self.mm_done = sem("w_multiplied")
        self.evacuated = sem("w_evacuated")
        self.t = 0

    def buffers(self, ctx, tag, k=SLOTK, raw=None):
        nc = self.nc
        sb = lambda n, s, d: ctx.enter_context(nc.sbuf_tensor(n, s, d))
        self.raw = sb("w_raw" + tag, [P, 4, k, P], F32) if raw is None else raw
        self.wh = sb("w_hi" + tag, [P, 2, k, P], F32R)
        self.wl = sb("w_lo" + tag, [P, 2, k, P], F32R)
        self.ps = ctx.enter_context(nc.psum_tensor("ps" + tag, [P, 4, 2, 512], F32))

    def stage(self, count):
        first, self.t = self.t, self.t + count
        return first, count

    def seed(self, sp):
        sp.nop().then_inc(self.split_done, 4)
        sp.nop().then_inc(self.mm_done, 4)
        sp.nop().then_inc(self.evacuated, 4)

    def load(self, sp, st, kn, src):
        for x in tiles(sp, *st):
            sp.wait_ge(self.split_done, x.t + 1)
            sp.dma_start(self.raw[:, x.slot, 0:kn], src(x.n)).then_inc(self.landed[x.slot], 16)

    def split(self, dve, st, kn):
        for x in tiles(dve, *st):
            dve.wait_ge(self.landed[x.slot], 16 * x.use + 16)
            dve.wait_ge(self.mm_done, x.t + 3)
            hi, lo, raw = self.wh[:, x.pair, 0:kn], self.wl[:, x.pair, 0:kn], self.raw[:, x.slot, 0:kn]
            self.nc.vector.tensor_copy(hi, raw).then_inc(self.rounded, 1)
            dve.wait_ge(self.rounded, x.t + 1)
            self.nc.vector.tensor_tensor(lo, raw, hi.bitcast(F32), ALU.subtract).then_inc(self.split_done, 1)

    def multiply(self, pe, st, groups):
        for x in tiles(pe, *st):
            pe.wait_ge(self.split_done, x.t + 5)
            pe.wait_ge(self.evacuated, x.t + 1)
            for out, k0, operands in groups(x):
                for half in range(2):
                    cut = slice(half * HALF, (half + 1) * HALF)
                    for k, (hi, lo) in enumerate(operands):
                        wh, wl = self.wh[:, x.pair, k0 + k], self.wl[:, x.pair, k0 + k]
                        self.nc.tensor.matmul(out(half), wh, hi[:, cut], start=k == 0, stop=False)
                        self.nc.tensor.matmul(out(half), wh, lo[:, cut], start=False, stop=False)
                        last = self.nc.tensor.matmul(out(half), wl, hi[:, cut], start=False,
                                                     stop=k == len(operands) - 1)
            last.then_inc(self.mm_done, 1)

    def whole(self, hi, lo, kn):
        ops = [(hi[:, k], lo[:, k]) for k in range(kn)]
        return lambda x: [(lambda half: self.ps[:, x.slot, half, 0:HALF], 0, ops)]

    def out(self, x):
        return self.ps[:, x.slot, :, 0:HALF]


def halves(ap):
    return ap.rearrange("p (h n) -> p h n", h=2)


class Norm:

    BLOCKS = [(j * P, j * P, j * P + P) for j in range(SEQ // P)] + [(TOK - P, SEQ, TOK)]

    def __init__(self, ctx, sems, nc, tag, x, gain, consts, nh, nl, ps):
        sb = lambda n, s, d=F32: ctx.enter_context(nc.sbuf_tensor(n + tag, s, d))
        sem = lambda n: sems(n + tag)
        self.nc, self.x, self.gain, self.consts, self.nh, self.nl, self.ps = nc, x, gain, consts, nh, nl, ps
        self.sq = sb("n_sq", [P, 2, TOK])
        self.sum = sb("n_sum", [P, TOK])
        self.rs = sb("n_rs", [P, 8])
        self.y = sb("n_y", [P, 2, TOK])
        self.squared, self.added, self.summed, self.meaned = sem("n_squared"), sem("n_added"), sem("n_summed"), sem("n_meaned")
        self.rooted, self.inverted, self.spread = sem("n_rooted"), sem("n_inverted"), sem("n_spread")
        self.scaled, self.high, self.split = sem("n_scaled"), sem("n_high"), sem("n_split")

    def act(self, act):
        nc = self.nc
        for k in range(DK):
            if k >= 2:
                act.wait_ge(self.added, k - 1)
            nc.scalar.activation(self.sq[:, k % 2], self.x[:, k], ACT.Square).then_inc(self.squared, 1)
        act.wait_ge(self.meaned, 1)
        nc.scalar.activation(self.rs[:, 0:5], self.ps[:, 0, 0, 0:5], ACT.Sqrt, scale=1.0 / D,
                             bias=self.consts["eps"]).then_inc(self.rooted, 1)
        for k in range(DK):
            act.wait_ge(self.scaled, k + 1)
            nc.scalar.activation(self.nh[:, k], self.y[:, k % 2], ACT.Copy).then_inc(self.high, 1)

    def pe(self, pe):
        nc = self.nc
        pe.wait_ge(self.summed, 1)
        for j, (a, _, _) in enumerate(self.BLOCKS):
            mm = nc.tensor.matmul(self.ps[:, 0, 0, j:j + 1], self.sum[:, a:a + P],
                                  self.consts["ones"][:, 0:1], start=True, stop=True)
        mm.then_inc(self.meaned, 1)
        pe.wait_ge(self.inverted, 1)
        for j, (at, lo, hi) in enumerate(self.BLOCKS):
            for a, b in ((lo, min(hi, HALF)), (max(lo, HALF), hi)):
                if b > a:
                    h, o = divmod(a, HALF)
                    mm = nc.tensor.matmul(self.ps[:, 1, h, o:o + b - a], self.rs[:, j:j + 1].broadcast_to([P, P]),
                                          self.consts["ident"][:, a - at:b - at], start=True, stop=True)
        mm.then_inc(self.spread, 1)

    def dve(self, dve):
        nc = self.nc
        for k in range(DK):
            dve.wait_ge(self.squared, k + 1)
            if k:
                dve.wait_ge(self.added, k)
                nc.vector.tensor_tensor(self.sum[:], self.sum[:], self.sq[:, k % 2], ALU.add).then_inc(self.added, 1)
            else:
                nc.vector.tensor_copy(self.sum[:], self.sq[:, 0]).then_inc(self.added, 1)
        dve.wait_ge(self.added, DK)
        dve.nop().then_inc(self.summed, 1)
        dve.wait_ge(self.rooted, 1)
        nc.vector.reciprocal(self.rs[:, 0:5], self.rs[:, 0:5]).then_inc(self.inverted, 1)
        dve.wait_ge(self.spread, 1)
        for k in range(DK):
            if k >= 2:
                dve.wait_ge(self.split, k - 1)
            nc.vector.scalar_tensor_tensor(halves(self.y[:, k % 2]), halves(self.x[:, k]), self.gain[:, k:k + 1],
                                           self.ps[:, 1, :, 0:HALF], ALU.mult, ALU.mult).then_inc(self.scaled, 1)
            if k:
                self.low(dve, k - 1)
        self.low(dve, DK - 1)

    def low(self, dve, k):
        dve.wait_ge(self.high, k + 1)
        self.nc.vector.tensor_tensor(self.nl[:, k], self.y[:, k % 2], self.nh[:, k].bitcast(F32),
                                     ALU.subtract).then_inc(self.split, 1)


def ffn(sems, nc, dense, tag, x, gain, consts, w_up, w_down, load_first=None, store=None):
    with ExitStack() as ctx:
        sb = lambda n, s, d=F32: ctx.enter_context(nc.sbuf_tensor(n + tag, s, d))
        sem = lambda n: sems(n + tag)
        dense.buffers(ctx, tag)
        nh, nl = sb("f_nh", [P, DK, TOK], F32R), sb("f_nl", [P, DK, TOK], F32R)
        hh, hl = sb("f_hh", [P, UP[0], TOK], F32R), sb("f_hl", [P, UP[0], TOK], F32R)
        gate, up, y = sb("f_gate", [P, 2, TOK]), sb("f_up", [P, 2, TOK]), sb("f_y", [P, 2, TOK])
        norm = Norm(ctx, sems, nc, tag, x, gain, consts, nh, nl, dense.ps)
        hid_link, hid_split, y_added = sem("hid_link"), sem("hid_split"), sem("y_added")
        x_loaded, x_stored = sem("x_loaded"), sem("x_stored")
        stages = []
        for n in UP:
            stages += [dense.stage(2 * n), dense.stage(DK)]
        before = [0, UP[0]]

        def wait_x(eng):
            if load_first is not None:
                eng.wait_ge(x_loaded, load_first.count)

        block = ctx.enter_context(nc.Block())

        @block.sync
        def _(sp):
            if load_first is not None:
                load_first(sp, x_loaded)
            for half, n in enumerate(UP):
                src = w_up[2 * before[half]:2 * before[half] + 2 * n]
                dense.load(sp, stages[2 * half], DK, lambda t: src[bass.ds(t, 1)].rearrange("a p k n -> p (a k) n"))
                down = w_down[half]
                dense.load(sp, stages[2 * half + 1], n, lambda t: down[bass.ds(t, 1)].rearrange("a p k n -> p (a k) n"))
            if store is not None:
                sp.wait_ge(y_added, 2 + 2 * DK)
                store(sp, x_stored)

        @block.vector
        def _(dve):
            wait_x(dve)
            norm.dve(dve)
            for half, n in enumerate(UP):
                dense.split(dve, stages[2 * half], DK)
                dense.split(dve, stages[2 * half + 1], n)

        @block.scalar
        def _(act):
            wait_x(act)
            norm.act(act)
            for half, n in enumerate(UP):
                for t in tiles(act, *stages[2 * half]):
                    act.wait_ge(dense.mm_done, t.t + 5)
                    if not t.odd:
                        act.wait_ge(hid_split, before[half] + t.couple + 1)
                    buf, func = ((gate, ACT.Silu), (up, ACT.Copy))[t.odd]
                    nc.scalar.activation(halves(buf[:, t.twin]), dense.out(t), func).then_inc(dense.evacuated, 1)
                for t in tiles(act, *stages[2 * half + 1]):
                    act.wait_ge(dense.mm_done, t.t + 5)
                    act.wait_ge(y_added, DK * half + t.n + 1)
                    nc.scalar.activation(halves(y[:, t.odd]), dense.out(t), ACT.Copy, scale=0.5)\
                        .then_inc(dense.evacuated, 1)

        @block.gpsimd
        def _(pool):
            pool.nop().then_inc(hid_split, 2)
            pool.nop().then_inc(y_added, 2)
            wait_x(pool)
            for half, n in enumerate(UP):
                if half:
                    pool.wait_ge(dense.mm_done, stages[2][0] + 4)
                for t in tiles(pool, *stages[2 * half]):
                    if not t.odd:
                        continue
                    pool.wait_ge(dense.evacuated, t.t + 5)
                    c = before[half] + t.couple
                    k, b = bass.ds(t.couple, 1), slice(t.twin, t.twin + 1)
                    nc.gpsimd.tensor_tensor(up[:, b], gate[:, b], up[:, b], ALU.mult).then_inc(hid_link, 1)
                    pool.wait_ge(hid_link, 2 * c + 1)
                    nc.gpsimd.tensor_copy(hh[:, k], up[:, b]).then_inc(hid_link, 1)
                    pool.wait_ge(hid_link, 2 * c + 2)
                    nc.gpsimd.tensor_tensor(hl[:, k], up[:, b], hh[:, k].bitcast(F32), ALU.subtract)\
                        .then_inc(hid_split, 1)
                for t in tiles(pool, *stages[2 * half + 1]):
                    pool.wait_ge(dense.evacuated, t.t + 5)
                    xn = x[:, bass.ds(t.n, 1)]
                    nc.gpsimd.tensor_tensor(xn, y[:, t.odd:t.odd + 1], xn, ALU.add).then_inc(y_added, 1)

        @block.tensor
        def _(pe):
            wait_x(pe)
            norm.pe(pe)
            pe.wait_ge(norm.split, DK)
            for half, n in enumerate(UP):
                dense.multiply(pe, stages[2 * half], dense.whole(nh, nl, DK))
                pe.wait_ge(hid_split, 2 + before[half] + n)
                dense.multiply(pe, stages[2 * half + 1], dense.whole(hh, hl, n))


def project(sems, nc, dense, x, gain, consts, w_in, pb, gates_dram, x_dram):
    with ExitStack() as ctx:
        sb = lambda n, s, d=F32: ctx.enter_context(nc.sbuf_tensor(n, s, d))
        sem = sems
        dense.buffers(ctx, "_p")
        nh, nl = sb("p_nh", [P, DK, TOK], F32R), sb("p_nl", [P, DK, TOK], F32R)
        gate = sb("p_gate", [P, 2, TOK])
        norm = Norm(ctx, sems, nc, "_p", x, gain, consts, nh, nl, dense.ps)
        gate_stored = [sem("gate_stored0"), sem("gate_stored1")]
        x_saved = sem("x_saved")
        plain, gates = dense.stage(N_P), dense.stage(N_GATE)
        block = ctx.enter_context(nc.Block())

        @block.sync
        def _(sp):
            sp.dma_start(x_dram, x[:]).then_inc(x_saved, 16)
            dense.load(sp, plain, DK, lambda n: w_in[bass.ds(n, 1)].rearrange("a p k n -> p (a k) n"))
            dense.load(sp, gates, DK, lambda n: w_in[N_P:][bass.ds(n, 1)].rearrange("a p k n -> p (a k) n"))
            sp.wait_ge(x_saved, 16)

        @block.gpsimd
        def _(pool):
            for s in gate_stored:
                pool.nop().then_inc(s, 16)

        @block.vector
        def _(dve):
            norm.dve(dve)
            dense.split(dve, plain, DK)
            dense.split(dve, gates, DK)

        @block.scalar
        def _(act):
            norm.act(act)
            for t in tiles(act, *plain):
                act.wait_ge(dense.mm_done, t.t + 5)
                out = pb[:, bass.ds(t.n, 1)].rearrange("p a (h n) -> p (a h) n", h=2)
                nc.scalar.activation(out, dense.out(t), ACT.Copy).then_inc(dense.evacuated, 1)
            for t in tiles(act, *gates):
                act.wait_ge(dense.mm_done, t.t + 5)
                act.wait_ge(gate_stored[t.odd], 16 * t.couple + 16)
                nc.scalar.activation(halves(gate[:, t.odd]), dense.out(t), ACT.Sigmoid).then_inc(dense.evacuated, 1)
                act.wait_ge(dense.evacuated, t.t + 5)
                act.dma_start(gates_dram[bass.ds(t.n, 1)].rearrange("a p n -> p (a n)"), gate[:, t.odd])\
                   .then_inc(gate_stored[t.odd], 16)
            for s in gate_stored:
                act.wait_ge(s, 16 * (N_GATE // 2) + 16)

        @block.tensor
        def _(pe):
            norm.pe(pe)
            pe.wait_ge(norm.split, DK)
            dense.multiply(pe, plain, dense.whole(nh, nl, DK))
            dense.multiply(pe, gates, dense.whole(nh, nl, DK))


RK0 = 12
R0, K0, V0, LW0, LG0, FQ0, FK0, FV0, FF0 = 0, 4, 8, 12, 13, 14, 18, 22, 26


def prepare(sems, nc, pb, C, keep, dram):
    with ExitStack() as ctx:
        sb = lambda n, s, d=F32: ctx.enter_context(nc.sbuf_tensor(n, s, d))
        sem = sems
        ps = ctx.enter_context(nc.psum_tensor("c_ps", [P, 4, 2, 512], F32))
        c2 = sb("c_c2", [P, N_CCOL2])
        K = lambda name, rows=P: c2[0:rows, CCOL2[name]:CCOL2[name] + CC2_COLS[name]]
        lora = sb("c_lora", [P, 512])
        shift = sb("c_shift", [P, N_SH, NB])
        newshift = sb("c_newshift", [P, N_SH, 1 + NB])
        diff = sb("c_diff", [P, 4, TOK])
        lw = sb("c_lw", [P, FT, TOK])
        sq = sb("c_sq", [P, 2, TOK])
        st = sb("c_st", [24, TOK])
        gq = sb("c_gq", [P, 1])
        tmp = sb("c_tmp", [P, 2, TOK])
        f_z, f_m, f_a, f_e = sb("c_fz", [NH, TOK]), sb("c_fm", [NH, TOK]), sb("c_fa", [NH, TOK]), sb("c_fe", [NH, TOK])
        cum, kk, kka, cnt = keep["cum"], keep["kk"], keep["kka"], keep["cnt"]
        rk8, cn = pb[0:NH, RK0], pb[0:NH, FF0]
        par = C["par"]

        loaded, mixed, shifted, lora_act = sem("c_loaded"), sem("c_mixed"), sem("c_shifted"), sem("c_lora_act")
        lora_mm, lora_out, squares = sem("c_lora_mm"), sem("c_lora_out"), sem("c_squares")
        sq_used, kraw, biased, rooted, inverted = sem("c_sq_used"), sem("c_kraw"), sem("c_biased"), sem("c_rooted"), sem("c_inverted")
        spread, normed, scanned = sem("c_spread"), sem("c_normed"), sem("c_scanned")
        f_abs, f_exp, f_log, f_done = sem("c_f_abs"), sem("c_f_exp"), sem("c_f_log"), sem("c_f_done")
        rkprod, rksum, tp, mids, mids_done = sem("c_rkprod"), sem("c_rksum"), sem("c_tp"), sem("c_mids"), sem("c_mids_done")
        v_link, a_link, stored = sem("c_v_link"), sem("c_a_link"), sem("c_stored")
        block = ctx.enter_context(nc.Block())

        @block.sync
        def _(sp):
            sp.dma_start(lora[:], dram["lora"]).then_inc(loaded, 16)
            sp.dma_start(shift[:], dram["shift_in"]).then_inc(loaded, 16)
            sp.dma_start(c2[:], dram["c2"]).then_inc(loaded, 16)
            sp.dma_start(dram["v_out"], pb[:, FV0:FV0 + FT]).then_inc(stored, 16)
            sp.wait_ge(shifted, 1)
            sp.dma_start(dram["shift_out"], newshift[:]).then_inc(stored, 16)
            sp.wait_ge(f_done, 1)
            sp.dma_start(dram["logf_out"], f_z[:]).then_inc(stored, 16)
            sp.wait_ge(normed, 8)
            sp.dma_start(dram["k_out"], pb[:, FK0:FK0 + FT]).then_inc(stored, 16)
            sp.wait_ge(stored, 64)

        @block.vector
        def _(dve):
            link = Chain(dve, v_link)
            tail = lambda a: a[:, :, SEQ:TOK].rearrange("p i (b t) -> p i b t", b=NB)
            dve.wait_ge(loaded, 48)
            nc.vector.tensor_copy(newshift[:, :, 0:1], pb[:, 0:N_SH, SEQ - 1:SEQ])
            link(nc.vector.tensor_copy(newshift[:, :, 1:1 + NB], tail(pb)[:, 0:N_SH, :, NT - 1]))
            dve.nop().then_inc(shifted, 1)
            for a, n in ((LW0, 2), (K0, 4), (R0, 4), (V0, 4)):
                p, d = pb[:, a:a + n], diff[:, 0:n]
                nc.vector.tensor_tensor(d[:, :, 1:SEQ], p[:, :, 0:SEQ - 1], p[:, :, 1:SEQ], ALU.subtract)
                nc.vector.tensor_scalar(d[:, :, 0:1], p[:, :, 0:1], -1.0, None, ALU.mult)
                ps_, ds_ = tail(p), tail(d)
                for i in range(n):
                    nc.vector.tensor_tensor(ds_[:, i, :, 1:NT], ps_[:, i, :, 0:NT - 1], ps_[:, i, :, 1:NT], ALU.subtract)
                link(nc.vector.tensor_tensor(ds_[:, :, :, 0], shift[:, a:a + n], ps_[:, :, :, 0], ALU.subtract))
                for i in range(n):
                    last = nc.vector.scalar_tensor_tensor(p[:, i], d[:, i], par("mu", a + i), p[:, i], ALU.mult, ALU.add)
                link(last)
                dve.nop().then_inc(mixed, 1)
            for ft in range(FT):
                last = nc.vector.tensor_scalar(kk[:, ft], pb[:, K0 + ft], par("kk", ft), -1.0, ALU.mult, ALU.mult)
            link(last)
            dve.nop().then_inc(kraw, 1)
            z = pb[0:NH, FF0]
            link(nc.vector.tensor_scalar(f_z[:], z, par("bf", 0, NH), None, ALU.add))
            nc.vector.tensor_scalar(f_m[:], f_z[:], 0.0, None, ALU.min)
            nc.vector.scalar_tensor_tensor(f_a[:], f_z[:], -1.0, f_z[:], ALU.mult, ALU.max).then_inc(f_abs, 1)
            for ft in range(FT):
                dve.wait_ge(lora_out, ft + 1)
                nc.vector.tensor_tensor_scan(cum[:, ft], K("reset"), lw[:, ft], 0.0, ALU.mult, ALU.add)\
                    .then_inc(scanned, 1)
            dve.wait_ge(scanned, FT)
            dve.wait_ge(f_abs, 1)
            m, e = keep["mid"], keep["mexp"]
            nc.vector.tensor_copy(m[:], cum[:, :, CH // 2 - 1:SEQ:CH])
            link(nc.vector.tensor_copy(e[:, 1], cum[:, :, CH - 1:SEQ:CH]))
            link(nc.vector.tensor_tensor(e[:, 1], e[:, 1], m[:], ALU.subtract))
            dve.nop().then_inc(mids, 1)
            dve.wait_ge(f_log, 1)
            link(nc.vector.tensor_tensor(f_z[:], f_m[:], f_e[:], ALU.subtract))
            dve.nop().then_inc(f_done, 1)
            link(nc.vector.tensor_tensor_scan(cn, K("fresh", NH), f_z[:], 0.0, ALU.mult, ALU.add))
            dve.nop().then_inc(f_done, 1)
            dve.wait_ge(sq_used, 12)
            link(nc.vector.tensor_scalar(halves(st[:]), ps[0:24, 0, :, 0:HALF], par("sc", 0, 24), par("ad", 0, 24),
                                         ALU.mult, ALU.add))
            nc.vector.tensor_scalar(st[:], st[:], 1e-24, None, ALU.max).then_inc(biased, 1)
            link(nc.vector.tensor_scalar(gq[:], par("qn", 0), float(DH) ** -0.5, None, ALU.mult))
            dve.wait_ge(rooted, 1)
            nc.vector.reciprocal(st[:], st[:]).then_inc(inverted, 1)
            for i in range(12):
                dve.wait_ge(spread, i + 1)
                src = ps[:, i % 4, :, 0:HALF]
                if i < 8:
                    t = pb[:, FQ0 + i]
                    g = gq[:] if i < 4 else par("kn", 0)
                    nc.vector.scalar_tensor_tensor(halves(t), halves(t), g, src, ALU.mult, ALU.mult).then_inc(normed, 1)
                else:
                    t = kk[:, i - 8]
                    nc.vector.tensor_tensor(halves(t), halves(t), src, ALU.mult).then_inc(normed, 1)
            for ft in range(FT):
                dve.wait_ge(lora_out, FT + ft + 1)
                k, r = pb[:, K0 + ft], pb[:, R0 + ft]
                link(nc.vector.tensor_scalar(tmp[:, 0], kka[:, ft], 1.0, par("ka", ft), ALU.subtract, ALU.mult))
                link(nc.vector.scalar_tensor_tensor(k, tmp[:, 0], 1.0, k, ALU.add, ALU.mult))
                if ft:
                    dve.wait_ge(rksum, ft)
                nc.vector.scalar_tensor_tensor(tmp[:, 1], r, par("rk", ft), k, ALU.mult, ALU.mult).then_inc(rkprod, 1)
                dve.wait_ge(normed, 9 + ft)
                link(nc.vector.scalar_tensor_tensor(kka[:, ft], kk[:, ft], -1.0, kka[:, ft], ALU.mult, ALU.mult))
            dve.wait_ge(rksum, FT)
            nc.vector.tensor_copy(halves(rk8), ps[0:NH, 0, :, 0:HALF])
            dve.wait_ge(tp, 1)
            nc.vector.tensor_copy(keep["vn"][:], ps[0:64, 1, 0, :])
            nc.vector.tensor_copy(cnt[:], ps[0:64, 1, 1, 0:NH])

        @block.scalar
        def _(act):
            act.wait_ge(loaded, 48)
            act.wait_ge(mixed, 1)
            nc.scalar.activation(pb[0:64, LW0], pb[0:64, LW0], ACT.Tanh).then_inc(lora_act, 1)
            nc.scalar.activation(pb[:, LG0], pb[:, LG0], ACT.Sigmoid)
            for i in range(2 * FT):
                act.wait_ge(lora_mm, i + 1)
                out = lw[:, i] if i < FT else kka[:, i - FT]
                nc.scalar.activation(halves(out), ps[:, i % 4, :, 0:HALF], ACT.Sigmoid,
                                     bias=par("w0" if i < FT else "a0", i % FT)).then_inc(lora_out, 1)
            act.wait_ge(kraw, 1)
            for i in range(12):
                if i >= 2:
                    act.wait_ge(sq_used, i - 1)
                src = pb[:, FQ0 + i] if i < 8 else kk[:, i - 8]
                nc.scalar.activation(sq[:, i % 2], src, ACT.Square).then_inc(squares, 1)
            act.wait_ge(f_abs, 1)
            nc.scalar.activation(f_e[:], f_a[:], ACT.Exp, scale=-1.0).then_inc(f_exp, 1)
            act.wait_ge(f_exp, 1)
            nc.scalar.activation(f_e[:], f_e[:], ACT.Ln, bias=1.0).then_inc(f_log, 1)
            act.wait_ge(biased, 1)
            nc.scalar.activation(st[:], st[:], ACT.Sqrt).then_inc(rooted, 1)
            act.wait_ge(mids, 1)
            e = keep["mexp"]
            nc.scalar.activation(e[:, 0], keep["mid"][:], ACT.Exp, scale=-KAPPA)
            nc.scalar.activation(e[:, 2], keep["mid"][:], ACT.Exp, scale=KAPPA)
            nc.scalar.activation(e[:, 1], e[:, 1], ACT.Exp, scale=-KAPPA)

        @block.gpsimd
        def _(pool):
            q = keep["qbd"]
            nc.gpsimd.memset(q[:], 0.0).then_inc(mids_done, 1)
            pool.wait_ge(mids_done, 1)
            pool.wait_ge(normed, 4)
            for u in range(2):
                for i in range(FT):
                    src = pb[64 * u:64 * u + 64, FQ0 + i, SEQ:TOK].rearrange("p (b t) -> p b t", b=NB)
                    nc.gpsimd.tensor_copy(q[64 * u:64 * u + 64, i, :, u, :], src)

        @block.tensor
        def _(pe):
            pe.wait_ge(loaded, 48)
            pe.wait_ge(lora_act, 1)
            for i in range(2 * FT):
                if i >= 4:
                    pe.wait_ge(lora_out, i - 3)
                r = slice(0, 64) if i < FT else slice(64, P)
                for half in range(2):
                    mm = nc.tensor.matmul(ps[:, i % 4, half, 0:HALF], lora[r, (i % FT) * P:(i % FT) * P + P],
                                          pb[r, LW0, half * HALF:half * HALF + HALF], start=True, stop=True)
                mm.then_inc(lora_mm, 1)
            pe.wait_ge(lora_out, 2 * FT)
            sel = K("sel24").rearrange("p (i m) -> p i m", i=12)
            for i in range(12):
                pe.wait_ge(squares, i + 1)
                for half in range(2):
                    mm = nc.tensor.matmul(ps[0:24, 0, half, 0:HALF], sel[:, i], sq[:, i % 2, half * HALF:half * HALF + HALF],
                                          start=i == 0, stop=i == 11)
                mm.then_inc(sq_used, 1)
            pe.wait_ge(inverted, 1)
            selt = K("selt", 24).rearrange("p (i m) -> p i m", i=12)
            for i in range(12):
                if i >= 4:
                    pe.wait_ge(normed, i - 3)
                for half in range(2):
                    mm = nc.tensor.matmul(ps[:, i % 4, half, 0:HALF], selt[:, i], st[:, half * HALF:half * HALF + HALF],
                                          start=True, stop=True)
                mm.then_inc(spread, 1)
            pe.wait_ge(normed, 12)
            for ft in range(FT):
                pe.wait_ge(rkprod, ft + 1)
                for half in range(2):
                    mm = nc.tensor.matmul(ps[0:NH, 0, half, 0:HALF], sel[:, 8 + ft, 16:24],
                                          tmp[:, 1, half * HALF:half * HALF + HALF], start=ft == 0, stop=ft == FT - 1)
                mm.then_inc(rksum, 1)
            pe.wait_ge(f_done, 2)
            for i in range(FT):
                nc.tensor.transpose(ps[0:64, 1, 0, i * P:(i + 1) * P], pb[:, FV0 + i, SEQ:TOK], C["ident"])
            nc.tensor.transpose(ps[0:64, 1, 1, 0:NH], cn[:, SEQ:TOK], C["ident"][0:NH, 0:NH]).then_inc(tp, 1)


class Rwkv:

    TR, BANKS = 3, 2

    def __init__(self, ctx, sems, nc, tag, T, levels, pb, C, keep, buf, sample):
        self.nc, self.T, self.levels, self.pb, self.C, self.keep, self.sample = nc, T, levels, pb, C, keep, sample
        self.bank, self.cc, self.e1, self.e3, self.ar = buf["bank"], buf["cc"], buf["e1"], buf["e3"], buf["ar"]
        self.bf, self.kf, self.vf, self.bt, self.kt, self.vt = (buf[n] for n in ("bf", "kf", "vf", "bt", "kt", "vt"))
        self.ntg, self.nkg, self.x, self.xt, self.tt = (buf[n] for n in ("ntg", "nkg", "x", "xt", "tt"))
        self.rs, self.us = buf["rs"], buf["us"]
        if sample:
            self.s0, self.sa, self.ux, self.vx = buf["s0"], buf["sa"], buf["ux"], buf["vx"]
            self.s_loaded, self.x_part, self.y_taken, self.s_added = (
                buf[n] for n in ("s_loaded", "x_part", "y_taken", "s_added"))
        else:
            self.s, self.s_mid = buf["s"], buf["s_mid"]
        sem = lambda n: sems(n + tag)
        self.gram_heads = 512 // (2 * T)
        self.rounds = 3 + 2 * (NH // self.gram_heads)
        self.centred, self.exped, self.shifted, self.ready = sem("rw_centred"), sem("rw_exped"), sem("rw_shifted"), sem("rw_ready")
        self.v_copied, self.mm, self.ev = sem("rw_v_copied"), sem("rw_mm"), sem("rw_evacuated")
        self.t_mm, self.t_ev = [sem("rw_t_mm0"), sem("rw_t_mm1")], [sem("rw_t_ev0"), sem("rw_t_ev1")]
        self.xt_mm, self.xt_ev = [sem("rw_xt_mm0"), sem("rw_xt_mm1")], [sem("rw_xt_ev0"), sem("rw_xt_ev1")]
        self.x_mm, self.x_ev = [sem("rw_x_mm0"), sem("rw_x_mm1")], [sem("rw_x_ev0"), sem("rw_x_ev1")]
        self.sm, self.r_mm, self.r_ev, self.u_mm, self.u_ev = sem("rw_sm"), sem("rw_r_mm"), sem("rw_r_ev"), sem("rw_u_mm"), sem("rw_u_ev")
        self.y_mm, self.d_mm, self.d_part, self.done = sem("rw_y_mm"), sem("rw_d_mm"), sem("rw_d_part"), sem("rw_done")

    def seed(self, dve):
        dve.nop().then_inc(self.done, 1)

    def cols(self, c):
        return slice(SEQ, TOK) if self.sample else bass.ds(c * CH, CH)

    def heads(self, g):
        first = g % (NH // self.gram_heads)
        return [first % 2 + 2 * (first // 2 * self.gram_heads + j) for j in range(self.gram_heads)]

    def act_exps(self, act, c):
        T = self.T
        act.wait_ge(self.centred, c + 1)
        self.nc.scalar.activation(self.e1[:, :, 0:T], self.cc[:, :, 0:T], ACT.Exp, scale=-KAPPA).then_inc(self.exped, 1)
        self.nc.scalar.activation(self.e3[:, :, 0:T], self.cc[:, :, 0:T], ACT.Exp, scale=KAPPA).then_inc(self.exped, 1)

    def pool_v(self, pool, c):
        pool.wait_ge(self.done, c + 1)
        self.nc.gpsimd.tensor_copy(self.vf[:, :, 0:self.T], self.pb[:, V0:V0 + FT, self.cols(c)]).then_inc(self.v_copied, 1)

    def dve_operands(self, dve, c):
        nc, T, t, pb, keep = self.nc, self.T, self.cols(c), self.pb, self.keep
        if self.sample:
            nc.vector.tensor_copy(self.cc[:, :, 0:T], keep["cum"][:, :, t]).then_inc(self.centred, 1)
        else:
            mid = keep["mid"][:, :, bass.ds(c, 1)].broadcast_to([P, FT, T])
            nc.vector.tensor_tensor(self.cc[:, :, 0:T], keep["cum"][:, :, t], mid, ALU.subtract).then_inc(self.centred, 1)
        dve.wait_ge(self.exped, 2 * c + 1)
        nc.vector.tensor_tensor(self.ar[:, :, 1, 0:T], pb[:, R0:R0 + FT, t], self.e1[:, :, 0:T], ALU.mult)
        if self.sample:
            g = lambda a: a.rearrange("p f (b t) -> p f b t", t=NT)
            for f in range(FT):
                a, k, e = (g(x)[:, f] for x in (self.ar[:, :, 0, 0:T], keep["kk"][:, :, t], self.e1[:, :, 0:T]))
                nc.vector.tensor_tensor(a[:, :, 1:NT], k[:, :, 1:NT], e[:, :, 0:NT - 1], ALU.mult)
                nc.vector.tensor_copy(a[:, :, 0:1], k[:, :, 0:1])
        else:
            first = keep["mexp"][:, 2, :, bass.ds(c, 1)]
            nc.vector.tensor_tensor(self.ar[:, :, 0, 1:T], keep["kk"][:, :, bass.ds(c * CH + 1, CH - 1)],
                                    self.e1[:, :, 0:T - 1], ALU.mult)
            nc.vector.tensor_tensor(self.ar[:, :, 0, 0:1], keep["kk"][:, :, bass.ds(c * CH, 1)], first, ALU.mult)
        dve.wait_ge(self.exped, 2 * c + 2)
        nc.vector.tensor_tensor(self.bf[:, :, 0:T], keep["kka"][:, :, t], self.e3[:, :, 0:T], ALU.mult)
        nc.vector.tensor_tensor(self.kf[:, :, 0:T], pb[:, K0:K0 + FT, t], self.e3[:, :, 0:T], ALU.mult).then_inc(self.ready, 1)

    def pe_grams(self, pe, c):
        nc, T, gh = self.nc, self.T, self.gram_heads
        pe.wait_ge(self.ready, c + 1)
        pe.wait_ge(self.done, c + 1)
        for n in range(self.rounds):
            if n >= self.BANKS:
                pe.wait_ge(self.ev, c * self.rounds + n - self.BANKS + 1)
            bank = self.bank[n % 2]
            if n < self.TR:
                if n == 2:
                    pe.wait_ge(self.v_copied, c + 1)
                src = (self.bf, self.kf, self.vf)[n]
                for f in range(FT):
                    mm = nc.tensor.transpose(bank[0:T, f * P:f * P + P], src[:, f, 0:T], self.C["ident"])
            else:
                g = n - self.TR
                src = self.bf if g < NH // gh else self.kf
                for j in range(gh):
                    h = self.heads(g)[j]
                    po, f = h % 2 * DH, h // 2
                    out = bank[0:T, j * 2 * T:j * 2 * T + 2 * T]
                    mm = nc.tensor.matmul(out.rearrange("p (a t) -> p a t", a=2), src[po:po + DH, f, 0:T],
                                          self.ar[po:po + DH, f, :, 0:T], start=True, stop=True)
            mm.then_inc(self.mm, 1)

    def dve_grams(self, dve, c):
        nc, T, gh = self.nc, self.T, self.gram_heads
        mask = self.C["lows"][0:T, 0:2 * T] if self.sample else self.C["low"]
        mask = mask[:, None, :].broadcast_to([T, gh, 2 * T])
        for n in range(self.rounds):
            dve.wait_ge(self.mm, c * self.rounds + n + 1)
            bank = self.bank[n % 2]
            if n < self.TR:
                nc.vector.tensor_copy((self.bt, self.kt, self.vt)[n][0:T], bank[0:T, 0:512]).then_inc(self.ev, 1)
            else:
                g = n - self.TR
                dst, h = (self.ntg if g < NH // gh else self.nkg), self.heads(g)
                nc.vector.tensor_tensor(dst[0:T, h[0]:h[-1] + 1:2, 0:2 * T], bank[0:T].rearrange("p (h m) -> p h m", h=gh),
                                        mask, ALU.mult).then_inc(self.ev, 1)

    def view(self, buf, bt):
        return buf[0:self.T, 4 * bt:4 * bt + 4, 0:self.T]

    def pe_level(self, pe, c, level, bt):
        nc, T, L, ident = self.nc, self.T, self.levels, self.C["ident"]
        out = self.bank[bt].rearrange("p (h m) -> p h m", h=4)
        if level == 0 and bt == 0:
            pe.wait_ge(self.ev, (c + 1) * self.rounds)
        if level:
            pe.wait_ge(self.x_ev[bt], c * (L - 1) + level)
        for j in range(4):
            h = 4 * bt + j
            if level == 0:
                mm = nc.tensor.transpose(out[0:T, j, 0:T], self.ntg[0:T, h, 0:T], ident[0:T, 0:T])
            else:
                mm = nc.tensor.matmul(out[0:T, j, 0:T], self.ntg[0:T, h, 0:T], self.x[0:T, h, 0:T], start=True, stop=True)
        mm.then_inc(self.t_mm[bt], 1)

    def pe_level_xt(self, pe, c, level, bt):
        nc, T, L, ident = self.nc, self.T, self.levels, self.C["ident"]
        out = self.bank[bt].rearrange("p (h m) -> p h m", h=4)
        pe.wait_ge(self.t_ev[bt], c * L + level + 1)
        for j in range(4):
            h = 4 * bt + j
            if level == 0:
                mm = nc.tensor.transpose(out[0:T, j, 0:T], self.tt[0:T, h, 0:T], ident[0:T, 0:T])
            else:
                mm = nc.tensor.matmul(out[0:T, j, 0:T], self.tt[0:T, h, 0:T], self.xt[0:T, h, 0:T], start=True, stop=True)
        mm.then_inc(self.xt_mm[bt], 1)

    def pe_level_x(self, pe, c, level, bt):
        nc, T, L = self.nc, self.T, self.levels
        out = self.bank[bt].rearrange("p (h m) -> p h m", h=4)
        pe.wait_ge(self.xt_ev[bt], c * L + level + 1)
        for j in range(4):
            mm = nc.tensor.transpose(out[0:T, j, 0:T], self.xt[0:T, 4 * bt + j, 0:T], self.C["ident"][0:T, 0:T])
        mm.then_inc(self.x_mm[bt], 1)

    def pe_invert(self, pe, c):
        for level in range(self.levels):
            for bt in range(2):
                self.pe_level(pe, c, level, bt)
            for bt in range(2):
                self.pe_level_xt(pe, c, level, bt)
            if level < self.levels - 1:
                for bt in range(2):
                    self.pe_level_x(pe, c, level, bt)

    def dve_invert(self, dve, c):
        nc, T, L = self.nc, self.T, self.levels
        ident = self.C["ident"][0:T, None, 0:T].broadcast_to([T, 4, T])
        for level in range(L):
            mask = self.C["lev"][0:T, level * P:level * P + T][:, None, :].broadcast_to([T, 4, T])
            for bt in range(2):
                src = self.bank[bt].rearrange("p (h m) -> p h m", h=4)[0:T, :, 0:T]
                dve.wait_ge(self.t_mm[bt], c * L + level + 1)
                nc.vector.tensor_tensor(self.view(self.tt, bt), src, mask, ALU.mult).then_inc(self.t_ev[bt], 1)
            for bt in range(2):
                src = self.bank[bt].rearrange("p (h m) -> p h m", h=4)[0:T, :, 0:T]
                dve.wait_ge(self.xt_mm[bt], c * L + level + 1)
                if level:
                    dve.wait_ge(self.xt_ev[bt], c * L + level)
                add = self.view(self.xt, bt) if level else ident
                nc.vector.tensor_tensor(self.view(self.xt, bt), src, add, ALU.add).then_inc(self.xt_ev[bt], 1)

    def act_invert(self, act, c):
        for level in range(self.levels - 1):
            for bt in range(2):
                src = self.bank[bt].rearrange("p (h m) -> p h m", h=4)[0:self.T, :, 0:self.T]
                act.wait_ge(self.x_mm[bt], c * (self.levels - 1) + level + 1)
                self.nc.scalar.activation(self.view(self.x, bt), src, ACT.Copy).then_inc(self.x_ev[bt], 1)


    def pe_chunk(self, pe, c):
        nc, L = self.nc, self.levels
        b0, b1 = self.bank
        for bt in range(2):
            pe.wait_ge(self.xt_ev[bt], (c + 1) * L)
        pe.wait_ge(self.sm, c + 1)
        for h in range(NH):
            po, f, hs = h % 2 * DH, h // 2, slice(h * DH, h * DH + DH)
            out = self.bank[h % 2][:, f * DH:f * DH + DH]
            nc.tensor.matmul(out, self.ar[po:po + DH, f, 0], self.s_mid[po:po + DH, f], start=True, stop=False)
            mm = nc.tensor.matmul(out, self.nkg[:, h, 0:CH], self.vt[:, hs], start=False, stop=True)
        mm.then_inc(self.r_mm, 1)
        pe.wait_ge(self.r_ev, 2 * c + 2)
        for h in range(NH):
            hs = slice(h * DH, h * DH + DH)
            mm = nc.tensor.matmul(b0[:, hs], self.xt[:, h], self.rs[:, hs], start=True, stop=True)
        mm.then_inc(self.u_mm, 1)
        pe.wait_ge(self.u_ev, c + 1)
        for h in range(NH):
            po, f, hs = h % 2 * DH, h // 2, slice(h * DH, h * DH + DH)
            out = b1[po:po + DH, f * CH:f * CH + CH]
            nc.tensor.matmul(out, self.us[:, hs], self.ntg[:, h, CH:2 * CH], start=True, stop=False)
            nc.tensor.matmul(out, self.vt[:, hs], self.nkg[:, h, CH:2 * CH], start=False, stop=False)
            mm = nc.tensor.matmul(out, self.s_mid[po:po + DH, f], self.ar[po:po + DH, f, 1], start=False, stop=True)
        mm.then_inc(self.y_mm, 1)
        for h in range(NH):
            po, f, hs = h % 2 * DH, h // 2, slice(h * DH, h * DH + DH)
            out = b0[po:po + DH, f * DH:f * DH + DH]
            nc.tensor.matmul(out, self.bt[:, hs], self.us[:, hs], start=True, stop=False)
            mm = nc.tensor.matmul(out, self.kt[:, hs], self.vt[:, hs], start=False, stop=True)
        mm.then_inc(self.d_mm, 1)

    def act_chunk(self, act, c):
        act.wait_ge(self.r_mm, c + 1)
        for u in range(2):
            dst = self.rs.rearrange("p (f u v) -> p f u v", f=FT, u=2)[:, :, u]
            src = self.bank[u][:, 0:FT * DH].rearrange("p (f v) -> p f v", f=FT)
            self.nc.scalar.activation(dst, src, ACT.Copy).then_inc(self.r_ev, 1)

    def dve_state_in(self, dve, c):
        e = self.keep["mexp"][:, 0, :, bass.ds(c, 1)].broadcast_to([P, FT, DH])
        dve.wait_ge(self.done, c + 1)
        self.nc.vector.tensor_tensor(self.s_mid[:], self.s[:], e, ALU.mult).then_inc(self.sm, 1)

    def dve_chunk(self, dve, c):
        nc = self.nc
        dve.wait_ge(self.u_mm, c + 1)
        nc.vector.tensor_copy(self.us[:], self.bank[0]).then_inc(self.u_ev, 1)
        dve.wait_ge(self.y_mm, c + 1)
        nc.vector.tensor_scalar(self.pb[:, R0:R0 + FT, self.cols(c)], self.bank[1].rearrange("p (f t) -> p f t", f=FT),
                                1.0, None, ALU.mult)
        dve.wait_ge(self.d_mm, c + 1)
        src = self.bank[0][:, 0:FT * DH].rearrange("p (f v) -> p f v", f=FT)
        e = self.keep["mexp"][:, 1, :, bass.ds(c, 1)].broadcast_to([P, FT, DH])
        nc.vector.tensor_tensor(self.s[:], src, self.s_mid[:], ALU.add).then_inc(self.d_part, 1)
        dve.wait_ge(self.d_part, c + 1)
        nc.vector.tensor_tensor(self.s[:], self.s[:], e, ALU.mult).then_inc(self.done, 1)


    def pe_sample(self, pe):
        nc, T, L = self.nc, self.T, self.levels
        b0, b1 = self.bank
        for bt in range(2):
            pe.wait_ge(self.xt_ev[bt], L)
        pe.wait_ge(self.s_loaded, 16)
        view = b0.rearrange("p (f a t) -> p f a t", f=FT, a=2)
        for f in range(FT):
            for b in range(NB):
                for po in (0, DH):
                    mm = nc.tensor.matmul(view[po:po + DH, f, :, NT * b:NT * b + NT], self.s0[po:po + DH, f, b],
                                          self.ar[po:po + DH, f, :, NT * b:NT * b + NT], start=True, stop=True)
        mm.then_inc(self.sm, 1)
        pe.wait_ge(self.d_part, 1)
        for f in range(FT):
            for u in range(2):
                h = 2 * f + u
                hs = slice(h * DH, h * DH + DH)
                nc.tensor.matmul(b1[0:T, hs], self.sa[:, f, 0], self.C["ident"][:, u * DH:u * DH + DH], start=True, stop=False)
                mm = nc.tensor.matmul(b1[0:T, hs], self.nkg[0:T, h, 0:T], self.vt[0:T, hs], start=False, stop=True)
        mm.then_inc(self.r_mm, 1)
        pe.wait_ge(self.r_ev, 1)
        for h in range(NH):
            hs = slice(h * DH, h * DH + DH)
            mm = nc.tensor.matmul(b0[0:T, hs], self.xt[0:T, h, 0:T], self.rs[0:T, hs], start=True, stop=True)
        mm.then_inc(self.u_mm, 1)
        pe.wait_ge(self.u_ev, 1)
        for h in range(NH):
            po, f, hs = h % 2 * DH, h // 2, slice(h * DH, h * DH + DH)
            out = b1[po:po + DH, f * T:f * T + T]
            nc.tensor.matmul(out, self.us[0:T, hs], self.ntg[0:T, h, T:2 * T], start=True, stop=False)
            mm = nc.tensor.matmul(out, self.vt[0:T, hs], self.nkg[0:T, h, T:2 * T], start=False, stop=True)
        mm.then_inc(self.y_mm, 1)
        for f in range(FT):
            pe.wait_ge(self.x_part, f + 1)
            if f >= 2:
                pe.wait_ge(self.done, f)
            if f == 1:
                pe.wait_ge(self.y_taken, 1)
            for po in (0, DH):
                h = 2 * f + po // DH
                hs = slice(h * DH, h * DH + DH)
                ux, vx = self.ux[0:T, f % 2, po // DH], self.vx[0:T, f % 2, po // DH]
                nc.tensor.matmul(self.bank[f % 2][po:po + DH], self.bt[0:T, hs], ux, start=True, stop=False)
                mm = nc.tensor.matmul(self.bank[f % 2][po:po + DH], self.kt[0:T, hs], vx, start=False, stop=True)
            mm.then_inc(self.d_mm, 1)

    def act_sample(self, act):
        act.wait_ge(self.r_mm, 1)
        self.nc.scalar.activation(self.rs[0:self.T], self.bank[1][0:self.T], ACT.Copy).then_inc(self.r_ev, 1)

    def dve_sample(self, dve):
        nc, T = self.nc, self.T
        b0, b1 = self.bank
        dve.wait_ge(self.sm, 1)
        nc.vector.tensor_copy(self.sa[:], b0.rearrange("p (f a t) -> p f a t", f=FT, a=2)).then_inc(self.d_part, 1)
        dve.wait_ge(self.u_mm, 1)
        nc.vector.tensor_copy(self.us[0:T], b0[0:T]).then_inc(self.u_ev, 1)
        dve.wait_ge(self.u_ev, 1)
        dve.wait_ge(self.y_mm, 1)
        nc.vector.tensor_tensor(self.pb[:, R0:R0 + FT, SEQ:TOK], b1[:, 0:FT * T].rearrange("p (f t) -> p f t", f=FT),
                                self.sa[:, :, 1], ALU.add).then_inc(self.y_taken, 1)
        bm = self.C["bmask"][0:T, :, None].broadcast_to([T, NB, DH])
        for f in range(FT):
            if f >= 2:
                dve.wait_ge(self.d_mm, f - 1)
            for u in range(2):
                h = 2 * f + u
                for src, dst in ((self.us, self.ux), (self.vt, self.vx)):
                    v = src[0:T, h * DH:h * DH + DH][:, None, :].broadcast_to([T, NB, DH])
                    last = nc.vector.tensor_tensor(dst[0:T, f % 2, u].rearrange("p (b v) -> p b v", b=NB), v, bm, ALU.mult)
            last.then_inc(self.x_part, 1)
            if f >= 1:
                self.dve_state_out(dve, f - 1)
        self.dve_state_out(dve, FT - 1)

    def dve_state_out(self, dve, f):
        nc = self.nc
        dve.wait_ge(self.d_mm, f + 1)
        src = self.bank[f % 2].rearrange("p (b v) -> p b v", b=NB)
        nc.vector.tensor_tensor(self.s0[:, f], src, self.s0[:, f], ALU.add).then_inc(self.s_added, 1)
        dve.wait_ge(self.s_added, f + 1)
        e = self.e1[:, f, NT - 1:NB * NT:NT][:, :, None].broadcast_to([P, NB, DH])
        nc.vector.tensor_tensor(self.s0[:, f], self.s0[:, f], e, ALU.mult).then_inc(self.done, 1)


class FoxPrompt:

    UNITS = [(u, i) for i in range(SEQ // P) for u in range(2)]

    def __init__(self, ctx, sems, nc, pb, C, keep, banks):
        self.nc, self.pb, self.C, self.keep = nc, pb, C, keep
        sb = lambda n, s, d=F32: ctx.enter_context(nc.sbuf_tensor(n, s, d))
        sem = sems
        self.b_s, self.b_t, self.b_o = banks
        self.q, self.k, self.v = sb("fp_q", [P, SEQ], F32), sb("fp_k", [P, SEQ]), sb("fp_v", [P, SEQ])
        self.cm, self.bias, self.vt = sb("fp_cm", [NH, 2, SEQ]), sb("fp_bias", [P, 2, SEQ]), sb("fp_vt", [P, 4, P])
        self.diag = sb("fp_diag", [P, 2, SEQ])
        self.s, self.p, self.pt = sb("fp_s", [P, 2, SEQ]), sb("fp_p", [P, 2, SEQ]), sb("fp_pt", [P, 2, 4, P])
        self.nm, self.rsum = sb("fp_nm", [P, 8]), sb("fp_rsum", [P, 8])
        self.copied, self.masked, self.bias_mm, self.bias_ev = sem("fp_copied"), sem("fp_masked"), sem("fp_bias_mm"), sem("fp_bias_ev")
        self.bias_diag, self.vt_mm, self.vt_ev = sem("fp_bias_diag"), sem("fp_vt_mm"), sem("fp_vt_ev")
        self.s_mm, self.s_ev, self.maxed, self.exped = sem("fp_s_mm"), sem("fp_s_ev"), sem("fp_maxed"), sem("fp_exped")
        self.inverted, self.p_done, self.t_mm, self.t_ev, self.o_mm, self.o_ev = (
            sem("fp_inverted"), sem("fp_p_done"), sem("fp_t_mm"), sem("fp_t_ev"), sem("fp_o_mm"), sem("fp_o_ev"))

    def seed(self, dve):
        dve.nop().then_inc(self.s_ev, 1)
        dve.nop().then_inc(self.o_ev, 1)
        dve.nop().then_inc(self.o_mm, 1)

    def pool(self, pool, c):
        pool.wait_ge(self.o_mm, 8 * c + 1)
        for dst, a in ((self.k, FK0), (self.q, FQ0), (self.v, FV0)):
            src = self.pb[:, a:a + FT][:, bass.ds(c, 1), 0:SEQ].rearrange("p a n -> p (a n)")
            self.nc.gpsimd.tensor_copy(dst[:], src).then_inc(self.copied, 1)

    def pe(self, pe, c):
        nc = self.nc
        pe.wait_ge(self.copied, 3 * c + 3)
        for u in range(2):
            pe.wait_ge(self.masked, 2 * c + u + 1)
            if u == 0:
                pe.wait_ge(self.s_ev, 8 * c + 1)
            else:
                pe.wait_ge(self.bias_ev, 2 * c + 1)
            nc.tensor.matmul(self.b_s[:], self.C["minus"][0:NH], self.cm[:, u], start=True, stop=True).then_inc(self.bias_mm, 1)
        for j in range(4):
            mm = nc.tensor.transpose(self.b_t[:, j * P:j * P + P], self.v[:, j * P:j * P + P], self.C["ident"])
        mm.then_inc(self.vt_mm, 1)
        pe.wait_ge(self.bias_ev, 2 * c + 2)
        pe.wait_ge(self.vt_ev, c + 1)
        self.scores(pe, c, 0)
        for n in range(8):
            if n < 7:
                self.scores(pe, c, n + 1)
            u, i = self.UNITS[n]
            pe.wait_ge(self.p_done, 8 * c + n + 1)
            if n:
                pe.wait_ge(self.t_ev, 8 * c + n)
            for j in range(i + 1):
                mm = nc.tensor.transpose(self.b_t[:, j * P:j * P + P], self.p[:, n % 2, j * P:j * P + P], self.C["ident"])
            mm.then_inc(self.t_mm, 1)
            pe.wait_ge(self.t_ev, 8 * c + n + 1)
            if n == 0:
                pe.wait_ge(self.o_ev, c + 1)
            po = u * DH
            for j in range(i + 1):
                mm = nc.tensor.matmul(self.b_o[po:po + DH, i * P:i * P + P], self.vt[:, j, po:po + DH],
                                      self.pt[:, n % 2, j], start=j == 0, stop=j == i)
            mm.then_inc(self.o_mm, 1)

    def scores(self, pe, c, n):
        u, i = self.UNITS[n]
        if n:
            pe.wait_ge(self.s_ev, 8 * c + n + 1)
        r = slice(u * DH, u * DH + DH)
        self.nc.tensor.matmul(self.b_s[:, 0:i * P + P], self.q[r, i * P:i * P + P], self.k[r, 0:i * P + P],
                              start=True, stop=True).then_inc(self.s_mm, 1)

    def dve(self, dve, c):
        nc = self.nc
        for u in range(2):
            nc.vector.tensor_scalar(self.cm[:, u], self.pb[0:NH, FF0, 0:SEQ], self.C["ident"][0:NH, bass.ds(2 * c + u, 1)],
                                    None, ALU.mult).then_inc(self.masked, 1)
        causal = self.C["causal"][:, None, :].broadcast_to([P, 4, P])
        for u in range(2):
            dve.wait_ge(self.bias_ev, 2 * c + u + 1)
            g = lambda a: a[:, u].rearrange("p (j n) -> p j n", j=4)
            nc.vector.tensor_tensor(g(self.diag), g(self.bias), causal, ALU.add).then_inc(self.bias_diag, 1)
        dve.wait_ge(self.bias_diag, 2 * c + 2)
        self.softmax_in(dve, c, 0)
        for n in range(8):
            if n < 7:
                self.softmax_in(dve, c, n + 1)
            u, i = self.UNITS[n]
            w = i * P + P
            dve.wait_ge(self.exped, 8 * c + n + 1)
            nc.vector.reciprocal(self.rsum[:, n:n + 1], self.rsum[:, n:n + 1]).then_inc(self.inverted, 1)
            dve.wait_ge(self.inverted, 8 * c + n + 1)
            nc.vector.tensor_scalar(self.p[:, n % 2, 0:w], self.p[:, n % 2, 0:w], self.rsum[:, n:n + 1], None,
                                    ALU.mult).then_inc(self.p_done, 1)

    def softmax_in(self, dve, c, n):
        nc = self.nc
        u, i = self.UNITS[n]
        a, w = i * P, i * P + P
        dve.wait_ge(self.s_mm, 8 * c + n + 1)
        if i:
            nc.vector.tensor_tensor(self.s[:, n % 2, 0:a], self.b_s[:, 0:a], self.bias[:, u, 0:a], ALU.add)
        nc.vector.tensor_tensor(self.s[:, n % 2, a:w], self.b_s[:, a:w], self.diag[:, u, a:w], ALU.add).then_inc(self.s_ev, 1)
        dve.wait_ge(self.s_ev, 8 * c + n + 2)
        nc.vector.tensor_reduce(self.nm[:, n:n + 1], self.s[:, n % 2, 0:w], AX.X, ALU.max, negate=True).then_inc(self.maxed, 1)

    def act(self, act, c):
        nc = self.nc
        for u in range(2):
            act.wait_ge(self.bias_mm, 2 * c + u + 1)
            nc.scalar.activation(self.bias[:, u], self.b_s[:], ACT.Copy).then_inc(self.bias_ev, 1)
        act.wait_ge(self.vt_mm, c + 1)
        nc.scalar.activation(self.vt[:].rearrange("p j n -> p (j n)"), self.b_t[:], ACT.Copy).then_inc(self.vt_ev, 1)
        for n in range(8):
            u, i = self.UNITS[n]
            w = i * P + P
            act.wait_ge(self.maxed, 8 * c + n + 1)
            if n >= 2:
                act.wait_ge(self.t_mm, 8 * c + n - 1)
            nc.scalar.activation(self.p[:, n % 2, 0:w], self.s[:, n % 2, 0:w], ACT.Exp, bias=self.nm[:, n:n + 1],
                                 accum_out=self.rsum[:, n:n + 1]).then_inc(self.exped, 1)
            if n:
                self.evacuate_turned(act, c, n - 1)
        self.evacuate_turned(act, c, 7)
        act.wait_ge(self.o_mm, 8 * c + 9)
        dst = self.pb[:, FQ0:FQ0 + FT][:, bass.ds(c, 1), 0:SEQ]
        nc.scalar.activation(dst, self.b_o[:][:, None, :], ACT.Copy).then_inc(self.o_ev, 1)

    def evacuate_turned(self, act, c, n):
        u, i = self.UNITS[n]
        act.wait_ge(self.t_mm, 8 * c + n + 1)
        self.nc.scalar.activation(self.pt[:, n % 2, 0:i + 1].rearrange("p j n -> p (j n)"), self.b_t[:, 0:i * P + P],
                                  ACT.Copy).then_inc(self.t_ev, 1)


class FoxSample:

    KR, VR = 4, 4

    def __init__(self, ctx, sems, nc, pb, C, keep, banks, dram):
        self.nc, self.pb, self.C, self.keep, self.dram = nc, pb, C, keep, dram
        sb = lambda n, s, d=F32: ctx.enter_context(nc.sbuf_tensor(n, s, d))
        sem = sems
        self.b0, self.b1, self.b2 = banks
        self.table = sb("fs_table", [1, NB * PAGES], I32)
        self.kr, self.vr = sb("fs_keys", [P, self.KR, KROW]), sb("fs_values", [P, self.VR, FT * P])
        self.lf, self.later, self.suf = sb("fs_lf", [P, PAGES, NH]), sb("fs_later", [P, PAGES, NH]), sb("fs_suf", [P, PAGES, NH])
        self.s, self.p = sb("fs_s", [P, PAGES + 1, 64]), sb("fs_p", [P, PAGES + 1, 64])
        self.mx, self.m1, self.sums, self.rden = sb("fs_mx", [P, P]), sb("fs_m1", [64, 1]), sb("fs_sums", [P, 64]), sb("fs_rden", [P, 64])
        self.k_in = [sem(f"fs_k_in{s}") for s in range(self.KR)]
        self.v_in = [sem(f"fs_v_in{s}") for s in range(self.VR)]
        self.t_in = sem("fs_table_in")
        self.k_used, self.lf_copied, self.v_used = sem("fs_k_used"), sem("fs_lf_copied"), sem("fs_v_used")
        self.lf_link, self.suffixes, self.s_mm, self.suf_ev, self.s_ev = sem("fs_lf_link"), sem("fs_suffixes"), sem("fs_s_mm"), sem("fs_suf_ev"), sem("fs_s_ev")
        self.new_link, self.maxed, self.turned, self.max1, self.max_mm = sem("fs_new_link"), sem("fs_maxed"), sem("fs_turned"), sem("fs_max1"), sem("fs_max_mm")
        self.less, self.exped, self.summed, self.den_mm, self.inverted = sem("fs_less"), sem("fs_exped"), sem("fs_summed"), sem("fs_den_mm"), sem("fs_inverted")
        self.o_mm, self.done, self.zeroed = sem("fs_o_mm"), sem("fs_done"), sem("fs_zeroed")

    def seed(self, pool, dve):
        if pool is not None:
            pool.nop().then_inc(self.lf_copied, self.KR)
            pool.nop().then_inc(self.k_used, self.KR)
            pool.nop().then_inc(self.v_used, self.VR)
            self.nc.gpsimd.memset(self.later[:, PAGES - 1], 0.0).then_inc(self.zeroed, 1)
        if dve is not None:
            dve.nop().then_inc(self.done, 1)
            self.nc.vector.memset(self.s[:, PAGES], NEG).then_inc(self.zeroed, 1)
            self.nc.vector.memset(self.mx[:, 64:P], 0.0).then_inc(self.zeroed, 1)
            dve.wait_ge(self.zeroed, 3)

    def load_table(self, sp):
        sp.dma_start(self.table[:], self.dram["table"]).then_inc(self.t_in, 16)
        sp.wait_ge(self.t_in, 16)

    def load(self, sp, b):
        for j in range(PAGES):
            page = sp.value_load(self.table[0:1, bass.ds(PAGES * b + PAGES - 1 - j, 1)], min_val=0, max_val=NPOOL - 1)
            sp.wait_ge(self.k_used, PAGES * b + j + 1)
            sp.wait_ge(self.lf_copied, PAGES * b + j + 1)
            sp.dma_start(self.kr[:, j % self.KR], self.dram["keys"][bass.ds(page, 1)].rearrange("a p n -> p (a n)"))\
              .then_inc(self.k_in[j % self.KR], 16)
        for j in range(PAGES):
            page = sp.value_load(self.table[0:1, bass.ds(PAGES * b + j, 1)], min_val=0, max_val=NPOOL - 1)
            sp.wait_ge(self.v_used, PAGES * b + j + 1)
            sp.dma_start(self.vr[:, j % self.VR], self.dram["values"][bass.ds(page, 1)].rearrange("a p n -> p (a n)"))\
              .then_inc(self.v_in[j % self.VR], 16)

    def in_value(self, b, j, ring):
        return 16 * (PAGES // ring * b + j // ring + 1)

    def pool(self, pool, b):
        pool.wait_ge(self.done, b + 1)
        for j in range(PAGES):
            g = PAGES - 1 - j
            pool.wait_ge(self.k_in[j % self.KR], self.in_value(b, j, self.KR))
            self.nc.gpsimd.tensor_tensor(self.lf[:, g], self.kr[:, j % self.KR, FT * PAGE:KROW], self.C["ones"][:, 0:NH],
                                         ALU.mult).then_inc(self.lf_copied, 1)
            if j < PAGES - 1:
                pool.wait_ge(self.lf_copied, self.KR + PAGES * b + j + 1)
                if j:
                    pool.wait_ge(self.lf_link, (PAGES - 1) * b + j)
                self.nc.gpsimd.tensor_tensor(self.later[:, g - 1], self.later[:, g], self.lf[:, g], ALU.add)\
                    .then_inc(self.lf_link, 1)

    def pe_scores(self, pe, b):
        nc, q = self.nc, self.keep["qbd"]
        pe.wait_ge(self.done, b + 1)
        cols = lambda i: q[:, i, bass.ds(b, 1)].rearrange("p a u t -> p (a u t)")
        for j in range(PAGES):
            g = PAGES - 1 - j
            pe.wait_ge(self.k_in[j % self.KR], self.in_value(b, j, self.KR))
            bank = (self.b0, self.b1)[g // 8]
            for i in range(FT):
                at = g % 8 * 64 + 16 * i
                mm = nc.tensor.matmul(bank[:, at:at + 16], self.kr[:, j % self.KR, i * PAGE:i * PAGE + PAGE], cols(i),
                                      start=True, stop=True)
            mm.then_inc(self.k_used, 1)
        for i in range(FT):
            nc.tensor.matmul(self.b2[0:64, 128 + 16 * i:144 + 16 * i], self.pb[:, FK0 + i, SEQ:TOK], cols(i), start=True, stop=True)
        pe.wait_ge(self.lf_link, (PAGES - 1) * (b + 1))
        pe.wait_ge(self.lf_copied, self.KR + PAGES * (b + 1))
        flat = lambda a: a[:].rearrange("p g h -> p (g h)")
        nc.tensor.matmul(self.b2[:, 0:128], self.C["tri"], flat(self.lf), start=True, stop=False)
        nc.tensor.matmul(self.b2[:, 0:128], self.C["ones"], flat(self.later), start=False, stop=True).then_inc(self.s_mm, 1)

    def pe_max(self, pe, b):
        nc = self.nc
        pe.wait_ge(self.maxed, b + 1)
        nc.tensor.transpose(self.b2[:, 192:320], self.mx[:], self.C["ident"]).then_inc(self.turned, 1)
        pe.wait_ge(self.max1, b + 1)
        nc.tensor.matmul(self.b2[:, 320:384], self.m1[:].broadcast_to([64, P]), self.C["ident"][0:64, 0:64],
                         start=True, stop=True).then_inc(self.max_mm, 1)

    def pe_values(self, pe, b):
        nc = self.nc
        pe.wait_ge(self.summed, b + 1)
        nc.tensor.matmul(self.b2[:, 384:448], self.C["ones"], self.sums[:], start=True, stop=True).then_inc(self.den_mm, 1)
        for j in range(PAGES):
            pe.wait_ge(self.v_in[j % self.VR], self.in_value(b, j, self.VR))
            for i in range(FT):
                mm = nc.tensor.matmul(self.b0[:, 16 * i:16 * i + 16], self.vr[:, j % self.VR, i * P:i * P + P],
                                      self.p[:, j, 16 * i:16 * i + 16], start=j == 0 and i == 0, stop=False,
                                      skip_group_check=True)
            mm.then_inc(self.v_used, 1)
        for i in range(FT):
            mm = nc.tensor.matmul(self.b0[:, 16 * i:16 * i + 16], self.keep["vn"][:, i * P:i * P + P],
                                  self.p[0:64, PAGES, 16 * i:16 * i + 16], start=False, stop=i == FT - 1,
                                  skip_group_check=True)
        mm.then_inc(self.o_mm, 1)

    def dve_scores(self, dve, b):
        nc = self.nc
        dve.wait_ge(self.s_mm, b + 1)
        nc.vector.tensor_copy(self.suf[:].rearrange("p g h -> p (g h)"), self.b2[:, 0:128]).then_inc(self.suf_ev, 1)
        g4 = lambda a: a.rearrange("p (g h t) -> p g h t", h=NH, t=NT)
        new, h8 = self.s[0:64, PAGES], (lambda a: a.rearrange("p (h t) -> p h t", h=NH))
        m = self.C["mnew"][0:64, bass.ds(NT * b, NT)][:, None, :].broadcast_to([64, NH, NT])
        nc.vector.tensor_tensor(h8(new), h8(self.b2[0:64, 128:192]), m, ALU.add).then_inc(self.new_link, 1)
        dve.wait_ge(self.suf_ev, b + 1)
        for k, bank in enumerate((self.b0, self.b1)):
            suf = self.suf[:, 8 * k:8 * k + 8, :, None].broadcast_to([P, 8, NH, NT])
            dst = self.s[:, 8 * k:8 * k + 8].rearrange("p g (h t) -> p g h t", h=NH)
            nc.vector.tensor_tensor(dst, g4(bank), suf, ALU.add)
        dve.wait_ge(self.new_link, b + 1)
        cn = self.keep["cnt"][:, :, None].broadcast_to([64, NH, NT])
        nc.vector.tensor_tensor(h8(new), h8(new), cn, ALU.subtract).then_inc(self.s_ev, 1)
        dve.wait_ge(self.s_ev, b + 1)
        nc.vector.tensor_reduce(self.mx[:, 0:64], self.s[:].rearrange("p g n -> p n g"), AX.X, ALU.max).then_inc(self.maxed, 1)
        dve.wait_ge(self.turned, b + 1)
        nc.vector.tensor_reduce(self.m1[:], self.b2[0:64, 192:320], AX.X, ALU.max).then_inc(self.max1, 1)
        dve.wait_ge(self.max_mm, b + 1)
        mb = self.b2[:, None, 320:384].broadcast_to([P, PAGES + 1, 64])
        nc.vector.tensor_tensor(self.p[:], self.s[:], mb, ALU.subtract).then_inc(self.less, 1)

    def act(self, act, b):
        act.wait_ge(self.less, b + 1)
        self.nc.scalar.activation(self.p[:], self.p[:], ACT.Exp).then_inc(self.exped, 1)

    def dve_values(self, dve, b):
        nc = self.nc
        dve.wait_ge(self.exped, b + 1)
        nc.vector.tensor_reduce(self.sums[:], self.p[:].rearrange("p g n -> p n g"), AX.X, ALU.add).then_inc(self.summed, 1)
        dve.wait_ge(self.den_mm, b + 1)
        nc.vector.reciprocal(self.rden[:], self.b2[:, 384:448]).then_inc(self.inverted, 1)
        dve.wait_ge(self.inverted, b + 1)
        dve.wait_ge(self.o_mm, b + 1)
        for u in range(2):
            r = slice(64 * u, 64 * u + 64)
            g = lambda a: a[r, 0:64].rearrange("p (i u t) -> p i u t", i=FT, u=2)[:, :, u]
            last = nc.vector.tensor_tensor(self.pb[r, FQ0:FQ0 + FT, bass.ds(SEQ + NT * b, NT)], g(self.b0), g(self.rden), ALU.mult)
        last.then_inc(self.done, 1)


def mix(nc, pb, C, keep, spare, dram):
    with Semaphores(nc) as sems, ExitStack() as ctx:
        sb = lambda n, s, d=F32: ctx.enter_context(nc.sbuf_tensor(n, s, d))
        sem = sems
        bank = [ctx.enter_context(nc.psum_tensor(f"m_bank{i}", [P, 512], F32)) for i in range(8)]
        room = spare[:].rearrange("p k n -> p (k n)")[:, 0:4 * NH * CH].rearrange("p (a h n) -> p a h n", a=2, h=NH)
        early = [sb(n, [P, 2, FT, CH]) for n in ("rw_exps", "rw_bk", "rw_cc_v")]
        late = [e[:].rearrange("p a f n -> p (a f) n") for e in early]
        buf = dict(bank=[bank[0][:], bank[1][:]], e1=early[0][:, 0], e3=early[0][:, 1], bf=early[1][:, 0], kf=early[1][:, 1],
                   cc=early[2][:, 0], vf=early[2][:, 1], tt=late[0], xt=late[1], x=late[2],
                   ar=sb("rw_ar", [P, FT, 2, CH]), ntg=room[:, 0], nkg=room[:, 1], rs=spare[:, DK - 1, TOK - 512:TOK],
                   bt=sb("rw_bt", [P, 512]), kt=sb("rw_kt", [P, 512]), vt=sb("rw_vt", [P, 512]), us=sb("rw_us", [P, 512]),
                   s_mid=sb("rw_s_mid", [P, FT, DH]), s=sb("rw_s", [P, FT, DH]))
        chunk = Rwkv(ctx, sems, nc, "", CH, 7, pb, C, keep, buf, False)
        zeroed, out = sem("m_zeroed"), sem("m_out")
        fp = FoxPrompt(ctx, sems, nc, pb, C, keep, [b[:] for b in bank[2:5]])
        fs = FoxSample(ctx, sems, nc, pb, C, keep, [b[:] for b in bank[5:8]], dram)
        block = ctx.enter_context(nc.Block())

        @block.sync
        def _(sp):
            fs.load_table(sp)
            with sp.Fori(0, NCH) as c:
                for k in range(2):
                    fs.load(sp, 2 * c + k)
            sp.wait_ge(chunk.done, 1 + NCH)
            sp.dma_start(dram["state_prompt"], buf["s"][:]).then_inc(out, 16)
            sp.wait_ge(out, 16)

        @block.gpsimd
        def _(pool):
            fs.seed(pool, None)
            with pool.Fori(0, NCH) as c:
                chunk.pool_v(pool, c)
                fp.pool(pool, c)
                for k in range(2):
                    fs.pool(pool, 2 * c + k)

        @block.vector
        def _(dve):
            nc.vector.memset(buf["s"][:], 0.0).then_inc(zeroed, 1)
            chunk.seed(dve)
            fp.seed(dve)
            fs.seed(None, dve)
            dve.wait_ge(zeroed, 1)
            with dve.Fori(0, NCH) as c:
                chunk.dve_operands(dve, c)
                chunk.dve_state_in(dve, c)
                chunk.dve_grams(dve, c)
                chunk.dve_invert(dve, c)
                chunk.dve_chunk(dve, c)
                fp.dve(dve, c)
                for k in range(2):
                    fs.dve_scores(dve, 2 * c + k)
                    fs.dve_values(dve, 2 * c + k)

        @block.scalar
        def _(act):
            with act.Fori(0, NCH) as c:
                chunk.act_exps(act, c)
                chunk.act_invert(act, c)
                chunk.act_chunk(act, c)
                fp.act(act, c)
                for k in range(2):
                    fs.act(act, 2 * c + k)

        @block.tensor
        def _(pe):
            with pe.Fori(0, NCH) as c:
                chunk.pe_grams(pe, c)
                chunk.pe_invert(pe, c)
                chunk.pe_chunk(pe, c)
                fp.pe(pe, c)
                for k in range(2):
                    fs.pe_scores(pe, 2 * c + k)
                    fs.pe_max(pe, 2 * c + k)
                    fs.pe_values(pe, 2 * c + k)
    with Semaphores(nc) as sems, ExitStack() as ctx:
        sb = lambda n, s, d=F32: ctx.enter_context(nc.sbuf_tensor(n, s, d))
        sem = sems
        bank = [ctx.enter_context(nc.psum_tensor(f"s_bank{i}", [P, 512], F32)) for i in range(2)]
        T = NB * NT
        buf = dict(bank=[bank[0][:], bank[1][:]],
                   cc=sb("sw_cc", [P, FT, T]), e1=sb("sw_e1", [P, FT, T]), e3=sb("sw_e3", [P, FT, T]),
                   ar=sb("sw_ar", [P, FT, 2, T]), bf=sb("sw_bf", [P, FT, T]), kf=sb("sw_kf", [P, FT, T]),
                   vf=sb("sw_vf", [P, FT, T]), bt=sb("sw_bt", [P, 512]), kt=sb("sw_kt", [P, 512]), vt=sb("sw_vt", [P, 512]),
                   ntg=sb("sw_ntg", [P, NH, 2 * T]), nkg=sb("sw_nkg", [P, NH, 2 * T]),
                   x=sb("sw_x", [P, NH, T]), xt=sb("sw_xt", [P, NH, T]), tt=sb("sw_tt", [P, NH, T]),
                   rs=sb("sw_rs", [P, 512]), us=sb("sw_us", [P, 512]), s0=sb("sw_s0", [P, FT, NB, DH]),
                   sa=sb("sw_sa", [P, FT, 2, T]), ux=sb("sw_ux", [P, 2, 2, 512]), vx=sb("sw_vx", [P, 2, 2, 512]),
                   s_loaded=sem("sw_s_loaded"), x_part=sem("sw_x_part"), y_taken=sem("sw_y_taken"), s_added=sem("sw_s_added"))
        sample = Rwkv(ctx, sems, nc, "_s", T, 3, pb, C, keep, buf, True)
        out = sem("s_out")
        block = ctx.enter_context(nc.Block())

        @block.sync
        def _(sp):
            sp.dma_start(buf["s0"][:], dram["state_in"]).then_inc(sample.s_loaded, 16)
            sp.wait_ge(sample.done, 1 + FT)
            sp.dma_start(dram["state_sample"], buf["s0"][:]).then_inc(out, 16)
            sp.wait_ge(out, 16)

        @block.gpsimd
        def _(pool):
            sample.pool_v(pool, 0)

        @block.vector
        def _(dve):
            sample.seed(dve)
            sample.dve_operands(dve, 0)
            sample.dve_grams(dve, 0)
            sample.dve_invert(dve, 0)
            dve.wait_ge(sample.s_loaded, 16)
            sample.dve_sample(dve)

        @block.scalar
        def _(act):
            sample.act_exps(act, 0)
            sample.act_invert(act, 0)
            sample.act_sample(act)

        @block.tensor
        def _(pe):
            sample.pe_grams(pe, 0)
            sample.pe_invert(pe, 0)
            sample.pe_sample(pe)


def finish_mixers(sems, nc, pb, C, dram, ya, yb):
    with ExitStack() as ctx:
        sb = lambda n, s, d=F32: ctx.enter_context(nc.sbuf_tensor(n, s, d))
        sem = sems
        ps = ctx.enter_context(nc.psum_tensor("d_ps", [P, 4, 2, 512], F32))
        par, rk8 = C["par"], pb[0:NH, RK0]
        g2, sq = sb("d_g2", [P, 512]), sb("d_sq", [P, 2, TOK])
        mean, rstd, bonus = sb("d_mean", [NH, TOK]), sb("d_rstd", [NH, TOK]), sb("d_bonus", [P, 2, TOK])
        loaded, sum_mm, mean_ev, mean_mm, centred = sem("d_loaded"), sem("d_sum_mm"), sem("d_mean_ev"), sem("d_mean_mm"), sem("d_centred")
        squared, sq_mm, rooted, inverted = sem("d_squared"), sem("d_sq_mm"), sem("d_rooted"), sem("d_inverted")
        spread, used, high, low, v_link = sem("d_spread"), sem("d_used"), sem("d_high"), sem("d_low"), sem("d_v_link")
        sel8 = C["sel8"].rearrange("p (f h) -> p f h", f=FT)
        selt8 = C["selt8"][0:NH].rearrange("p (f n) -> p f n", f=FT)
        cut = lambda half: slice(half * HALF, half * HALF + HALF)
        y = lambda f: pb[:, R0 + f]
        block = ctx.enter_context(nc.Block())

        @block.sync
        def _(sp):
            sp.dma_start(g2[:], dram["g2"]).then_inc(loaded, 16)

        @block.tensor
        def _(pe):
            for f in range(FT):
                for half in range(2):
                    mm = nc.tensor.matmul(ps[0:NH, 0, half, 0:HALF], sel8[:, f], y(f)[:, cut(half)], start=f == 0, stop=f == FT - 1)
            mm.then_inc(sum_mm, 1)
            pe.wait_ge(mean_ev, 1)
            for f in range(FT):
                for half in range(2):
                    mm = nc.tensor.matmul(ps[:, f, half, 0:HALF], selt8[:, f], mean[:, cut(half)], start=True, stop=True)
                mm.then_inc(mean_mm, 1)
            pe.wait_ge(centred, FT)
            for f in range(FT):
                pe.wait_ge(squared, f + 1)
                for half in range(2):
                    mm = nc.tensor.matmul(ps[0:NH, 0, half, 0:HALF], sel8[:, f], sq[:, f % 2, cut(half)], start=f == 0, stop=f == FT - 1)
                mm.then_inc(sq_mm, 1)
            pe.wait_ge(loaded, 16)
            pe.wait_ge(inverted, 1)
            for f in range(FT):
                for n in range(3):
                    k = 3 * f + n
                    if k >= 4:
                        pe.wait_ge(used, k - 3)
                    src = ((selt8[:, f], rstd), (selt8[:, f], rk8), (g2[:, f * P:f * P + P], pb[:, LG0]))[n]
                    for half in range(2):
                        mm = nc.tensor.matmul(ps[:, k % 4, half, 0:HALF], src[0], src[1][:, cut(half)], start=True, stop=True)
                    mm.then_inc(spread, 1)

        @block.scalar
        def _(act):
            act.wait_ge(sum_mm, 1)
            nc.scalar.activation(halves(mean[:]), ps[0:NH, 0, :, 0:HALF], ACT.Copy, scale=1.0 / DH).then_inc(mean_ev, 1)
            for f in range(FT):
                act.wait_ge(centred, f + 1)
                if f >= 2:
                    act.wait_ge(sq_mm, f - 1)
                nc.scalar.activation(sq[:, f % 2], y(f), ACT.Square).then_inc(squared, 1)
            act.wait_ge(sq_mm, FT)
            nc.scalar.activation(halves(rstd[:]), ps[0:NH, 0, :, 0:HALF], ACT.Sqrt, scale=1.0 / DH,
                                 bias=C["lnx_eps"]).then_inc(rooted, 1)
            for f in range(FT):
                nc.scalar.activation(yb[0][:, f], pb[:, FQ0 + f], ACT.Copy).then_inc(high, 1)
            for f in range(FT):
                act.wait_ge(v_link, 5 * f + 5)
                nc.scalar.activation(ya[0][:, f], y(f), ACT.Copy).then_inc(high, 1)

        @block.gpsimd
        def _(pool):
            for f in range(FT):
                pool.wait_ge(high, f + 1)
                nc.gpsimd.tensor_tensor(yb[1][:, f], pb[:, FQ0 + f], yb[0][:, f].bitcast(F32), ALU.subtract)
            for f in range(FT):
                pool.wait_ge(high, FT + f + 1)
                nc.gpsimd.tensor_tensor(ya[1][:, f], y(f), ya[0][:, f].bitcast(F32), ALU.subtract).then_inc(low, 1)

        @block.vector
        def _(dve):
            for f in range(FT):
                dve.wait_ge(mean_mm, f + 1)
                nc.vector.tensor_tensor(halves(y(f)), halves(y(f)), ps[:, f, :, 0:HALF], ALU.subtract).then_inc(centred, 1)
            dve.wait_ge(rooted, 1)
            nc.vector.reciprocal(rstd[:], rstd[:]).then_inc(inverted, 1)
            link = Chain(dve, v_link)
            for f in range(FT):
                bank = lambda n: ps[:, (3 * f + n) % 4, :, 0:HALF]
                dve.wait_ge(spread, 3 * f + 1)
                link(nc.vector.scalar_tensor_tensor(halves(y(f)), halves(y(f)), par("lnw", f), bank(0), ALU.mult, ALU.mult))
                dve.nop().then_inc(used, 1)
                dve.wait_ge(spread, 3 * f + 2)
                link(nc.vector.tensor_tensor(halves(bonus[:, f % 2]), halves(pb[:, V0 + f]), bank(1), ALU.mult))
                dve.nop().then_inc(used, 1)
                link(nc.vector.scalar_tensor_tensor(y(f), y(f), par("lnb", f), bonus[:, f % 2], ALU.add, ALU.add))
                dve.wait_ge(spread, 3 * f + 3)
                link(nc.vector.tensor_tensor(halves(y(f)), halves(y(f)), bank(2), ALU.mult))
                link(dve.nop())
                dve.nop().then_inc(used, 1)


def merge(sems, nc, dense, x, pb, dram, ya, yb, w_o, w_out):
    with ExitStack() as ctx:
        sb = lambda n, s, d=F32: ctx.enter_context(nc.sbuf_tensor(n, s, d))
        sem = sems
        raw = pb[:, 0:8].rearrange("p i n -> p (i n)")[:, 0:4 * DK * P].rearrange("p (s k n) -> p s k n", s=4, k=DK)
        gates = pb[:, 8:12].rearrange("p (b a) n -> p b a n", b=2)
        prod = pb[:, 12:16].rearrange("p (b a) n -> p b a n", b=2)
        y = pb[:, 16:18]
        dense.buffers(ctx, "_m", DK, raw)
        mh, ml = sb("e_mh", [P, DK, TOK], F32R), sb("e_ml", [P, DK, TOK], F32R)
        x_in, gate_in = sem("e_x_in"), [sem("e_gate_in0"), sem("e_gate_in1")]
        m_link, merged, high, y_added = sem("e_m_link"), sem("e_merged"), sem("e_high"), sem("e_y_added")
        outs, proj = dense.stage(2 * DK), dense.stage(DK)
        block = ctx.enter_context(nc.Block())

        @block.sync
        def _(sp):
            sp.dma_start(x[:], dram["x_saved"]).then_inc(x_in, 16)
            dense.load(sp, outs, FT, lambda n: w_o[bass.ds(n, 1)].rearrange("a p k n -> p (a k) n"))
            dense.load(sp, proj, DK, lambda n: w_out[bass.ds(n, 1)].rearrange("a p k n -> p (a k) n"))

        @block.vector
        def _(dve):
            dense.split(dve, outs, FT)
            dense.split(dve, proj, DK)

        @block.scalar
        def _(act):
            for t in tiles(act, *outs):
                if not t.odd:
                    act.wait_ge(merged, t.couple + 1)
                    src = dram["gates"].rearrange("(a n) p m -> n p a m", a=2)
                    act.dma_start(gates[:, t.twin], src[bass.ds(t.couple, 1)].rearrange("o p a m -> p (o a) m"))\
                       .then_inc(gate_in[t.twin], 16)
                act.wait_ge(dense.mm_done, t.t + 5)
                nc.scalar.activation(halves(prod[:, t.twin, t.odd]), dense.out(t), ACT.Copy).then_inc(dense.evacuated, 1)
            for t in tiles(act, *proj):
                act.wait_ge(dense.mm_done, t.t + 5)
                act.wait_ge(y_added, t.n + 1)
                nc.scalar.activation(halves(y[:, t.odd]), dense.out(t), ACT.Copy).then_inc(dense.evacuated, 1)

        @block.gpsimd
        def _(pool):
            pool.nop().then_inc(merged, 2)
            pool.nop().then_inc(y_added, 2)
            for t in tiles(pool, *outs):
                if not t.odd:
                    continue
                n, b = t.couple, t.twin
                pool.wait_ge(dense.evacuated, t.t + 5)
                pool.wait_ge(gate_in[b], 16 * t.turn + 16)
                nc.gpsimd.tensor_tensor(prod[:, b], prod[:, b], gates[:, b], ALU.mult).then_inc(m_link, 1)
                pool.wait_ge(m_link, 3 * n + 1)
                one = prod[:, b, 0:1]
                nc.gpsimd.tensor_tensor(one, one, prod[:, b, 1:2], ALU.add).then_inc(m_link, 1)
                pool.wait_ge(m_link, 3 * n + 2)
                nc.gpsimd.tensor_copy(mh[:, bass.ds(n, 1)], one).then_inc(m_link, 1)
                pool.wait_ge(m_link, 3 * n + 3)
                nc.gpsimd.tensor_tensor(ml[:, bass.ds(n, 1)], one, mh[:, bass.ds(n, 1)].bitcast(F32), ALU.subtract)\
                    .then_inc(merged, 1)
            pool.wait_ge(x_in, 16)
            for t in tiles(pool, *proj):
                pool.wait_ge(dense.evacuated, t.t + 5)
                xn = x[:, bass.ds(t.n, 1)]
                nc.gpsimd.tensor_tensor(xn, y[:, t.odd:t.odd + 1], xn, ALU.add).then_inc(y_added, 1)

        @block.tensor
        def _(pe):
            def branch(t):
                hi, lo = yb if t.odd else ya
                return dense.whole(hi, lo, FT)(t)
            dense.multiply(pe, outs, branch)
            pe.wait_ge(merged, 2 + DK)
            dense.multiply(pe, proj, dense.whole(mh, ml, DK))


def build(nc, a, o):
    with ExitStack() as top:
        sb = lambda n, s, d=F32: top.enter_context(nc.sbuf_tensor(n, s, d))
        dense = Dense(Semaphores(nc), nc)
        cc, pars = sb("t_consts", [P, N_CCOL]), sb("t_params", [P, N_PCOL])
        ones, minus, eps = sb("t_ones", [P, P]), sb("t_minus", [P, P]), sb("t_eps", [P, 2])
        x = sb("t_x", [P, DK, TOK])
        C = {n: cc[:, CCOL[n]:CCOL[n] + w] for n, w in CC_COLS.items()}
        C["par"] = lambda n, i=0, rows=P: pars[0:rows, PCOL[n] + i:PCOL[n] + i + 1]
        C.update(ones=ones[:], minus=minus[:], eps=eps[:, 0:1], lnx_eps=eps[0:NH, 1:2])
        gain = lambda n: pars[:, PCOL[n]:PCOL[n] + DK]
        started = nc.alloc_semaphore(name="t_started")
        with nc.Block() as block:
            @block.vector
            def _(dve):
                nc.vector.memset(ones[:], 1.0)
                nc.vector.memset(minus[:], -1.0)
                nc.vector.memset(eps[:, 0:1], NORM_EPS)
                nc.vector.memset(eps[:, 1:2], LNX_EPS)

            @block.sync
            def _(sp):
                dense.seed(sp)
                sp.dma_start(pars[:], a["params"]).then_inc(started, 16)
                sp.dma_start(x[:], a["x"]).then_inc(started, 16)
                sp.dma_start(cc[:], a["c1"]).then_inc(started, 16)
                sp.wait_ge(started, 48)

        with Semaphores(nc) as sems:
            ffn(sems, nc, dense, "_1", x, gain("n1"), C, a["up1"], [a["down1a"], a["down1b"]])

        gates = nc.dram_tensor("gates_saved", [N_GATE, P, TOK], F32, kind="Internal").ap()
        x_saved = nc.dram_tensor("x_saved", [P, DK, TOK], F32, kind="Internal").ap()
        with ExitStack() as mid:
            pb = mid.enter_context(nc.sbuf_tensor("t_pb", [P, N_P, TOK], F32))
            with Semaphores(nc) as sems:
                project(sems, nc, dense, x, gain("n2"), C, a["w_in"], pb, gates, x_saved)
            with ExitStack() as kept:
                kb = lambda n, s: kept.enter_context(nc.sbuf_tensor("k_" + n, s, F32))
                keep = {n: kb(n, s) for n, s in dict(
                    cum=[P, FT, TOK], kk=[P, FT, TOK], kka=[P, FT, TOK], cnt=[64, NH],
                    mid=[P, FT, NCH], mexp=[P, 3, FT, NCH], vn=[64, FT * P], qbd=[P, FT, NB, 2, NT]).items()}
                with Semaphores(nc) as sems:
                    prepare(sems, nc, pb, C, keep, dict(lora=a["lora"], shift_in=a["shift"], c2=a["c2"], v_out=o["v"],
                                                        k_out=o["k"], shift_out=o["shift"], logf_out=o["logf"]))
                mix(nc, pb, C, keep, x, dict(table=a["table"], keys=a["keys"], values=a["values"], state_in=a["state"],
                                             state_prompt=o["state_prompt"], state_sample=o["state_sample"]))
            fb = lambda n: mid.enter_context(nc.sbuf_tensor(n, [P, FT, TOK], F32R))
            ya, yb = (fb("t_ya_hi"), fb("t_ya_lo")), (fb("t_yb_hi"), fb("t_yb_lo"))
            with Semaphores(nc) as sems:
                finish_mixers(sems, nc, pb, C, dict(g2=a["g2"]), ya, yb)
            with Semaphores(nc) as sems:
                merge(sems, nc, dense, x, pb, dict(gates=gates, x_saved=x_saved), ya, yb, a["w_o"], a["w_out"])
        with Semaphores(nc) as sems:
            ffn(sems, nc, dense, "_2", x, gain("n3"), C, a["up2"], [a["down2a"], a["down2b"]],
                store=lambda sp, s: (sp.dma_start(o["x"], x[:]).then_inc(s, 16), sp.wait_ge(s, 16)))


def constants():
    s, t = np.arange(P)[:, None], np.arange(P)[None, :]
    f = lambda m: np.asarray(m, np.float32)
    c = {"ident": f(s == t), "low": f(np.concatenate([s < t, s <= t], 1)), "tri": f(s > t)}
    same = (s // NT == t // NT)[:64, :64]
    lows = np.concatenate([same & (s < t)[:64, :64], same & (s <= t)[:64, :64]], 1)
    c["lows"] = np.concatenate([f(lows), np.zeros((64, P), np.float32)])
    c["lev"] = f(np.concatenate([(s // (2 * b) == t // (2 * b)) & (s // b % 2 == 1) & (t // b % 2 == 0)
                                 for b in (1, 2, 4, 8, 16, 32, 64)], 1))
    c["causal"] = np.where(t > s, np.float32(NEG), np.float32(0))
    new = np.where(lows[:, 64:], np.float32(0), np.float32(NEG))
    c["mnew"] = np.concatenate([new, np.zeros((64, 64), np.float32)])
    c["bmask"] = f(s // NT == np.arange(NB)[None, :])
    head = lambda ft, n, at: f(np.arange(n)[None, :] == at + 2 * ft + s // DH)
    c["sel8"] = np.concatenate([head(ft, NH, 0) for ft in range(FT)], 1)
    pad = lambda m: np.concatenate([m, np.zeros((P - m.shape[0], m.shape[1]), np.float32)])
    c["selt8"] = np.concatenate([pad(head(ft, NH, 0).T) for ft in range(FT)], 1)
    col = np.arange(TOK)[None, :]
    start = (col - SEQ) % NT == 0
    c2 = {"sel24": np.concatenate([head(i % FT, 24, 8 * (i // FT)) for i in range(12)], 1),
          "selt": np.concatenate([pad(head(i % FT, 24, 8 * (i // FT)).T) for i in range(12)], 1),
          "reset": np.tile(f(~np.where(col < SEQ, col % CH == 0, start)), (P, 1)),
          "fresh": np.tile(f(~np.where(col < SEQ, col == 0, start)), (P, 1))}
    pack = lambda d, widths: np.ascontiguousarray(np.concatenate([d[n] for n in widths], 1))
    return pack(c, CC_COLS), pack(c2, CC2_COLS)


def weight_tiles(w):
    k, n = w.shape
    return w.reshape(k // P, P, n // P, P).transpose(2, 1, 0, 3)


def columns_of(v):
    return v.reshape(-1, P).T


def kernel(x_prompt, x_sample, cache_k, cache_v, cache_logf, state_wkv, state_shift, page_table,
           ffn1_norm, ffn1_wg, ffn1_wu, ffn1_wd, mix_norm, w_in, shift_mu,
           rwkv_w0, rwkv_w2, rwkv_a0, rwkv_a2, rwkv_g2, rwkv_k_k, rwkv_k_a, rwkv_r_k, rwkv_lnx_w, rwkv_lnx_b,
           fox_b_f, fox_q_norm, fox_k_norm, w_o_a, w_o_b, w_out,
           ffn2_norm, ffn2_wg, ffn2_wu, ffn2_wd):
    import concourse.bacc as bacc
    from concourse.bass_utils import run_bass_kernel_spmd

    A = lambda v: np.asarray(v)
    arrays = {}

    def put(name, v):
        arrays[name] = np.ascontiguousarray(v)

    x = np.concatenate([A(x_prompt)[0], A(x_sample).reshape(NB * NT, D)])
    put("x", x.T.reshape(DK, P, TOK).transpose(1, 0, 2))
    for n, wg, wu, wd in (("1", ffn1_wg, ffn1_wu, ffn1_wd), ("2", ffn2_wg, ffn2_wu, ffn2_wd)):
        up = np.stack([weight_tiles(A(wg)[0]), weight_tiles(A(wu)[0])], 1)
        put("up" + n, up.reshape(2 * sum(UP), P, DK, P))
        put(f"down{n}a", weight_tiles(A(wd)[0][:UP[0] * P]))
        put(f"down{n}b", weight_tiles(A(wd)[0][UP[0] * P:]))
    w = A(w_in)[0]
    f0 = (N_P - 1) * P
    w = np.concatenate([w[:, :f0 + NH], np.zeros((D, P - NH), w.dtype), w[:, f0 + NH:]], 1)
    put("w_in", weight_tiles(w))
    put("w_o", np.stack([weight_tiles(A(w_o_a)[0]), weight_tiles(A(w_o_b)[0])], 1).reshape(2 * DK, P, FT, P))
    put("w_out", weight_tiles(A(w_out)[0]))
    put("lora", np.concatenate([A(rwkv_w2)[0], A(rwkv_a2)[0]]))
    put("g2", A(rwkv_g2)[0])
    put("shift", A(state_shift)[0].T.reshape(N_SH, P, NB).transpose(1, 0, 2))
    put("state", A(state_wkv)[0].transpose(1, 3, 0, 2).reshape(FT, P, NB, DH).transpose(1, 0, 2, 3))
    put("table", A(page_table).reshape(1, -1))
    keys = A(cache_k)[0].reshape(NPOOL, PAGE, FT, 2 * DH).transpose(0, 3, 2, 1).reshape(NPOOL, P, FT * PAGE)
    put("keys", np.concatenate([keys, A(cache_logf)[0]], 2))
    put("values", A(cache_v)[0].reshape(NPOOL, PAGE, NH * DH))
    fill = lambda v, n: np.concatenate([v, np.zeros(P - n, np.float32)])
    stat = lambda p, q: np.concatenate([np.full(16, p, np.float32), np.full(8, q, np.float32)])
    cols = dict(n1=A(ffn1_norm)[0], n2=A(mix_norm)[0], n3=A(ffn2_norm)[0], mu=A(shift_mu)[0], w0=A(rwkv_w0)[0],
                a0=A(rwkv_a0)[0], kk=A(rwkv_k_k)[0], ka=A(rwkv_k_a)[0], rk=A(rwkv_r_k)[0].reshape(-1),
                lnw=A(rwkv_lnx_w)[0], lnb=A(rwkv_lnx_b)[0], qn=np.tile(A(fox_q_norm)[0], 2), kn=np.tile(A(fox_k_norm)[0], 2),
                bf=fill(A(fox_b_f)[0], NH), sc=fill(stat(1 / DH, 1), 24), ad=fill(stat(NORM_EPS, 0), 24))
    put("params", np.concatenate([columns_of(cols[n]) for n in PC_COLS], 1))
    c1, c2 = constants()
    put("c1", c1)
    put("c2", c2)

    outs = dict(x=(P, DK, TOK), k=(P, FT, TOK), v=(P, FT, TOK), logf=(NH, TOK), shift=(P, N_SH, 1 + NB),
                state_prompt=(P, FT, DH), state_sample=(P, FT, NB, DH))
    nc = bacc.Bacc("TRN2", target_bir_lowering=False, num_devices=1)
    a = {n: nc.dram_tensor("in_" + n, v.shape, mybir.dt.from_np(v.dtype), kind="ExternalInput").ap() for n, v in arrays.items()}
    o = {n: nc.dram_tensor("out_" + n, s, F32, kind="ExternalOutput").ap() for n, s in outs.items()}
    build(nc, a, o)
    r = run_bass_kernel_spmd(nc, [{"in_" + n: v for n, v in arrays.items()}], core_ids=[0]).results[0]
    r = {n: np.asarray(r["out_" + n]) for n in outs}

    rows = lambda v: v.transpose(2, 1, 0).reshape(v.shape[2], -1)
    xo, ko, vo, sh = rows(r["x"]), rows(r["k"]), rows(r["v"]), rows(r["shift"])
    lf = r["logf"].T
    p = lambda v, *s: np.ascontiguousarray(v[:SEQ]).reshape(1, 1, SEQ, *s)
    q = lambda v, *s: np.ascontiguousarray(v[SEQ:]).reshape(1, NB, NT, *s)
    sp = r["state_prompt"].reshape(2, DH, FT, 1, DH).transpose(3, 2, 0, 4, 1).reshape(1, 1, NH, DH, DH)
    ss = r["state_sample"].reshape(2, DH, FT, NB, DH).transpose(3, 2, 0, 4, 1).reshape(1, NB, NH, DH, DH)
    return (np.ascontiguousarray(xo[:SEQ])[None], np.ascontiguousarray(xo[SEQ:]).reshape(NB, NT, D),
            p(ko, NH, DH), p(vo, NH, DH), p(lf, NH), np.ascontiguousarray(sp), np.ascontiguousarray(sh[:1])[None],
            q(ko, NH, DH), q(vo, NH, DH), q(lf, NH), np.ascontiguousarray(ss), np.ascontiguousarray(sh[1:])[None])
```

```python
from contextlib import ExitStack

import numpy as np

import concourse.bass as bass
from concourse import mybir

F32 = mybir.dt.float32
F32R = mybir.dt.float32r
I32 = mybir.dt.int32
ACT = mybir.ActivationFunctionType
ALU = mybir.AluOpType
AX = mybir.AxisListType

P = 128
D = 1024
DK = D // P
SEQ = 512
NB, NT = 8, 8
TOK = SEQ + NB * NT
HALF = TOK // 2
DH = 64
NH = 8
FT = NH * DH // P
D_FF = 2816
UP = (12, 10)
N_SH = 14
N_P = 27
N_GATE = 16
CH = 128
NCH = SEQ // CH
PAGES = 16
PAGE = 128
NPOOL = 160
KAPPA = float(np.exp(-0.5))
NORM_EPS, LNX_EPS = 1e-6, 64e-5
NEG = -1e30
PAST = PAGES * PAGE
SLOTK = 12

PC_COLS = dict(n1=8, n2=8, n3=8, mu=14, w0=4, a0=4, kk=4, ka=4, rk=4, lnw=4, lnb=4, qn=1, kn=1, bf=1, sc=1, ad=1)
CC_COLS = dict(ident=P, low=2 * P, lows=P, lev=7 * P, causal=P, bmask=NB, sel8=FT * NH, selt8=FT * P)
CC2_COLS = dict(sel24=12 * 24, selt=12 * P, reset=TOK, fresh=TOK, mnew=NCH * 64, nsel=P)


def columns(widths):
    at, out = 0, {}
    for name, n in widths.items():
        out[name] = at
        at += n
    return out, at


CCOL, N_CCOL = columns(CC_COLS)
CCOL2, N_CCOL2 = columns(CC2_COLS)
PCOL, N_PCOL = columns(PC_COLS)


class Tile:

    def __init__(self, first, i, j):
        self.n = 4 * i + j
        self.t = first + self.n
        self.slot = (first + j) % 4
        self.pair = (first + j) % 2
        self.use = i + (first + j) // 4
        self.couple = 2 * i + j // 2
        self.twin = j // 2 % 2
        self.odd = j % 2
        self.turn = i


def tiles(eng, first, count):
    turns = count // 4
    if turns > 1:
        with eng.Fori(0, turns) as i:
            for j in range(4):
                yield Tile(first, i, j)
    elif turns:
        for j in range(4):
            yield Tile(first, 0, j)
    for j in range(count % 4):
        yield Tile(first, turns, j)


class Chain:

    def __init__(self, eng, sem):
        self.eng, self.sem, self.n, self.turn, self.inside = eng, sem, 0, None, 0

    def __call__(self, ins):
        self.n += 1
        ins.then_inc(self.sem, 1)
        self.eng.wait_ge(self.sem, self.n if self.turn is None else self.turn + self.n)

    def loop(self, i, per):
        self.before, self.per, self.n, self.turn = self.n, per, 0, i * per + self.n

    def end(self, turns):
        assert self.n == self.per, (self.sem, self.n, self.per)
        self.n, self.turn = self.before + turns * self.per, None


class Semaphores:

    def __init__(self, nc):
        self.nc, self.held = nc, []

    def __call__(self, name):
        self.held.append(self.nc.alloc_semaphore(name=name))
        return self.held[-1]

    def __enter__(self):
        return self

    def __exit__(self, kind, error, trace):
        if kind is None:
            self.nc.clear_and_free_semaphores(self.held)
            self.nc.all_engine_barrier()


class Dense:

    def __init__(self, sems, nc):
        self.nc = nc
        sem = sems
        self.landed = [sem(f"w_landed{s}") for s in range(4)]
        self.rounded = sem("w_rounded")
        self.split_done = sem("w_split")
        self.mm_done = sem("w_multiplied")
        self.evacuated = sem("w_evacuated")
        self.t = 0

    def buffers(self, ctx, tag, k=SLOTK, raw=None):
        nc = self.nc
        sb = lambda n, s, d: ctx.enter_context(nc.sbuf_tensor(n, s, d))
        self.raw = sb("w_raw" + tag, [P, 4, k, P], F32) if raw is None else raw
        self.wh = sb("w_hi" + tag, [P, 2, k, P], F32R)
        self.wl = sb("w_lo" + tag, [P, 2, k, P], F32R)
        self.ps = ctx.enter_context(nc.psum_tensor("ps" + tag, [P, 4, 2, 512], F32))

    def stage(self, count):
        first, self.t = self.t, self.t + count
        return first, count

    def seed(self, sp):
        sp.nop().then_inc(self.split_done, 4)
        sp.nop().then_inc(self.mm_done, 4)
        sp.nop().then_inc(self.evacuated, 4)

    def load(self, sp, st, kn, src):
        for x in tiles(sp, *st):
            sp.wait_ge(self.split_done, x.t + 1)
            sp.dma_start(self.raw[:, x.slot, 0:kn], src(x.n)).then_inc(self.landed[x.slot], 16)

    def split(self, dve, st, kn):
        for x in tiles(dve, *st):
            dve.wait_ge(self.landed[x.slot], 16 * x.use + 16)
            dve.wait_ge(self.mm_done, x.t + 3)
            hi, lo, raw = self.wh[:, x.pair, 0:kn], self.wl[:, x.pair, 0:kn], self.raw[:, x.slot, 0:kn]
            self.nc.vector.tensor_copy(hi, raw).then_inc(self.rounded, 1)
            dve.wait_ge(self.rounded, x.t + 1)
            self.nc.vector.tensor_tensor(lo, raw, hi.bitcast(F32), ALU.subtract).then_inc(self.split_done, 1)

    def multiply(self, pe, st, groups):
        for x in tiles(pe, *st):
            pe.wait_ge(self.split_done, x.t + 5)
            pe.wait_ge(self.evacuated, x.t + 1)
            for out, k0, operands in groups(x):
                for half in range(2):
                    cut = slice(half * HALF, (half + 1) * HALF)
                    for k, (hi, lo) in enumerate(operands):
                        wh, wl = self.wh[:, x.pair, k0 + k], self.wl[:, x.pair, k0 + k]
                        self.nc.tensor.matmul(out(half), wh, hi[:, cut], start=k == 0, stop=False)
                        self.nc.tensor.matmul(out(half), wh, lo[:, cut], start=False, stop=False)
                        last = self.nc.tensor.matmul(out(half), wl, hi[:, cut], start=False,
                                                     stop=k == len(operands) - 1)
            last.then_inc(self.mm_done, 1)

    def whole(self, hi, lo, kn):
        ops = [(hi[:, k], lo[:, k]) for k in range(kn)]
        return lambda x: [(lambda half: self.ps[:, x.slot, half, 0:HALF], 0, ops)]

    def out(self, x):
        return self.ps[:, x.slot, :, 0:HALF]


def halves(ap):
    return ap.rearrange("p (h n) -> p h n", h=2)


class Norm:

    BLOCKS = [(j * P, j * P, j * P + P) for j in range(SEQ // P)] + [(TOK - P, SEQ, TOK)]

    def __init__(self, ctx, sems, nc, tag, x, gain, consts, nh, nl, ps):
        sb = lambda n, s, d=F32: ctx.enter_context(nc.sbuf_tensor(n + tag, s, d))
        sem = lambda n: sems(n + tag)
        self.nc, self.x, self.gain, self.consts, self.nh, self.nl, self.ps = nc, x, gain, consts, nh, nl, ps
        self.sq = sb("n_sq", [P, 2, TOK])
        self.sum = sb("n_sum", [P, TOK])
        self.rs = sb("n_rs", [P, 8])
        self.y = sb("n_y", [P, 2, TOK])
        self.squared, self.added, self.summed, self.meaned = sem("n_squared"), sem("n_added"), sem("n_summed"), sem("n_meaned")
        self.rooted, self.inverted, self.spread = sem("n_rooted"), sem("n_inverted"), sem("n_spread")
        self.scaled, self.high, self.split = sem("n_scaled"), sem("n_high"), sem("n_split")

    def act(self, act):
        nc = self.nc
        for k in range(DK):
            if k >= 2:
                act.wait_ge(self.added, k - 1)
            nc.scalar.activation(self.sq[:, k % 2], self.x[:, k], ACT.Square).then_inc(self.squared, 1)
        act.wait_ge(self.meaned, 1)
        nc.scalar.activation(self.rs[:, 0:5], self.ps[:, 0, 0, 0:5], ACT.Sqrt, scale=1.0 / D,
                             bias=self.consts["eps"]).then_inc(self.rooted, 1)
        for k in range(DK):
            act.wait_ge(self.scaled, k + 1)
            nc.scalar.activation(self.nh[:, k], self.y[:, k % 2], ACT.Copy).then_inc(self.high, 1)

    def pe(self, pe):
        nc = self.nc
        pe.wait_ge(self.summed, 1)
        for j, (a, _, _) in enumerate(self.BLOCKS):
            mm = nc.tensor.matmul(self.ps[:, 0, 0, j:j + 1], self.sum[:, a:a + P],
                                  self.consts["ones"][:, 0:1], start=True, stop=True)
        mm.then_inc(self.meaned, 1)
        pe.wait_ge(self.inverted, 1)
        for j, (at, lo, hi) in enumerate(self.BLOCKS):
            for a, b in ((lo, min(hi, HALF)), (max(lo, HALF), hi)):
                if b > a:
                    h, o = divmod(a, HALF)
                    mm = nc.tensor.matmul(self.ps[:, 1, h, o:o + b - a], self.rs[:, j:j + 1].broadcast_to([P, P]),
                                          self.consts["ident"][:, a - at:b - at], start=True, stop=True)
        mm.then_inc(self.spread, 1)

    def dve(self, dve):
        nc = self.nc
        for k in range(DK):
            dve.wait_ge(self.squared, k + 1)
            if k:
                dve.wait_ge(self.added, k)
                nc.vector.tensor_tensor(self.sum[:], self.sum[:], self.sq[:, k % 2], ALU.add).then_inc(self.added, 1)
            else:
                nc.vector.tensor_copy(self.sum[:], self.sq[:, 0]).then_inc(self.added, 1)
        dve.wait_ge(self.added, DK)
        dve.nop().then_inc(self.summed, 1)
        dve.wait_ge(self.rooted, 1)
        nc.vector.reciprocal(self.rs[:, 0:5], self.rs[:, 0:5]).then_inc(self.inverted, 1)
        dve.wait_ge(self.spread, 1)
        for k in range(DK):
            if k >= 2:
                dve.wait_ge(self.split, k - 1)
            nc.vector.scalar_tensor_tensor(halves(self.y[:, k % 2]), halves(self.x[:, k]), self.gain[:, k:k + 1],
                                           self.ps[:, 1, :, 0:HALF], ALU.mult, ALU.mult).then_inc(self.scaled, 1)
            if k:
                self.low(dve, k - 1)
        self.low(dve, DK - 1)

    def low(self, dve, k):
        dve.wait_ge(self.high, k + 1)
        self.nc.vector.tensor_tensor(self.nl[:, k], self.y[:, k % 2], self.nh[:, k].bitcast(F32),
                                     ALU.subtract).then_inc(self.split, 1)


def ffn(sems, nc, dense, tag, x, gain, consts, w_up, w_down, load_first=None, store=None):
    with ExitStack() as ctx:
        sb = lambda n, s, d=F32: ctx.enter_context(nc.sbuf_tensor(n + tag, s, d))
        sem = lambda n: sems(n + tag)
        dense.buffers(ctx, tag)
        nh, nl = sb("f_nh", [P, DK, TOK], F32R), sb("f_nl", [P, DK, TOK], F32R)
        hh, hl = sb("f_hh", [P, UP[0], TOK], F32R), sb("f_hl", [P, UP[0], TOK], F32R)
        gate, up, y = sb("f_gate", [P, 2, TOK]), sb("f_up", [P, 2, TOK]), sb("f_y", [P, 2, TOK])
        norm = Norm(ctx, sems, nc, tag, x, gain, consts, nh, nl, dense.ps)
        hid_link, hid_split, y_added = sem("hid_link"), sem("hid_split"), sem("y_added")
        x_loaded, x_stored = sem("x_loaded"), sem("x_stored")
        stages = []
        for n in UP:
            stages += [dense.stage(2 * n), dense.stage(DK)]
        before = [0, UP[0]]

        def wait_x(eng):
            if load_first is not None:
                eng.wait_ge(x_loaded, load_first.count)

        block = ctx.enter_context(nc.Block())

        @block.sync
        def _(sp):
            if load_first is not None:
                load_first(sp, x_loaded)
            for half, n in enumerate(UP):
                src = w_up[2 * before[half]:2 * before[half] + 2 * n]
                dense.load(sp, stages[2 * half], DK, lambda t: src[bass.ds(t, 1)].rearrange("a p k n -> p (a k) n"))
                down = w_down[half]
                dense.load(sp, stages[2 * half + 1], n, lambda t: down[bass.ds(t, 1)].rearrange("a p k n -> p (a k) n"))
            if store is not None:
                sp.wait_ge(y_added, 2 + 2 * DK)
                store(sp, x_stored)

        @block.vector
        def _(dve):
            wait_x(dve)
            norm.dve(dve)
            for half, n in enumerate(UP):
                dense.split(dve, stages[2 * half], DK)
                dense.split(dve, stages[2 * half + 1], n)

        @block.scalar
        def _(act):
            wait_x(act)
            norm.act(act)
            for half, n in enumerate(UP):
                for t in tiles(act, *stages[2 * half]):
                    act.wait_ge(dense.mm_done, t.t + 5)
                    if not t.odd:
                        act.wait_ge(hid_split, before[half] + t.couple + 1)
                    buf, func = ((gate, ACT.Silu), (up, ACT.Copy))[t.odd]
                    nc.scalar.activation(halves(buf[:, t.twin]), dense.out(t), func).then_inc(dense.evacuated, 1)
                for t in tiles(act, *stages[2 * half + 1]):
                    act.wait_ge(dense.mm_done, t.t + 5)
                    act.wait_ge(y_added, DK * half + t.n + 1)
                    nc.scalar.activation(halves(y[:, t.odd]), dense.out(t), ACT.Copy, scale=0.5)\
                        .then_inc(dense.evacuated, 1)

        @block.gpsimd
        def _(pool):
            pool.nop().then_inc(hid_split, 2)
            pool.nop().then_inc(y_added, 2)
            wait_x(pool)
            for half, n in enumerate(UP):
                if half:
                    pool.wait_ge(dense.mm_done, stages[2][0] + 4)
                for t in tiles(pool, *stages[2 * half]):
                    if not t.odd:
                        continue
                    pool.wait_ge(dense.evacuated, t.t + 5)
                    c = before[half] + t.couple
                    k, b = bass.ds(t.couple, 1), slice(t.twin, t.twin + 1)
                    nc.gpsimd.tensor_tensor(up[:, b], gate[:, b], up[:, b], ALU.mult).then_inc(hid_link, 1)
                    pool.wait_ge(hid_link, 2 * c + 1)
                    nc.gpsimd.tensor_copy(hh[:, k], up[:, b]).then_inc(hid_link, 1)
                    pool.wait_ge(hid_link, 2 * c + 2)
                    nc.gpsimd.tensor_tensor(hl[:, k], up[:, b], hh[:, k].bitcast(F32), ALU.subtract)\
                        .then_inc(hid_split, 1)
                for t in tiles(pool, *stages[2 * half + 1]):
                    pool.wait_ge(dense.evacuated, t.t + 5)
                    xn = x[:, bass.ds(t.n, 1)]
                    nc.gpsimd.tensor_tensor(xn, y[:, t.odd:t.odd + 1], xn, ALU.add).then_inc(y_added, 1)

        @block.tensor
        def _(pe):
            wait_x(pe)
            norm.pe(pe)
            pe.wait_ge(norm.split, DK)
            for half, n in enumerate(UP):
                dense.multiply(pe, stages[2 * half], dense.whole(nh, nl, DK))
                pe.wait_ge(hid_split, 2 + before[half] + n)
                dense.multiply(pe, stages[2 * half + 1], dense.whole(hh, hl, n))


def project(sems, nc, dense, x, gain, consts, w_in, pb, gates_dram, x_dram, past, table_dram, logf_dram):
    with ExitStack() as ctx:
        sb = lambda n, s, d=F32: ctx.enter_context(nc.sbuf_tensor(n, s, d))
        sem = sems
        dense.buffers(ctx, "_p")
        nh, nl = sb("p_nh", [P, DK, TOK], F32R), sb("p_nl", [P, DK, TOK], F32R)
        gate = sb("p_gate", [P, 2, TOK])
        norm = Norm(ctx, sems, nc, "_p", x, gain, consts, nh, nl, dense.ps)
        gate_stored = [sem("gate_stored0"), sem("gate_stored1")]
        table = sb("p_table", [1, NB * PAGES], I32)
        x_saved, table_in, past_in = sem("x_saved"), sem("p_table_in"), sem("p_past_in")
        plain, gates = dense.stage(N_P), dense.stage(N_GATE)
        block = ctx.enter_context(nc.Block())

        @block.sync
        def _(sp):
            sp.dma_start(x_dram, x[:]).then_inc(x_saved, 16)
            dense.load(sp, plain, DK, lambda n: w_in[bass.ds(n, 1)].rearrange("a p k n -> p (a k) n"))
            dense.load(sp, gates, DK, lambda n: w_in[N_P:][bass.ds(n, 1)].rearrange("a p k n -> p (a k) n"))
            sp.wait_ge(x_saved, 16)

        @block.gpsimd
        def _(pool):
            for s in gate_stored:
                pool.nop().then_inc(s, 16)
            pool.dma_start(table[:], table_dram).then_inc(table_in, 16)
            nc.gpsimd.memset(past[0:64, 0:1], 0.0)
            pool.wait_ge(table_in, 16)
            for b in range(NB):
                with pool.Fori(0, PAGES) as j:
                    page = pool.value_load(table[0:1, bass.ds(PAGES * b + PAGES - 1 - j, 1)], min_val=0, max_val=NPOOL - 1)
                    pool.dma_start(past[NH * b:NH * b + NH, bass.ds(1 + j * PAGE, PAGE)],
                                   logf_dram[bass.ds(page, 1)].rearrange("a h n -> (a h) n")).then_inc(past_in, 16)
            pool.wait_ge(past_in, 16 * NB * PAGES)

        @block.vector
        def _(dve):
            norm.dve(dve)
            dense.split(dve, plain, DK)
            dense.split(dve, gates, DK)

        @block.scalar
        def _(act):
            norm.act(act)
            for t in tiles(act, *plain):
                act.wait_ge(dense.mm_done, t.t + 5)
                out = pb[:, bass.ds(t.n, 1)].rearrange("p a (h n) -> p (a h) n", h=2)
                nc.scalar.activation(out, dense.out(t), ACT.Copy).then_inc(dense.evacuated, 1)
            for t in tiles(act, *gates):
                act.wait_ge(dense.mm_done, t.t + 5)
                act.wait_ge(gate_stored[t.odd], 16 * t.couple + 16)
                nc.scalar.activation(halves(gate[:, t.odd]), dense.out(t), ACT.Sigmoid).then_inc(dense.evacuated, 1)
                act.wait_ge(dense.evacuated, t.t + 5)
                act.dma_start(gates_dram[bass.ds(t.n, 1)].rearrange("a p n -> p (a n)"), gate[:, t.odd])\
                   .then_inc(gate_stored[t.odd], 16)
            for s in gate_stored:
                act.wait_ge(s, 16 * (N_GATE // 2) + 16)

        @block.tensor
        def _(pe):
            norm.pe(pe)
            pe.wait_ge(norm.split, DK)
            dense.multiply(pe, plain, dense.whole(nh, nl, DK))
            dense.multiply(pe, gates, dense.whole(nh, nl, DK))


RK0 = 12
R0, K0, V0, LW0, LG0, FQ0, FK0, FV0, FF0 = 0, 4, 8, 12, 13, 14, 18, 22, 26


def prepare(sems, nc, pb, C, keep, past, dram):
    with ExitStack() as ctx:
        sb = lambda n, s, d=F32: ctx.enter_context(nc.sbuf_tensor(n, s, d))
        sem = sems
        ps = ctx.enter_context(nc.psum_tensor("c_ps", [P, 4, 2, 512], F32))
        c2 = sb("c_c2", [P, N_CCOL2])
        K = lambda name, rows=P: c2[0:rows, CCOL2[name]:CCOL2[name] + CC2_COLS[name]]
        lora = sb("c_lora", [P, 512])
        shift = sb("c_shift", [P, N_SH, NB])
        newshift = sb("c_newshift", [P, N_SH, 1 + NB])
        diff = sb("c_diff", [P, 4, TOK])
        lw = sb("c_lw", [P, FT, TOK])
        sq = sb("c_sq", [P, 2, TOK])
        st = sb("c_st", [24, TOK])
        gq = sb("c_gq", [P, 1])
        tmp = sb("c_tmp", [P, 2, TOK])
        f_z, f_m, f_a, f_e = sb("c_fz", [NH, TOK]), sb("c_fm", [NH, TOK]), sb("c_fa", [NH, TOK]), sb("c_fe", [NH, TOK])
        cum, kk, kka = keep["cum"], keep["kk"], keep["kka"]
        rk8, cn = pb[0:NH, RK0], pb[0:NH, FF0]
        par = C["par"]

        loaded, mixed, shifted, lora_act = sem("c_loaded"), sem("c_mixed"), sem("c_shifted"), sem("c_lora_act")
        lora_mm, lora_out, squares = sem("c_lora_mm"), sem("c_lora_out"), sem("c_squares")
        sq_used, kraw, biased, rooted, inverted = sem("c_sq_used"), sem("c_kraw"), sem("c_biased"), sem("c_rooted"), sem("c_inverted")
        spread, normed, scanned = sem("c_spread"), sem("c_normed"), sem("c_scanned")
        f_abs, f_exp, f_log, f_done = sem("c_f_abs"), sem("c_f_exp"), sem("c_f_log"), sem("c_f_done")
        rkprod, rksum, tp, mids, summed = sem("c_rkprod"), sem("c_rksum"), sem("c_tp"), sem("c_mids"), sem("c_summed")
        v_link, a_link, stored = sem("c_v_link"), sem("c_a_link"), sem("c_stored")
        block = ctx.enter_context(nc.Block())

        @block.sync
        def _(sp):
            sp.dma_start(lora[:], dram["lora"]).then_inc(loaded, 16)
            sp.dma_start(shift[:], dram["shift_in"]).then_inc(loaded, 16)
            sp.dma_start(c2[:], dram["c2"]).then_inc(loaded, 16)
            sp.dma_start(dram["v_out"], pb[:, FV0:FV0 + FT]).then_inc(stored, 16)
            sp.wait_ge(shifted, 1)
            sp.dma_start(dram["shift_out"], newshift[:]).then_inc(stored, 16)
            sp.wait_ge(f_done, 1)
            sp.dma_start(dram["logf_out"], f_z[:]).then_inc(stored, 16)
            sp.wait_ge(normed, 8)
            sp.dma_start(dram["k_out"], pb[:, FK0:FK0 + FT]).then_inc(stored, 16)
            sp.wait_ge(summed, 1)
            sp.dma_start(dram["later"], past[0:64, 0:PAST]).then_inc(stored, 16)
            sp.wait_ge(stored, 80)

        @block.vector
        def _(dve):
            link = Chain(dve, v_link)
            tail = lambda a: a[:, :, SEQ:TOK].rearrange("p i (b t) -> p i b t", b=NB)
            dve.wait_ge(loaded, 48)
            nc.vector.tensor_copy(newshift[:, :, 0:1], pb[:, 0:N_SH, SEQ - 1:SEQ])
            link(nc.vector.tensor_copy(newshift[:, :, 1:1 + NB], tail(pb)[:, 0:N_SH, :, NT - 1]))
            dve.nop().then_inc(shifted, 1)
            for a, n in ((LW0, 2), (K0, 4), (R0, 4), (V0, 4)):
                p, d = pb[:, a:a + n], diff[:, 0:n]
                nc.vector.tensor_tensor(d[:, :, 1:SEQ], p[:, :, 0:SEQ - 1], p[:, :, 1:SEQ], ALU.subtract)
                nc.vector.tensor_scalar(d[:, :, 0:1], p[:, :, 0:1], -1.0, None, ALU.mult)
                ps_, ds_ = tail(p), tail(d)
                for i in range(n):
                    nc.vector.tensor_tensor(ds_[:, i, :, 1:NT], ps_[:, i, :, 0:NT - 1], ps_[:, i, :, 1:NT], ALU.subtract)
                link(nc.vector.tensor_tensor(ds_[:, :, :, 0], shift[:, a:a + n], ps_[:, :, :, 0], ALU.subtract))
                for i in range(n):
                    last = nc.vector.scalar_tensor_tensor(p[:, i], d[:, i], par("mu", a + i), p[:, i], ALU.mult, ALU.add)
                link(last)
                dve.nop().then_inc(mixed, 1)
            for ft in range(FT):
                last = nc.vector.tensor_scalar(kk[:, ft], pb[:, K0 + ft], par("kk", ft), -1.0, ALU.mult, ALU.mult)
            link(last)
            dve.nop().then_inc(kraw, 1)
            z = pb[0:NH, FF0]
            link(nc.vector.tensor_scalar(f_z[:], z, par("bf", 0, NH), None, ALU.add))
            nc.vector.tensor_scalar(f_m[:], f_z[:], 0.0, None, ALU.min)
            nc.vector.scalar_tensor_tensor(f_a[:], f_z[:], -1.0, f_z[:], ALU.mult, ALU.max).then_inc(f_abs, 1)
            for ft in range(FT):
                dve.wait_ge(lora_out, ft + 1)
                nc.vector.tensor_tensor_scan(cum[:, ft], K("reset"), lw[:, ft], 0.0, ALU.mult, ALU.add)\
                    .then_inc(scanned, 1)
            dve.wait_ge(scanned, FT)
            dve.wait_ge(f_abs, 1)
            m, e = keep["mid"], keep["mexp"]
            nc.vector.tensor_copy(m[:], cum[:, :, CH // 2 - 1:SEQ:CH])
            link(nc.vector.tensor_copy(e[:, 1], cum[:, :, CH - 1:SEQ:CH]))
            link(nc.vector.tensor_tensor(e[:, 1], e[:, 1], m[:], ALU.subtract))
            dve.nop().then_inc(mids, 1)
            dve.wait_ge(f_log, 1)
            link(nc.vector.tensor_tensor(f_z[:], f_m[:], f_e[:], ALU.subtract))
            dve.nop().then_inc(f_done, 1)
            link(nc.vector.tensor_tensor_scan(cn, K("fresh", NH), f_z[:], 0.0, ALU.mult, ALU.add))
            dve.nop().then_inc(f_done, 1)
            dve.wait_ge(sq_used, 12)
            link(nc.vector.tensor_scalar(halves(st[:]), ps[0:24, 0, :, 0:HALF], par("sc", 0, 24), par("ad", 0, 24),
                                         ALU.mult, ALU.add))
            nc.vector.tensor_scalar(st[:], st[:], 1e-24, None, ALU.max).then_inc(biased, 1)
            link(nc.vector.tensor_scalar(gq[:], par("qn", 0), float(DH) ** -0.5, None, ALU.mult))
            dve.wait_ge(rooted, 1)
            nc.vector.reciprocal(st[:], st[:]).then_inc(inverted, 1)
            for i in range(12):
                dve.wait_ge(spread, i + 1)
                src = ps[:, i % 4, :, 0:HALF]
                if i < 8:
                    t = pb[:, FQ0 + i]
                    g = gq[:] if i < 4 else par("kn", 0)
                    nc.vector.scalar_tensor_tensor(halves(t), halves(t), g, src, ALU.mult, ALU.mult).then_inc(normed, 1)
                else:
                    t = kk[:, i - 8]
                    nc.vector.tensor_tensor(halves(t), halves(t), src, ALU.mult).then_inc(normed, 1)
            for ft in range(FT):
                dve.wait_ge(lora_out, FT + ft + 1)
                k, r = pb[:, K0 + ft], pb[:, R0 + ft]
                link(nc.vector.tensor_scalar(tmp[:, 0], kka[:, ft], 1.0, par("ka", ft), ALU.subtract, ALU.mult))
                link(nc.vector.scalar_tensor_tensor(k, tmp[:, 0], 1.0, k, ALU.add, ALU.mult))
                if ft:
                    dve.wait_ge(rksum, ft)
                nc.vector.scalar_tensor_tensor(tmp[:, 1], r, par("rk", ft), k, ALU.mult, ALU.mult).then_inc(rkprod, 1)
                dve.wait_ge(normed, 9 + ft)
                link(nc.vector.scalar_tensor_tensor(kka[:, ft], kk[:, ft], -1.0, kka[:, ft], ALU.mult, ALU.mult))
            nc.vector.tensor_tensor_scan(past[0:64, 0:PAST], C["ones"][0:64, 0:1].broadcast_to([64, PAST]), past[0:64, 0:PAST],
                                         0.0, ALU.mult, ALU.add).then_inc(summed, 1)
            dve.wait_ge(rksum, FT)
            nc.vector.tensor_copy(halves(rk8), ps[0:NH, 0, :, 0:HALF])
            dve.wait_ge(tp, 1)
            nc.vector.tensor_copy(keep["vn"][:], ps[0:64, 1, 0, :])
            new = ps[:, None, 2, 0, 0:64].broadcast_to([P, NCH, 64])
            nc.vector.tensor_tensor(keep["newb"][:], K("mnew").rearrange("p (c n) -> p c n", c=NCH), new, ALU.add)

        @block.scalar
        def _(act):
            act.wait_ge(loaded, 48)
            act.wait_ge(mixed, 1)
            nc.scalar.activation(pb[0:64, LW0], pb[0:64, LW0], ACT.Tanh).then_inc(lora_act, 1)
            nc.scalar.activation(pb[:, LG0], pb[:, LG0], ACT.Sigmoid)
            for i in range(2 * FT):
                act.wait_ge(lora_mm, i + 1)
                out = lw[:, i] if i < FT else kka[:, i - FT]
                nc.scalar.activation(halves(out), ps[:, i % 4, :, 0:HALF], ACT.Sigmoid,
                                     bias=par("w0" if i < FT else "a0", i % FT)).then_inc(lora_out, 1)
            act.wait_ge(kraw, 1)
            for i in range(12):
                if i >= 2:
                    act.wait_ge(sq_used, i - 1)
                src = pb[:, FQ0 + i] if i < 8 else kk[:, i - 8]
                nc.scalar.activation(sq[:, i % 2], src, ACT.Square).then_inc(squares, 1)
            act.wait_ge(f_abs, 1)
            nc.scalar.activation(f_e[:], f_a[:], ACT.Exp, scale=-1.0).then_inc(f_exp, 1)
            act.wait_ge(f_exp, 1)
            nc.scalar.activation(f_e[:], f_e[:], ACT.Ln, bias=1.0).then_inc(f_log, 1)
            act.wait_ge(biased, 1)
            nc.scalar.activation(st[:], st[:], ACT.Sqrt).then_inc(rooted, 1)
            act.wait_ge(mids, 1)
            e = keep["mexp"]
            nc.scalar.activation(e[:, 0], keep["mid"][:], ACT.Exp, scale=-KAPPA)
            nc.scalar.activation(e[:, 2], keep["mid"][:], ACT.Exp, scale=KAPPA)
            nc.scalar.activation(e[:, 1], e[:, 1], ACT.Exp, scale=-KAPPA)

        @block.tensor
        def _(pe):
            pe.wait_ge(loaded, 48)
            pe.wait_ge(lora_act, 1)
            for i in range(2 * FT):
                if i >= 4:
                    pe.wait_ge(lora_out, i - 3)
                r = slice(0, 64) if i < FT else slice(64, P)
                for half in range(2):
                    mm = nc.tensor.matmul(ps[:, i % 4, half, 0:HALF], lora[r, (i % FT) * P:(i % FT) * P + P],
                                          pb[r, LW0, half * HALF:half * HALF + HALF], start=True, stop=True)
                mm.then_inc(lora_mm, 1)
            pe.wait_ge(lora_out, 2 * FT)
            sel = K("sel24").rearrange("p (i m) -> p i m", i=12)
            for i in range(12):
                pe.wait_ge(squares, i + 1)
                for half in range(2):
                    mm = nc.tensor.matmul(ps[0:24, 0, half, 0:HALF], sel[:, i], sq[:, i % 2, half * HALF:half * HALF + HALF],
                                          start=i == 0, stop=i == 11)
                mm.then_inc(sq_used, 1)
            pe.wait_ge(inverted, 1)
            selt = K("selt", 24).rearrange("p (i m) -> p i m", i=12)
            for i in range(12):
                if i >= 4:
                    pe.wait_ge(normed, i - 3)
                for half in range(2):
                    mm = nc.tensor.matmul(ps[:, i % 4, half, 0:HALF], selt[:, i], st[:, half * HALF:half * HALF + HALF],
                                          start=True, stop=True)
                mm.then_inc(spread, 1)
            pe.wait_ge(normed, 12)
            for ft in range(FT):
                pe.wait_ge(rkprod, ft + 1)
                for half in range(2):
                    mm = nc.tensor.matmul(ps[0:NH, 0, half, 0:HALF], sel[:, 8 + ft, 16:24],
                                          tmp[:, 1, half * HALF:half * HALF + HALF], start=ft == 0, stop=ft == FT - 1)
                mm.then_inc(rksum, 1)
            pe.wait_ge(f_done, 2)
            for i in range(FT):
                nc.tensor.transpose(ps[0:64, 1, 0, i * P:(i + 1) * P], pb[:, FV0 + i, SEQ:TOK], C["ident"])
            nc.tensor.matmul(ps[:, 2, 0, 0:64], K("nsel", NH), cn[:, SEQ:TOK], start=True, stop=True).then_inc(tp, 1)


class Rwkv:

    TR, BANKS = 3, 2

    def __init__(self, ctx, sems, nc, tag, T, levels, pb, C, keep, buf, sample):
        self.nc, self.T, self.levels, self.pb, self.C, self.keep, self.sample = nc, T, levels, pb, C, keep, sample
        self.bank, self.cc, self.e1, self.e3, self.ar = buf["bank"], buf["cc"], buf["e1"], buf["e3"], buf["ar"]
        self.bf, self.kf, self.vf, self.bt, self.kt, self.vt = (buf[n] for n in ("bf", "kf", "vf", "bt", "kt", "vt"))
        self.ntg, self.nkg, self.x, self.xt, self.tt = (buf[n] for n in ("ntg", "nkg", "x", "xt", "tt"))
        self.rs, self.us = buf["rs"], buf["us"]
        if sample:
            self.s0, self.sa, self.ux, self.vx = buf["s0"], buf["sa"], buf["ux"], buf["vx"]
            self.s_loaded, self.x_part, self.y_taken, self.s_added = (
                buf[n] for n in ("s_loaded", "x_part", "y_taken", "s_added"))
        else:
            self.s, self.s_mid = buf["s"], buf["s_mid"]
        sem = lambda n: sems(n + tag)
        self.gram_heads = 512 // (2 * T)
        self.rounds = 3 + 2 * (NH // self.gram_heads)
        self.centred, self.exped, self.shifted, self.ready = sem("rw_centred"), sem("rw_exped"), sem("rw_shifted"), sem("rw_ready")
        self.v_copied, self.mm, self.ev = sem("rw_v_copied"), sem("rw_mm"), sem("rw_evacuated")
        self.t_mm, self.t_ev = [sem("rw_t_mm0"), sem("rw_t_mm1")], [sem("rw_t_ev0"), sem("rw_t_ev1")]
        self.xt_mm, self.xt_ev = [sem("rw_xt_mm0"), sem("rw_xt_mm1")], [sem("rw_xt_ev0"), sem("rw_xt_ev1")]
        self.x_mm, self.x_ev = [sem("rw_x_mm0"), sem("rw_x_mm1")], [sem("rw_x_ev0"), sem("rw_x_ev1")]
        self.sm, self.r_mm, self.r_ev, self.u_mm, self.u_ev = sem("rw_sm"), sem("rw_r_mm"), sem("rw_r_ev"), sem("rw_u_mm"), sem("rw_u_ev")
        self.y_mm, self.d_mm, self.d_part, self.done = sem("rw_y_mm"), sem("rw_d_mm"), sem("rw_d_part"), sem("rw_done")

    def seed(self, dve):
        dve.nop().then_inc(self.done, 1)

    def cols(self, c):
        return slice(SEQ, TOK) if self.sample else bass.ds(c * CH, CH)

    def heads(self, g):
        first = g % (NH // self.gram_heads)
        return [first % 2 + 2 * (first // 2 * self.gram_heads + j) for j in range(self.gram_heads)]

    def act_exps(self, act, c):
        T = self.T
        act.wait_ge(self.centred, c + 1)
        self.nc.scalar.activation(self.e1[:, :, 0:T], self.cc[:, :, 0:T], ACT.Exp, scale=-KAPPA).then_inc(self.exped, 1)
        self.nc.scalar.activation(self.e3[:, :, 0:T], self.cc[:, :, 0:T], ACT.Exp, scale=KAPPA).then_inc(self.exped, 1)

    def pool_v(self, pool, c):
        pool.wait_ge(self.done, c + 1)
        self.nc.gpsimd.tensor_copy(self.vf[:, :, 0:self.T], self.pb[:, V0:V0 + FT, self.cols(c)]).then_inc(self.v_copied, 1)

    def dve_operands(self, dve, c):
        nc, T, t, pb, keep = self.nc, self.T, self.cols(c), self.pb, self.keep
        if self.sample:
            nc.vector.tensor_copy(self.cc[:, :, 0:T], keep["cum"][:, :, t]).then_inc(self.centred, 1)
        else:
            mid = keep["mid"][:, :, bass.ds(c, 1)].broadcast_to([P, FT, T])
            nc.vector.tensor_tensor(self.cc[:, :, 0:T], keep["cum"][:, :, t], mid, ALU.subtract).then_inc(self.centred, 1)
        dve.wait_ge(self.exped, 2 * c + 1)
        nc.vector.tensor_tensor(self.ar[:, :, 1, 0:T], pb[:, R0:R0 + FT, t], self.e1[:, :, 0:T], ALU.mult)
        if self.sample:
            g = lambda a: a.rearrange("p f (b t) -> p f b t", t=NT)
            for f in range(FT):
                a, k, e = (g(x)[:, f] for x in (self.ar[:, :, 0, 0:T], keep["kk"][:, :, t], self.e1[:, :, 0:T]))
                nc.vector.tensor_tensor(a[:, :, 1:NT], k[:, :, 1:NT], e[:, :, 0:NT - 1], ALU.mult)
                nc.vector.tensor_copy(a[:, :, 0:1], k[:, :, 0:1])
        else:
            first = keep["mexp"][:, 2, :, bass.ds(c, 1)]
            nc.vector.tensor_tensor(self.ar[:, :, 0, 1:T], keep["kk"][:, :, bass.ds(c * CH + 1, CH - 1)],
                                    self.e1[:, :, 0:T - 1], ALU.mult)
            nc.vector.tensor_tensor(self.ar[:, :, 0, 0:1], keep["kk"][:, :, bass.ds(c * CH, 1)], first, ALU.mult)
        dve.wait_ge(self.exped, 2 * c + 2)
        nc.vector.tensor_tensor(self.bf[:, :, 0:T], keep["kka"][:, :, t], self.e3[:, :, 0:T], ALU.mult)
        nc.vector.tensor_tensor(self.kf[:, :, 0:T], pb[:, K0:K0 + FT, t], self.e3[:, :, 0:T], ALU.mult).then_inc(self.ready, 1)

    def pe_gram(self, pe, c, n):
        nc, T, gh = self.nc, self.T, self.gram_heads
        if n == 0:
            pe.wait_ge(self.ready, c + 1)
            pe.wait_ge(self.done, c + 1)
        if n == 2:
            pe.wait_ge(self.v_copied, c + 1)
        if n >= self.BANKS:
            pe.wait_ge(self.ev, c * self.rounds + n - self.BANKS + 1)
        bank = self.bank[n % 2]
        if n < self.TR:
            src = (self.bf, self.kf, self.vf)[n]
            for f in range(FT):
                mm = nc.tensor.transpose(bank[0:T, f * P:f * P + P], src[:, f, 0:T], self.C["ident"])
        else:
            g = n - self.TR
            src = self.bf if g < NH // gh else self.kf
            for j in range(gh):
                h = self.heads(g)[j]
                po, f = h % 2 * DH, h // 2
                out = bank[0:T, j * 2 * T:j * 2 * T + 2 * T]
                mm = nc.tensor.matmul(out.rearrange("p (a t) -> p a t", a=2), src[po:po + DH, f, 0:T],
                                      self.ar[po:po + DH, f, :, 0:T], start=True, stop=True)
        mm.then_inc(self.mm, 1)

    def dve_gram(self, dve, c, n):
        nc, T, gh = self.nc, self.T, self.gram_heads
        mask = self.C["lows"][0:T, 0:2 * T] if self.sample else self.C["low"]
        mask = mask[:, None, :].broadcast_to([T, gh, 2 * T])
        dve.wait_ge(self.mm, c * self.rounds + n + 1)
        bank = self.bank[n % 2]
        if n < self.TR:
            nc.vector.tensor_copy((self.bt, self.kt, self.vt)[n][0:T], bank[0:T, 0:512]).then_inc(self.ev, 1)
        else:
            g = n - self.TR
            dst, h = (self.ntg if g < NH // gh else self.nkg), self.heads(g)
            nc.vector.tensor_tensor(dst[0:T, h[0]:h[-1] + 1:2, 0:2 * T], bank[0:T].rearrange("p (h m) -> p h m", h=gh),
                                    mask, ALU.mult).then_inc(self.ev, 1)

    def view(self, buf, bt):
        return buf[0:self.T, 4 * bt:4 * bt + 4, 0:self.T]

    def pe_level(self, pe, c, level, bt):
        nc, T, L, ident = self.nc, self.T, self.levels, self.C["ident"]
        out = self.bank[bt].rearrange("p (h m) -> p h m", h=4)
        if level == 0 and bt == 0:
            pe.wait_ge(self.ev, (c + 1) * self.rounds)
        if level:
            pe.wait_ge(self.x_ev[bt], c * (L - 1) + level)
        for j in range(4):
            h = 4 * bt + j
            if level == 0:
                mm = nc.tensor.transpose(out[0:T, j, 0:T], self.ntg[0:T, h, 0:T], ident[0:T, 0:T])
            else:
                mm = nc.tensor.matmul(out[0:T, j, 0:T], self.ntg[0:T, h, 0:T], self.x[0:T, h, 0:T], start=True, stop=True)
        mm.then_inc(self.t_mm[bt], 1)

    def pe_level_xt(self, pe, c, level, bt):
        nc, T, L, ident = self.nc, self.T, self.levels, self.C["ident"]
        out = self.bank[bt].rearrange("p (h m) -> p h m", h=4)
        pe.wait_ge(self.t_ev[bt], c * L + level + 1)
        for j in range(4):
            h = 4 * bt + j
            if level == 0:
                mm = nc.tensor.transpose(out[0:T, j, 0:T], self.tt[0:T, h, 0:T], ident[0:T, 0:T])
            else:
                mm = nc.tensor.matmul(out[0:T, j, 0:T], self.tt[0:T, h, 0:T], self.xt[0:T, h, 0:T], start=True, stop=True)
        mm.then_inc(self.xt_mm[bt], 1)

    def pe_level_x(self, pe, c, level, bt):
        nc, T, L = self.nc, self.T, self.levels
        out = self.bank[bt].rearrange("p (h m) -> p h m", h=4)
        pe.wait_ge(self.xt_ev[bt], c * L + level + 1)
        for j in range(4):
            mm = nc.tensor.transpose(out[0:T, j, 0:T], self.xt[0:T, 4 * bt + j, 0:T], self.C["ident"][0:T, 0:T])
        mm.then_inc(self.x_mm[bt], 1)

    def dve_t(self, dve, c, level, bt):
        T = self.T
        mask = self.C["lev"][0:T, level * P:level * P + T][:, None, :].broadcast_to([T, 4, T])
        src = self.bank[bt].rearrange("p (h m) -> p h m", h=4)[0:T, :, 0:T]
        dve.wait_ge(self.t_mm[bt], c * self.levels + level + 1)
        self.nc.vector.tensor_tensor(self.view(self.tt, bt), src, mask, ALU.mult).then_inc(self.t_ev[bt], 1)

    def dve_xt(self, dve, c, level, bt):
        T, L = self.T, self.levels
        src = self.bank[bt].rearrange("p (h m) -> p h m", h=4)[0:T, :, 0:T]
        dve.wait_ge(self.xt_mm[bt], c * L + level + 1)
        if level:
            dve.wait_ge(self.xt_ev[bt], c * L + level)
            add = self.view(self.xt, bt)
        else:
            add = self.C["ident"][0:T, None, 0:T].broadcast_to([T, 4, T])
        self.nc.vector.tensor_tensor(self.view(self.xt, bt), src, add, ALU.add).then_inc(self.xt_ev[bt], 1)

    def act_x(self, act, c, level, bt):
        src = self.bank[bt].rearrange("p (h m) -> p h m", h=4)[0:self.T, :, 0:self.T]
        act.wait_ge(self.x_mm[bt], c * (self.levels - 1) + level + 1)
        self.nc.scalar.activation(self.view(self.x, bt), src, ACT.Copy).then_inc(self.x_ev[bt], 1)


    def pe_r(self, pe, c):
        nc, L = self.nc, self.levels
        for bt in range(2):
            pe.wait_ge(self.xt_ev[bt], (c + 1) * L)
        pe.wait_ge(self.sm, c + 1)
        for h in range(NH):
            po, f, hs = h % 2 * DH, h // 2, slice(h * DH, h * DH + DH)
            out = self.bank[h % 2][:, f * DH:f * DH + DH]
            nc.tensor.matmul(out, self.ar[po:po + DH, f, 0], self.s_mid[po:po + DH, f], start=True, stop=False)
            mm = nc.tensor.matmul(out, self.nkg[:, h, 0:CH], self.vt[:, hs], start=False, stop=True)
        mm.then_inc(self.r_mm, 1)

    def pe_u(self, pe, c):
        nc, b0 = self.nc, self.bank[0]
        pe.wait_ge(self.r_ev, 2 * c + 2)
        for h in range(NH):
            hs = slice(h * DH, h * DH + DH)
            mm = nc.tensor.matmul(b0[:, hs], self.xt[:, h], self.rs[:, hs], start=True, stop=True)
        mm.then_inc(self.u_mm, 1)

    def pe_y(self, pe, c):
        nc, b1 = self.nc, self.bank[1]
        pe.wait_ge(self.u_ev, c + 1)
        for h in range(NH):
            po, f, hs = h % 2 * DH, h // 2, slice(h * DH, h * DH + DH)
            out = b1[po:po + DH, f * CH:f * CH + CH]
            nc.tensor.matmul(out, self.us[:, hs], self.ntg[:, h, CH:2 * CH], start=True, stop=False)
            nc.tensor.matmul(out, self.vt[:, hs], self.nkg[:, h, CH:2 * CH], start=False, stop=False)
            mm = nc.tensor.matmul(out, self.s_mid[po:po + DH, f], self.ar[po:po + DH, f, 1], start=False, stop=True)
        mm.then_inc(self.y_mm, 1)

    def pe_d(self, pe, c):
        nc, b0 = self.nc, self.bank[0]
        for h in range(NH):
            po, f, hs = h % 2 * DH, h // 2, slice(h * DH, h * DH + DH)
            out = b0[po:po + DH, f * DH:f * DH + DH]
            nc.tensor.matmul(out, self.bt[:, hs], self.us[:, hs], start=True, stop=False)
            mm = nc.tensor.matmul(out, self.kt[:, hs], self.vt[:, hs], start=False, stop=True)
        mm.then_inc(self.d_mm, 1)

    def act_r(self, act, c):
        act.wait_ge(self.r_mm, c + 1)
        for u in range(2):
            dst = self.rs.rearrange("p (f u v) -> p f u v", f=FT, u=2)[:, :, u]
            src = self.bank[u][:, 0:FT * DH].rearrange("p (f v) -> p f v", f=FT)
            self.nc.scalar.activation(dst, src, ACT.Copy).then_inc(self.r_ev, 1)

    def dve_state_in(self, dve, c):
        e = self.keep["mexp"][:, 0, :, bass.ds(c, 1)].broadcast_to([P, FT, DH])
        dve.wait_ge(self.done, c + 1)
        self.nc.vector.tensor_tensor(self.s_mid[:], self.s[:], e, ALU.mult).then_inc(self.sm, 1)

    def dve_u(self, dve, c):
        dve.wait_ge(self.u_mm, c + 1)
        self.nc.vector.tensor_copy(self.us[:], self.bank[0]).then_inc(self.u_ev, 1)

    def dve_yd(self, dve, c):
        nc = self.nc
        dve.wait_ge(self.y_mm, c + 1)
        nc.vector.tensor_scalar(self.pb[:, R0:R0 + FT, self.cols(c)], self.bank[1].rearrange("p (f t) -> p f t", f=FT),
                                1.0, None, ALU.mult)
        dve.wait_ge(self.d_mm, c + 1)
        src = self.bank[0][:, 0:FT * DH].rearrange("p (f v) -> p f v", f=FT)
        e = self.keep["mexp"][:, 1, :, bass.ds(c, 1)].broadcast_to([P, FT, DH])
        nc.vector.tensor_tensor(self.s[:], src, self.s_mid[:], ALU.add).then_inc(self.d_part, 1)
        dve.wait_ge(self.d_part, c + 1)
        nc.vector.tensor_tensor(self.s[:], self.s[:], e, ALU.mult).then_inc(self.done, 1)


    def pe_sample(self, pe):
        nc, T, L = self.nc, self.T, self.levels
        b0, b1 = self.bank
        for bt in range(2):
            pe.wait_ge(self.xt_ev[bt], L)
        pe.wait_ge(self.s_loaded, 16)
        view = b0.rearrange("p (f a t) -> p f a t", f=FT, a=2)
        for f in range(FT):
            for b in range(NB):
                for po in (0, DH):
                    mm = nc.tensor.matmul(view[po:po + DH, f, :, NT * b:NT * b + NT], self.s0[po:po + DH, f, b],
                                          self.ar[po:po + DH, f, :, NT * b:NT * b + NT], start=True, stop=True)
        mm.then_inc(self.sm, 1)
        pe.wait_ge(self.d_part, 1)
        for f in range(FT):
            for u in range(2):
                h = 2 * f + u
                hs = slice(h * DH, h * DH + DH)
                nc.tensor.matmul(b1[0:T, hs], self.sa[:, f, 0], self.C["ident"][:, u * DH:u * DH + DH], start=True, stop=False)
                mm = nc.tensor.matmul(b1[0:T, hs], self.nkg[0:T, h, 0:T], self.vt[0:T, hs], start=False, stop=True)
        mm.then_inc(self.r_mm, 1)
        pe.wait_ge(self.r_ev, 1)
        for h in range(NH):
            hs = slice(h * DH, h * DH + DH)
            mm = nc.tensor.matmul(b0[0:T, hs], self.xt[0:T, h, 0:T], self.rs[0:T, hs], start=True, stop=True)
        mm.then_inc(self.u_mm, 1)
        pe.wait_ge(self.u_ev, 1)
        for h in range(NH):
            po, f, hs = h % 2 * DH, h // 2, slice(h * DH, h * DH + DH)
            out = b1[po:po + DH, f * T:f * T + T]
            nc.tensor.matmul(out, self.us[0:T, hs], self.ntg[0:T, h, T:2 * T], start=True, stop=False)
            mm = nc.tensor.matmul(out, self.vt[0:T, hs], self.nkg[0:T, h, T:2 * T], start=False, stop=True)
        mm.then_inc(self.y_mm, 1)
        for f in range(FT):
            pe.wait_ge(self.x_part, f + 1)
            if f >= 2:
                pe.wait_ge(self.done, f)
            if f == 1:
                pe.wait_ge(self.y_taken, 1)
            for po in (0, DH):
                h = 2 * f + po // DH
                hs = slice(h * DH, h * DH + DH)
                ux, vx = self.ux[0:T, f % 2, po // DH], self.vx[0:T, f % 2, po // DH]
                nc.tensor.matmul(self.bank[f % 2][po:po + DH], self.bt[0:T, hs], ux, start=True, stop=False)
                mm = nc.tensor.matmul(self.bank[f % 2][po:po + DH], self.kt[0:T, hs], vx, start=False, stop=True)
            mm.then_inc(self.d_mm, 1)

    def act_sample(self, act):
        act.wait_ge(self.r_mm, 1)
        self.nc.scalar.activation(self.rs[0:self.T], self.bank[1][0:self.T], ACT.Copy).then_inc(self.r_ev, 1)

    def dve_sample(self, dve):
        nc, T = self.nc, self.T
        b0, b1 = self.bank
        dve.wait_ge(self.sm, 1)
        nc.vector.tensor_copy(self.sa[:], b0.rearrange("p (f a t) -> p f a t", f=FT, a=2)).then_inc(self.d_part, 1)
        dve.wait_ge(self.u_mm, 1)
        nc.vector.tensor_copy(self.us[0:T], b0[0:T]).then_inc(self.u_ev, 1)
        dve.wait_ge(self.u_ev, 1)
        dve.wait_ge(self.y_mm, 1)
        nc.vector.tensor_tensor(self.pb[:, R0:R0 + FT, SEQ:TOK], b1[:, 0:FT * T].rearrange("p (f t) -> p f t", f=FT),
                                self.sa[:, :, 1], ALU.add).then_inc(self.y_taken, 1)
        bm = self.C["bmask"][0:T, :, None].broadcast_to([T, NB, DH])
        for f in range(FT):
            if f >= 2:
                dve.wait_ge(self.d_mm, f - 1)
            for u in range(2):
                h = 2 * f + u
                for src, dst in ((self.us, self.ux), (self.vt, self.vx)):
                    v = src[0:T, h * DH:h * DH + DH][:, None, :].broadcast_to([T, NB, DH])
                    last = nc.vector.tensor_tensor(dst[0:T, f % 2, u].rearrange("p (b v) -> p b v", b=NB), v, bm, ALU.mult)
            last.then_inc(self.x_part, 1)
            if f >= 1:
                self.dve_state_out(dve, f - 1)
        self.dve_state_out(dve, FT - 1)

    def dve_state_out(self, dve, f):
        nc = self.nc
        dve.wait_ge(self.d_mm, f + 1)
        src = self.bank[f % 2].rearrange("p (b v) -> p b v", b=NB)
        nc.vector.tensor_tensor(self.s0[:, f], src, self.s0[:, f], ALU.add).then_inc(self.s_added, 1)
        dve.wait_ge(self.s_added, f + 1)
        e = self.e1[:, f, NT - 1:NB * NT:NT][:, :, None].broadcast_to([P, NB, DH])
        nc.vector.tensor_tensor(self.s0[:, f], self.s0[:, f], e, ALU.mult).then_inc(self.done, 1)


class FoxPrompt:

    UNITS = [(u, i) for i in range(SEQ // P) for u in range(2)]

    def __init__(self, ctx, sems, nc, pb, C, keep, banks):
        self.nc, self.pb, self.C, self.keep = nc, pb, C, keep
        sb = lambda n, s, d=F32: ctx.enter_context(nc.sbuf_tensor(n, s, d))
        sem = sems
        self.b_s, self.b_t, self.b_o = banks
        self.q, self.k, self.v = sb("fp_q", [P, SEQ], F32), sb("fp_k", [P, SEQ]), sb("fp_v", [P, SEQ])
        self.sel, self.bias, self.vt = sb("fp_sel", [NH, 2, P]), sb("fp_bias", [P, 2, SEQ]), sb("fp_vt", [P, 4, P])
        self.s, self.p, self.pt = sb("fp_s", [P, 2, SEQ]), sb("fp_p", [P, 2, SEQ]), sb("fp_pt", [P, 2, 4, P])
        self.nm, self.rsum = sb("fp_nm", [P, 8]), sb("fp_rsum", [P, 8])
        self.copied, self.masked, self.bias_mm, self.bias_ev = sem("fp_copied"), sem("fp_masked"), sem("fp_bias_mm"), sem("fp_bias_ev")
        self.causal, self.vt_mm, self.vt_ev = sem("fp_causal"), sem("fp_vt_mm"), sem("fp_vt_ev")
        self.s_mm, self.s_ev, self.maxed, self.exped = sem("fp_s_mm"), sem("fp_s_ev"), sem("fp_maxed"), sem("fp_exped")
        self.inverted, self.p_done, self.t_mm, self.t_ev, self.o_mm, self.o_ev = (
            sem("fp_inverted"), sem("fp_p_done"), sem("fp_t_mm"), sem("fp_t_ev"), sem("fp_o_mm"), sem("fp_o_ev"))

    def seed(self, dve):
        dve.nop().then_inc(self.s_ev, 1)
        dve.nop().then_inc(self.o_ev, 1)
        dve.nop().then_inc(self.o_mm, 1)

    def pool(self, pool, c):
        pool.wait_ge(self.o_mm, 8 * c + 1)
        for dst, a in ((self.k, FK0), (self.q, FQ0), (self.v, FV0)):
            src = self.pb[:, a:a + FT][:, bass.ds(c, 1), 0:SEQ].rearrange("p a n -> p (a n)")
            self.nc.gpsimd.tensor_copy(dst[:], src).then_inc(self.copied, 1)

    def pe_in(self, pe, c):
        nc = self.nc
        pe.wait_ge(self.copied, 3 * c + 3)
        for u in range(2):
            pe.wait_ge(self.masked, 2 * c + u + 1)
            if u == 0:
                pe.wait_ge(self.s_ev, 8 * c + 1)
            else:
                pe.wait_ge(self.bias_ev, 2 * c + 1)
            nc.tensor.matmul(self.b_s[:], self.sel[:, u], self.pb[0:NH, FF0, 0:SEQ], start=True, stop=True).then_inc(self.bias_mm, 1)
        for j in range(4):
            mm = nc.tensor.transpose(self.b_t[:, j * P:j * P + P], self.v[:, j * P:j * P + P], self.C["ident"])
        mm.then_inc(self.vt_mm, 1)

    def pe_turn(self, pe, c, n):
        nc, (u, i) = self.nc, self.UNITS[n]
        pe.wait_ge(self.p_done, 8 * c + n + 1)
        if n:
            pe.wait_ge(self.t_ev, 8 * c + n)
        for j in range(i + 1):
            mm = nc.tensor.transpose(self.b_t[:, j * P:j * P + P], self.p[:, n % 2, j * P:j * P + P], self.C["ident"])
        mm.then_inc(self.t_mm, 1)

    def pe_values(self, pe, c, n):
        nc, (u, i) = self.nc, self.UNITS[n]
        pe.wait_ge(self.t_ev, 8 * c + n + 1)
        if n == 0:
            pe.wait_ge(self.o_ev, c + 1)
        po = u * DH
        for j in range(i + 1):
            mm = nc.tensor.matmul(self.b_o[po:po + DH, i * P:i * P + P], self.vt[:, j, po:po + DH],
                                  self.pt[:, n % 2, j], start=j == 0, stop=j == i)
        mm.then_inc(self.o_mm, 1)

    def pe_scores(self, pe, c, n):
        u, i = self.UNITS[n]
        if n == 0:
            pe.wait_ge(self.bias_ev, 2 * c + 2)
            pe.wait_ge(self.vt_ev, c + 1)
        if n:
            pe.wait_ge(self.s_ev, 8 * c + n + 1)
        r = slice(u * DH, u * DH + DH)
        self.nc.tensor.matmul(self.b_s[:, 0:i * P + P], self.q[r, i * P:i * P + P], self.k[r, 0:i * P + P],
                              start=True, stop=True).then_inc(self.s_mm, 1)

    def dve_in(self, dve, c):
        nc = self.nc
        for u in range(2):
            nc.vector.tensor_scalar(self.sel[:, u], self.C["minus"][0:NH], self.C["ident"][0:NH, bass.ds(2 * c + u, 1)],
                                    None, ALU.mult).then_inc(self.masked, 1)

    def dve_normalise(self, dve, c, n):
        nc, (u, i) = self.nc, self.UNITS[n]
        w = i * P + P
        dve.wait_ge(self.exped, 8 * c + n + 1)
        nc.vector.reciprocal(self.rsum[:, n:n + 1], self.rsum[:, n:n + 1]).then_inc(self.inverted, 1)
        dve.wait_ge(self.inverted, 8 * c + n + 1)
        nc.vector.tensor_scalar(self.p[:, n % 2, 0:w], self.p[:, n % 2, 0:w], self.rsum[:, n:n + 1], None,
                                ALU.mult).then_inc(self.p_done, 1)

    def dve_scores(self, dve, c, n):
        nc = self.nc
        u, i = self.UNITS[n]
        a, w = i * P, i * P + P
        dve.wait_ge(self.s_mm, 8 * c + n + 1)
        nc.vector.tensor_tensor(self.s[:, n % 2, 0:w], self.b_s[:, 0:w], self.bias[:, u, 0:w], ALU.add).then_inc(self.s_ev, 1)
        dve.wait_ge(self.s_ev, 8 * c + n + 2)
        nc.vector.tensor_tensor(self.s[:, n % 2, a:w], self.s[:, n % 2, a:w], self.C["causal"], ALU.add).then_inc(self.causal, 1)
        dve.wait_ge(self.causal, 8 * c + n + 1)
        nc.vector.tensor_reduce(self.nm[:, n:n + 1], self.s[:, n % 2, 0:w], AX.X, ALU.max, negate=True).then_inc(self.maxed, 1)

    def act_in(self, act, c):
        nc = self.nc
        for u in range(2):
            act.wait_ge(self.bias_mm, 2 * c + u + 1)
            nc.scalar.activation(self.bias[:, u], self.b_s[:], ACT.Copy).then_inc(self.bias_ev, 1)
        act.wait_ge(self.vt_mm, c + 1)
        nc.scalar.activation(self.vt[:].rearrange("p j n -> p (j n)"), self.b_t[:], ACT.Copy).then_inc(self.vt_ev, 1)

    def act_exp(self, act, c, n):
        nc, (u, i) = self.nc, self.UNITS[n]
        w = i * P + P
        act.wait_ge(self.maxed, 8 * c + n + 1)
        if n >= 2:
            act.wait_ge(self.t_mm, 8 * c + n - 1)
        nc.scalar.activation(self.p[:, n % 2, 0:w], self.s[:, n % 2, 0:w], ACT.Exp, bias=self.nm[:, n:n + 1],
                             accum_out=self.rsum[:, n:n + 1]).then_inc(self.exped, 1)

    def act_out(self, act, c):
        nc = self.nc
        act.wait_ge(self.o_mm, 8 * c + 9)
        dst = self.pb[:, FQ0:FQ0 + FT][:, bass.ds(c, 1), 0:SEQ]
        nc.scalar.activation(dst, self.b_o[:][:, None, :], ACT.Copy).then_inc(self.o_ev, 1)

    def act_turned(self, act, c, n):
        u, i = self.UNITS[n]
        act.wait_ge(self.t_mm, 8 * c + n + 1)
        self.nc.scalar.activation(self.pt[:, n % 2, 0:i + 1].rearrange("p j n -> p (j n)"), self.b_t[:, 0:i * P + P],
                                  ACT.Copy).then_inc(self.t_ev, 1)


class FoxSample:

    RING = 4

    def __init__(self, ctx, sems, nc, pb, C, keep, scores, banks, dram):
        self.nc, self.pb, self.C, self.keep, self.dram = nc, pb, C, keep, dram
        sb = lambda n, s, d=F32: ctx.enter_context(nc.sbuf_tensor(n, s, d))
        sem = sems
        self.ring, self.b_o = banks[0:2], banks[2]
        self.table = sb("fs_table", [1, NB * PAGES], I32)
        self.kr, self.vr = sb("fs_keys", [P, self.RING, FT * PAGE]), sb("fs_values", [P, self.RING, FT * P])
        self.s, self.pt = scores, sb("fs_pt", [P, PAGES + 1, P])
        self.o = self.pt[:, 0:FT].rearrange("p j n -> p (j n)")
        self.q = sb("fs_q", [P, FT * (P + 16)])
        self.nm, self.rsum = sb("fs_nm", [P, 1]), sb("fs_rsum", [P, 1])
        self.k_in = [sem(f"fs_k_in{s}") for s in range(self.RING)]
        self.v_in = [sem(f"fs_v_in{s}") for s in range(self.RING)]
        self.t_in, self.bias_in, self.k_used, self.v_used = sem("fs_table_in"), sem("fs_bias_in"), sem("fs_k_used"), sem("fs_v_used")
        self.q_in, self.s_mm, self.s_ev, self.maxed, self.exped = sem("fs_q_in"), sem("fs_s_mm"), sem("fs_s_ev"), sem("fs_maxed"), sem("fs_exped")
        self.t_mm, self.t_ev, self.inverted = sem("fs_t_mm"), sem("fs_t_ev"), sem("fs_inverted")
        self.o_mm, self.o_ev, self.ot_mm, self.done, self.zeroed = sem("fs_o_mm"), sem("fs_o_ev"), sem("fs_ot_mm"), sem("fs_done"), sem("fs_zeroed")

    def seed(self, pool):
        pool.nop().then_inc(self.k_used, self.RING)
        pool.nop().then_inc(self.v_used, self.RING)
        pool.nop().then_inc(self.t_mm, 1)
        self.nc.gpsimd.memset(self.q[:], 0.0).then_inc(self.zeroed, 1)

    def seed_done(self, dve):
        dve.nop().then_inc(self.done, 1)

    def load_table(self, sp):
        sp.dma_start(self.table[:], self.dram["table"]).then_inc(self.t_in, 16)
        sp.wait_ge(self.t_in, 16)

    def load(self, sp, c):
        sp.wait_ge(self.t_mm, 5 * c + 1)
        later = self.dram["later"][bass.ds(2 * NH * c, 2 * NH)]
        sp.dma_start(self.s[:, 0:PAST], later[:, None, :].broadcast_to([2 * NH, NT, PAST])).then_inc(self.bias_in, 16)
        for buf, used, landed, src in ((self.kr, self.k_used, self.k_in, "keys"), (self.vr, self.v_used, self.v_in, "values")):
            with sp.Fori(0, 2 * PAGES // self.RING) as i:
                for n in range(self.RING):
                    j, k = n // 2, n % 2
                    at = 2 * PAGES * c + PAGES * k + PAGES - 1 - j - self.RING // 2 * i
                    page = sp.value_load(self.table[0:1, bass.ds(at, 1)], min_val=0, max_val=NPOOL - 1)
                    sp.wait_ge(used, 2 * PAGES * c + self.RING * i + n + 1)
                    sp.dma_start(buf[:, n], self.dram[src][bass.ds(page, 1)].rearrange("a p n -> p (a n)"))\
                      .then_inc(landed[n], 16)

    def landed(self, c, n):
        return 16 * (2 * PAGES // self.RING * c + n // self.RING + 1)

    def act_queries(self, act, c):
        act.wait_ge(self.k_used, 2 * PAGES * c + self.RING)
        for u in range(2):
            r = slice(64 * u, 64 * u + 64)
            src = self.pb[r, FQ0:FQ0 + FT, bass.ds(SEQ + 2 * NT * c, 2 * NT)].rearrange("p i (k t) -> p i k t", k=2)
            blocks = self.q[r].rearrange("p (i m) -> p i m", i=FT)[:, :, NT * u:NT * u + P]
            dst = blocks.rearrange("p i (k m) -> p i k m", k=2)[:, :, :, 0:NT]
            self.nc.scalar.activation(dst, src, ACT.Copy).then_inc(self.q_in, 1)

    def queries(self, i, k):
        return self.q[:, i * P + 64 * k:i * P + 64 * k + 64]

    def pe_new(self, pe, c):
        pe.wait_ge(self.q_in, 2 * c + 2)
        for k in range(2):
            for i in range(FT):
                mm = self.nc.tensor.matmul(self.ring[0][64 * k:64 * k + 64, 0:64], self.queries(i, k), self.pb[:, FK0 + i, SEQ:TOK],
                                           start=i == 0, stop=i == FT - 1)
        mm.then_inc(self.s_mm, 1)

    def pe_keys(self, pe, c, j, k):
        n, g = 2 * j + k, j // 4 + 1
        if n % 8 == 0 and g >= 2:
            pe.wait_ge(self.s_ev, 5 * c + g - 1)
        pe.wait_ge(self.k_in[n % self.RING], self.landed(c, n))
        out = self.ring[g % 2][64 * k:64 * k + 64, j % 4 * PAGE:j % 4 * PAGE + PAGE]
        for i in range(FT):
            mm = self.nc.tensor.matmul(out, self.queries(i, k), self.kr[:, n % self.RING, i * PAGE:i * PAGE + PAGE],
                                       start=i == 0, stop=i == FT - 1)
        mm.then_inc(self.k_used, 1)

    def pages(self, q):
        return range(4 * q, 4 * q + 4) if q < 3 else (12, 13, 14) if q == 3 else (15,)

    def pe_turn(self, pe, c, q):
        bank = self.ring[(5 + q) % 2]
        if q == 0:
            pe.wait_ge(self.exped, c + 1)
        if q >= 2:
            pe.wait_ge(self.t_ev, 5 * c + q - 1)
        for m, j in enumerate(self.pages(q)):
            mm = self.nc.tensor.transpose(bank[:, m * P:m * P + P], self.s[:, j * PAGE:j * PAGE + PAGE], self.C["ident"])
        if q == 4:
            mm = self.nc.tensor.transpose(bank[0:64, P:2 * P], self.s[:, PAST:PAST + 64], self.C["ident"])
        mm.then_inc(self.t_mm, 1)

    def pe_values(self, pe, c, j, k):
        n = 2 * j + k
        if n == 0:
            pe.wait_ge(self.t_ev, 5 * c + 5)
            pe.wait_ge(self.done, c + 1)
        pe.wait_ge(self.v_in[n % self.RING], self.landed(c, n))
        self.nc.tensor.matmul(self.b_o[64 * k:64 * k + 64], self.pt[:, j, 64 * k:64 * k + 64], self.vr[:, n % self.RING],
                              start=j == 0, stop=False).then_inc(self.v_used, 1)

    def pe_new_values(self, pe):
        for k in range(2):
            mm = self.nc.tensor.matmul(self.b_o[64 * k:64 * k + 64], self.pt[0:64, PAGES, 64 * k:64 * k + 64],
                                       self.keep["vn"][:], start=False, stop=True)
        mm.then_inc(self.o_mm, 1)

    def pe_out(self, pe, c):
        pe.wait_ge(self.o_ev, c + 1)
        for i in range(FT):
            mm = self.nc.tensor.transpose(self.b_o[:, i * P:i * P + P], self.o[:, i * P:i * P + P], self.C["ident"])
        mm.then_inc(self.ot_mm, 1)

    def dve_scores(self, dve, c, g):
        bank = self.ring[g % 2]
        if g == 0:
            dve.wait_ge(self.s_mm, c + 1)
            new = self.keep["newb"][:, bass.ds(c, 1)].rearrange("p a n -> p (a n)")
            self.nc.vector.tensor_tensor(self.s[:, PAST:PAST + 64], bank[:, 0:64], new, ALU.add).then_inc(self.s_ev, 1)
        else:
            dve.wait_ge(self.k_used, 2 * PAGES * c + self.RING + 8 * g)
            if g == 1:
                dve.wait_ge(self.bias_in, 16 * c + 16)
            s = self.s[:, 512 * (g - 1):512 * g]
            self.nc.vector.tensor_tensor(s, bank[:], s, ALU.add).then_inc(self.s_ev, 1)

    def dve_max(self, dve, c):
        dve.wait_ge(self.s_ev, 5 * c + 5)
        self.nc.vector.tensor_reduce(self.nm[:], self.s[:], AX.X, ALU.max, negate=True).then_inc(self.maxed, 1)

    def act_exp(self, act, c):
        act.wait_ge(self.maxed, c + 1)
        self.nc.scalar.activation(self.s[:], self.s[:], ACT.Exp, bias=self.nm[:], accum_out=self.rsum[:]).then_inc(self.exped, 1)

    def act_turned(self, act, c, q):
        nc, bank, pages = self.nc, self.ring[(5 + q) % 2], self.pages(q)
        act.wait_ge(self.t_mm, 5 * c + q + 2)
        w = len(pages) * P
        if q == 4:
            nc.scalar.activation(self.pt[0:64, PAGES], bank[0:64, P:2 * P], ACT.Copy)
        dst = self.pt[:, pages[0]:pages[-1] + 1].rearrange("p j n -> p (j n)")
        nc.scalar.activation(dst, bank[:, 0:w], ACT.Copy).then_inc(self.t_ev, 1)

    def dve_inverse(self, dve, c):
        dve.wait_ge(self.exped, c + 1)
        self.nc.vector.reciprocal(self.rsum[:], self.rsum[:]).then_inc(self.inverted, 1)

    def dve_normalise(self, dve, c):
        dve.wait_ge(self.inverted, c + 1)
        dve.wait_ge(self.o_mm, c + 1)
        self.nc.vector.tensor_scalar(self.o, self.b_o[:], self.rsum[:], None, ALU.mult).then_inc(self.o_ev, 1)

    def dve_out(self, dve, c):
        dve.wait_ge(self.ot_mm, c + 1)
        for u in range(2):
            r = slice(64 * u, 64 * u + 64)
            for i in range(FT):
                src = self.b_o[r, i * P:i * P + P].rearrange("p (k n) -> p k n", k=2)[:, :, 16 * i + NT * u:16 * i + NT * u + NT]
                dst = self.pb[r, FQ0 + i, bass.ds(SEQ + 2 * NT * c, 2 * NT)].rearrange("p (k t) -> p k t", k=2)
                last = self.nc.vector.tensor_scalar(dst, src, 1.0, None, ALU.mult)
        last.then_inc(self.done, 1)


def turn_steps():
    rw = [("operands", None, 3.0)] + [("gram", n, 0.9) for n in range(3 + 8)]
    for level in range(7):
        for kind, ns in (("t", 0.9), ("xt", 0.9), ("x", 0.4)):
            if kind != "x" or level < 6:
                rw += [(kind, (level, bt), ns) for bt in range(2)]
    rw += [("r", None, 2.6), ("u", None, 0.9), ("yd", None, 6.0)]
    units = FoxPrompt.UNITS
    fp = [("fp_copy", None, 8.0), ("fp_in", None, 4.0), ("scores", 0, 0.6), ("exp", 0, 0.5)]
    for n in range(8):
        w = units[n][1] + 1
        if n < 7:
            fp += [("scores", n + 1, 0.2 * w)]
        fp += [("normalise", n, 0.2)]
        if n < 7:
            fp += [("exp", n + 1, 0.2)]
        fp += [("turn", n, 0.2 * w)]
        fp += [("values", n, 0.4 * w)]
    fp += [("fp_out", None, 0.5)]
    fs = [("fs_in", None, 0.5), ("fs_new", None, 0.5), ("fs_scores", 0, 0.1)]
    for j in range(PAGES):
        fs += [("keys", (j, k), 0.85) for k in range(2)]
        if j % 4 == 3:
            fs += [("fs_scores", j // 4 + 1, 0.1)]
    fs += [("fs_max", None, 4.0), ("fs_exp", None, 4.0)] + [("fs_turn", q, 1.0) for q in range(5)]
    fs += [("cached", (j, k), 0.85) for j in range(PAGES) for k in range(2)]
    fs += [("fs_new_values", None, 2.5), ("fs_out", None, 1.0), ("fs_done", None, 1.0)]
    woven = []
    for order, chain in enumerate((rw, fp, fs)):
        total, at = sum(s[2] for s in chain), 0.0
        for step, n, time in chain:
            woven.append((at / total, order, len(woven), step, n))
            at += time
    return [(step, n) for _, _, _, step, n in sorted(woven, key=lambda s: s[:3])]


TURN = turn_steps()


def mix(nc, pb, C, keep, past, spare, dram):
    with Semaphores(nc) as sems, ExitStack() as ctx:
        sb = lambda n, s, d=F32: ctx.enter_context(nc.sbuf_tensor(n, s, d))
        sem = sems
        bank = [ctx.enter_context(nc.psum_tensor(f"m_bank{i}", [P, 512], F32)) for i in range(8)]
        room = spare[:].rearrange("p k n -> p (k n)")[:, 0:4 * NH * CH].rearrange("p (a h n) -> p a h n", a=2, h=NH)
        early = [sb(n, [P, 2, FT, CH]) for n in ("rw_exps", "rw_bk", "rw_cc_v")]
        late = [e[:].rearrange("p a f n -> p (a f) n") for e in early]
        buf = dict(bank=[bank[0][:], bank[1][:]], e1=early[0][:, 0], e3=early[0][:, 1], bf=early[1][:, 0], kf=early[1][:, 1],
                   cc=early[2][:, 0], vf=early[2][:, 1], tt=late[0], xt=late[1], x=late[2],
                   ar=sb("rw_ar", [P, FT, 2, CH]), ntg=room[:, 0], nkg=room[:, 1], rs=spare[:, DK - 1, TOK - 512:TOK],
                   bt=sb("rw_bt", [P, 512]), kt=sb("rw_kt", [P, 512]), vt=sb("rw_vt", [P, 512]), us=sb("rw_us", [P, 512]),
                   s_mid=sb("rw_s_mid", [P, FT, DH]), s=sb("rw_s", [P, FT, DH]))
        chunk = Rwkv(ctx, sems, nc, "", CH, 7, pb, C, keep, buf, False)
        zeroed, out = sem("m_zeroed"), sem("m_out")
        fp = FoxPrompt(ctx, sems, nc, pb, C, keep, [b[:] for b in bank[2:5]])
        fs = FoxSample(ctx, sems, nc, pb, C, keep, past, [b[:] for b in bank[5:8]], dram)
        block = ctx.enter_context(nc.Block())

        @block.sync
        def _(sp):
            fs.load_table(sp)
            with sp.Fori(0, NCH) as c:
                fs.load(sp, c)
            sp.wait_ge(chunk.done, 1 + NCH)
            sp.dma_start(dram["state_prompt"], buf["s"][:]).then_inc(out, 16)
            sp.wait_ge(out, 16)

        @block.gpsimd
        def _(pool):
            fs.seed(pool)
            with pool.Fori(0, NCH) as c:
                for step, n in TURN:
                    if step == "operands":
                        chunk.pool_v(pool, c)
                    if step == "fp_copy":
                        fp.pool(pool, c)

        @block.vector
        def _(dve):
            nc.vector.memset(buf["s"][:], 0.0).then_inc(zeroed, 1)
            chunk.seed(dve)
            fp.seed(dve)
            fs.seed_done(dve)
            dve.wait_ge(zeroed, 1)
            with dve.Fori(0, NCH) as c:
                for step, n in TURN:
                    if step == "operands":
                        chunk.dve_operands(dve, c)
                        chunk.dve_state_in(dve, c)
                    if step == "gram":
                        chunk.dve_gram(dve, c, n)
                    if step == "t":
                        chunk.dve_t(dve, c, *n)
                    if step == "xt":
                        chunk.dve_xt(dve, c, *n)
                    if step == "u":
                        chunk.dve_u(dve, c)
                    if step == "yd":
                        chunk.dve_yd(dve, c)
                    if step == "fp_in":
                        fp.dve_in(dve, c)
                    if step == "scores":
                        fp.dve_scores(dve, c, n)
                    if step == "normalise":
                        fp.dve_normalise(dve, c, n)
                    if step == "fs_scores":
                        fs.dve_scores(dve, c, n)
                    if step == "fs_max":
                        fs.dve_max(dve, c)
                    if step == "fs_turn" and n == 0:
                        fs.dve_inverse(dve, c)
                    if step == "fs_out":
                        fs.dve_normalise(dve, c)
                    if step == "fs_done":
                        fs.dve_out(dve, c)

        @block.scalar
        def _(act):
            act.wait_ge(fs.zeroed, 1)
            with act.Fori(0, NCH) as c:
                for step, n in TURN:
                    if step == "operands":
                        chunk.act_exps(act, c)
                    if step == "x":
                        chunk.act_x(act, c, *n)
                    if step == "r":
                        chunk.act_r(act, c)
                    if step == "fp_in":
                        fp.act_in(act, c)
                    if step == "exp":
                        fp.act_exp(act, c, n)
                    if step == "turn":
                        fp.act_turned(act, c, n)
                    if step == "fp_out":
                        fp.act_out(act, c)
                    if step == "fs_in":
                        fs.act_queries(act, c)
                    if step == "fs_exp":
                        fs.act_exp(act, c)
                    if step == "fs_turn":
                        fs.act_turned(act, c, n)

        @block.tensor
        def _(pe):
            with pe.Fori(0, NCH) as c:
                for step, n in TURN:
                    if step == "gram":
                        chunk.pe_gram(pe, c, n)
                    if step == "t":
                        chunk.pe_level(pe, c, *n)
                    if step == "xt":
                        chunk.pe_level_xt(pe, c, *n)
                    if step == "x":
                        chunk.pe_level_x(pe, c, *n)
                    if step == "r":
                        chunk.pe_r(pe, c)
                    if step == "u":
                        chunk.pe_u(pe, c)
                    if step == "yd":
                        chunk.pe_y(pe, c)
                        chunk.pe_d(pe, c)
                    if step == "fp_in":
                        fp.pe_in(pe, c)
                    if step == "scores":
                        fp.pe_scores(pe, c, n)
                    if step == "turn":
                        fp.pe_turn(pe, c, n)
                    if step == "values":
                        fp.pe_values(pe, c, n)
                    if step == "fs_new":
                        fs.pe_new(pe, c)
                    if step == "keys":
                        fs.pe_keys(pe, c, *n)
                    if step == "fs_turn":
                        fs.pe_turn(pe, c, n)
                    if step == "cached":
                        fs.pe_values(pe, c, *n)
                    if step == "fs_new_values":
                        fs.pe_new_values(pe)
                    if step == "fs_done":
                        fs.pe_out(pe, c)
    with Semaphores(nc) as sems, ExitStack() as ctx:
        sb = lambda n, s, d=F32: ctx.enter_context(nc.sbuf_tensor(n, s, d))
        sem = sems
        bank = [ctx.enter_context(nc.psum_tensor(f"s_bank{i}", [P, 512], F32)) for i in range(2)]
        T = NB * NT
        buf = dict(bank=[bank[0][:], bank[1][:]],
                   cc=sb("sw_cc", [P, FT, T]), e1=sb("sw_e1", [P, FT, T]), e3=sb("sw_e3", [P, FT, T]),
                   ar=sb("sw_ar", [P, FT, 2, T]), bf=sb("sw_bf", [P, FT, T]), kf=sb("sw_kf", [P, FT, T]),
                   vf=sb("sw_vf", [P, FT, T]), bt=sb("sw_bt", [P, 512]), kt=sb("sw_kt", [P, 512]), vt=sb("sw_vt", [P, 512]),
                   ntg=sb("sw_ntg", [P, NH, 2 * T]), nkg=sb("sw_nkg", [P, NH, 2 * T]),
                   x=sb("sw_x", [P, NH, T]), xt=sb("sw_xt", [P, NH, T]), tt=sb("sw_tt", [P, NH, T]),
                   rs=sb("sw_rs", [P, 512]), us=sb("sw_us", [P, 512]), s0=sb("sw_s0", [P, FT, NB, DH]),
                   sa=sb("sw_sa", [P, FT, 2, T]), ux=sb("sw_ux", [P, 2, 2, 512]), vx=sb("sw_vx", [P, 2, 2, 512]),
                   s_loaded=sem("sw_s_loaded"), x_part=sem("sw_x_part"), y_taken=sem("sw_y_taken"), s_added=sem("sw_s_added"))
        sample = Rwkv(ctx, sems, nc, "_s", T, 3, pb, C, keep, buf, True)
        out = sem("s_out")
        block = ctx.enter_context(nc.Block())

        @block.sync
        def _(sp):
            sp.dma_start(buf["s0"][:], dram["state_in"]).then_inc(sample.s_loaded, 16)
            sp.wait_ge(sample.done, 1 + FT)
            sp.dma_start(dram["state_sample"], buf["s0"][:]).then_inc(out, 16)
            sp.wait_ge(out, 16)

        @block.gpsimd
        def _(pool):
            sample.pool_v(pool, 0)

        @block.vector
        def _(dve):
            sample.seed(dve)
            sample.dve_operands(dve, 0)
            for n in range(sample.rounds):
                sample.dve_gram(dve, 0, n)
            for level in range(3):
                for bt in range(2):
                    sample.dve_t(dve, 0, level, bt)
                for bt in range(2):
                    sample.dve_xt(dve, 0, level, bt)
            dve.wait_ge(sample.s_loaded, 16)
            sample.dve_sample(dve)

        @block.scalar
        def _(act):
            sample.act_exps(act, 0)
            for level in range(2):
                for bt in range(2):
                    sample.act_x(act, 0, level, bt)
            sample.act_sample(act)

        @block.tensor
        def _(pe):
            for n in range(sample.rounds):
                sample.pe_gram(pe, 0, n)
            for level in range(3):
                for bt in range(2):
                    sample.pe_level(pe, 0, level, bt)
                for bt in range(2):
                    sample.pe_level_xt(pe, 0, level, bt)
                if level < 2:
                    for bt in range(2):
                        sample.pe_level_x(pe, 0, level, bt)
            sample.pe_sample(pe)


def finish_mixers(sems, nc, pb, C, dram, ya, yb):
    with ExitStack() as ctx:
        sb = lambda n, s, d=F32: ctx.enter_context(nc.sbuf_tensor(n, s, d))
        sem = sems
        ps = ctx.enter_context(nc.psum_tensor("d_ps", [P, 4, 2, 512], F32))
        par, rk8 = C["par"], pb[0:NH, RK0]
        g2, sq = sb("d_g2", [P, 512]), sb("d_sq", [P, 2, TOK])
        mean, rstd, bonus = sb("d_mean", [NH, TOK]), sb("d_rstd", [NH, TOK]), sb("d_bonus", [P, 2, TOK])
        loaded, sum_mm, mean_ev, mean_mm, centred = sem("d_loaded"), sem("d_sum_mm"), sem("d_mean_ev"), sem("d_mean_mm"), sem("d_centred")
        squared, sq_mm, rooted, inverted = sem("d_squared"), sem("d_sq_mm"), sem("d_rooted"), sem("d_inverted")
        spread, used, high, low, v_link = sem("d_spread"), sem("d_used"), sem("d_high"), sem("d_low"), sem("d_v_link")
        sel8 = C["sel8"].rearrange("p (f h) -> p f h", f=FT)
        selt8 = C["selt8"][0:NH].rearrange("p (f n) -> p f n", f=FT)
        cut = lambda half: slice(half * HALF, half * HALF + HALF)
        y = lambda f: pb[:, R0 + f]
        block = ctx.enter_context(nc.Block())

        @block.sync
        def _(sp):
            sp.dma_start(g2[:], dram["g2"]).then_inc(loaded, 16)

        @block.tensor
        def _(pe):
            for f in range(FT):
                for half in range(2):
                    mm = nc.tensor.matmul(ps[0:NH, 0, half, 0:HALF], sel8[:, f], y(f)[:, cut(half)], start=f == 0, stop=f == FT - 1)
            mm.then_inc(sum_mm, 1)
            pe.wait_ge(mean_ev, 1)
            for f in range(FT):
                for half in range(2):
                    mm = nc.tensor.matmul(ps[:, f, half, 0:HALF], selt8[:, f], mean[:, cut(half)], start=True, stop=True)
                mm.then_inc(mean_mm, 1)
            pe.wait_ge(centred, FT)
            for f in range(FT):
                pe.wait_ge(squared, f + 1)
                for half in range(2):
                    mm = nc.tensor.matmul(ps[0:NH, 0, half, 0:HALF], sel8[:, f], sq[:, f % 2, cut(half)], start=f == 0, stop=f == FT - 1)
                mm.then_inc(sq_mm, 1)
            pe.wait_ge(loaded, 16)
            pe.wait_ge(inverted, 1)
            for f in range(FT):
                for n in range(3):
                    k = 3 * f + n
                    if k >= 4:
                        pe.wait_ge(used, k - 3)
                    src = ((selt8[:, f], rstd), (selt8[:, f], rk8), (g2[:, f * P:f * P + P], pb[:, LG0]))[n]
                    for half in range(2):
                        mm = nc.tensor.matmul(ps[:, k % 4, half, 0:HALF], src[0], src[1][:, cut(half)], start=True, stop=True)
                    mm.then_inc(spread, 1)

        @block.scalar
        def _(act):
            act.wait_ge(sum_mm, 1)
            nc.scalar.activation(halves(mean[:]), ps[0:NH, 0, :, 0:HALF], ACT.Copy, scale=1.0 / DH).then_inc(mean_ev, 1)
            for f in range(FT):
                act.wait_ge(centred, f + 1)
                if f >= 2:
                    act.wait_ge(sq_mm, f - 1)
                nc.scalar.activation(sq[:, f % 2], y(f), ACT.Square).then_inc(squared, 1)
            act.wait_ge(sq_mm, FT)
            nc.scalar.activation(halves(rstd[:]), ps[0:NH, 0, :, 0:HALF], ACT.Sqrt, scale=1.0 / DH,
                                 bias=C["lnx_eps"]).then_inc(rooted, 1)
            for f in range(FT):
                nc.scalar.activation(yb[0][:, f], pb[:, FQ0 + f], ACT.Copy).then_inc(high, 1)
            for f in range(FT):
                act.wait_ge(v_link, 5 * f + 5)
                nc.scalar.activation(ya[0][:, f], y(f), ACT.Copy).then_inc(high, 1)

        @block.gpsimd
        def _(pool):
            for f in range(FT):
                pool.wait_ge(high, f + 1)
                nc.gpsimd.tensor_tensor(yb[1][:, f], pb[:, FQ0 + f], yb[0][:, f].bitcast(F32), ALU.subtract)
            for f in range(FT):
                pool.wait_ge(high, FT + f + 1)
                nc.gpsimd.tensor_tensor(ya[1][:, f], y(f), ya[0][:, f].bitcast(F32), ALU.subtract).then_inc(low, 1)

        @block.vector
        def _(dve):
            for f in range(FT):
                dve.wait_ge(mean_mm, f + 1)
                nc.vector.tensor_tensor(halves(y(f)), halves(y(f)), ps[:, f, :, 0:HALF], ALU.subtract).then_inc(centred, 1)
            dve.wait_ge(rooted, 1)
            nc.vector.reciprocal(rstd[:], rstd[:]).then_inc(inverted, 1)
            link = Chain(dve, v_link)
            for f in range(FT):
                bank = lambda n: ps[:, (3 * f + n) % 4, :, 0:HALF]
                dve.wait_ge(spread, 3 * f + 1)
                link(nc.vector.scalar_tensor_tensor(halves(y(f)), halves(y(f)), par("lnw", f), bank(0), ALU.mult, ALU.mult))
                dve.nop().then_inc(used, 1)
                dve.wait_ge(spread, 3 * f + 2)
                link(nc.vector.tensor_tensor(halves(bonus[:, f % 2]), halves(pb[:, V0 + f]), bank(1), ALU.mult))
                dve.nop().then_inc(used, 1)
                link(nc.vector.scalar_tensor_tensor(y(f), y(f), par("lnb", f), bonus[:, f % 2], ALU.add, ALU.add))
                dve.wait_ge(spread, 3 * f + 3)
                link(nc.vector.tensor_tensor(halves(y(f)), halves(y(f)), bank(2), ALU.mult))
                link(dve.nop())
                dve.nop().then_inc(used, 1)


def merge(sems, nc, dense, x, pb, dram, ya, yb, w_o, w_out):
    with ExitStack() as ctx:
        sb = lambda n, s, d=F32: ctx.enter_context(nc.sbuf_tensor(n, s, d))
        sem = sems
        raw = pb[:, 0:8].rearrange("p i n -> p (i n)")[:, 0:4 * DK * P].rearrange("p (s k n) -> p s k n", s=4, k=DK)
        gates = pb[:, 8:12].rearrange("p (b a) n -> p b a n", b=2)
        prod = pb[:, 12:16].rearrange("p (b a) n -> p b a n", b=2)
        y = pb[:, 16:18]
        dense.buffers(ctx, "_m", DK, raw)
        mh, ml = sb("e_mh", [P, DK, TOK], F32R), sb("e_ml", [P, DK, TOK], F32R)
        x_in, gate_in = sem("e_x_in"), [sem("e_gate_in0"), sem("e_gate_in1")]
        m_link, merged, high, y_added = sem("e_m_link"), sem("e_merged"), sem("e_high"), sem("e_y_added")
        outs, proj = dense.stage(2 * DK), dense.stage(DK)
        block = ctx.enter_context(nc.Block())

        @block.sync
        def _(sp):
            sp.dma_start(x[:], dram["x_saved"]).then_inc(x_in, 16)
            dense.load(sp, outs, FT, lambda n: w_o[bass.ds(n, 1)].rearrange("a p k n -> p (a k) n"))
            dense.load(sp, proj, DK, lambda n: w_out[bass.ds(n, 1)].rearrange("a p k n -> p (a k) n"))

        @block.vector
        def _(dve):
            dense.split(dve, outs, FT)
            dense.split(dve, proj, DK)

        @block.scalar
        def _(act):
            for t in tiles(act, *outs):
                if not t.odd:
                    act.wait_ge(merged, t.couple + 1)
                    src = dram["gates"].rearrange("(a n) p m -> n p a m", a=2)
                    act.dma_start(gates[:, t.twin], src[bass.ds(t.couple, 1)].rearrange("o p a m -> p (o a) m"))\
                       .then_inc(gate_in[t.twin], 16)
                act.wait_ge(dense.mm_done, t.t + 5)
                nc.scalar.activation(halves(prod[:, t.twin, t.odd]), dense.out(t), ACT.Copy).then_inc(dense.evacuated, 1)
            for t in tiles(act, *proj):
                act.wait_ge(dense.mm_done, t.t + 5)
                act.wait_ge(y_added, t.n + 1)
                nc.scalar.activation(halves(y[:, t.odd]), dense.out(t), ACT.Copy).then_inc(dense.evacuated, 1)

        @block.gpsimd
        def _(pool):
            pool.nop().then_inc(merged, 2)
            pool.nop().then_inc(y_added, 2)
            for t in tiles(pool, *outs):
                if not t.odd:
                    continue
                n, b = t.couple, t.twin
                pool.wait_ge(dense.evacuated, t.t + 5)
                pool.wait_ge(gate_in[b], 16 * t.turn + 16)
                nc.gpsimd.tensor_tensor(prod[:, b], prod[:, b], gates[:, b], ALU.mult).then_inc(m_link, 1)
                pool.wait_ge(m_link, 3 * n + 1)
                one = prod[:, b, 0:1]
                nc.gpsimd.tensor_tensor(one, one, prod[:, b, 1:2], ALU.add).then_inc(m_link, 1)
                pool.wait_ge(m_link, 3 * n + 2)
                nc.gpsimd.tensor_copy(mh[:, bass.ds(n, 1)], one).then_inc(m_link, 1)
                pool.wait_ge(m_link, 3 * n + 3)
                nc.gpsimd.tensor_tensor(ml[:, bass.ds(n, 1)], one, mh[:, bass.ds(n, 1)].bitcast(F32), ALU.subtract)\
                    .then_inc(merged, 1)
            pool.wait_ge(x_in, 16)
            for t in tiles(pool, *proj):
                pool.wait_ge(dense.evacuated, t.t + 5)
                xn = x[:, bass.ds(t.n, 1)]
                nc.gpsimd.tensor_tensor(xn, y[:, t.odd:t.odd + 1], xn, ALU.add).then_inc(y_added, 1)

        @block.tensor
        def _(pe):
            def branch(t):
                hi, lo = yb if t.odd else ya
                return dense.whole(hi, lo, FT)(t)
            dense.multiply(pe, outs, branch)
            pe.wait_ge(merged, 2 + DK)
            dense.multiply(pe, proj, dense.whole(mh, ml, DK))


def build(nc, a, o):
    with ExitStack() as top:
        sb = lambda n, s, d=F32: top.enter_context(nc.sbuf_tensor(n, s, d))
        dense = Dense(Semaphores(nc), nc)
        cc, pars = sb("t_consts", [P, N_CCOL]), sb("t_params", [P, N_PCOL])
        ones, minus, eps = sb("t_ones", [P, P]), sb("t_minus", [P, P]), sb("t_eps", [P, 2])
        x = sb("t_x", [P, DK, TOK])
        C = {n: cc[:, CCOL[n]:CCOL[n] + w] for n, w in CC_COLS.items()}
        C["par"] = lambda n, i=0, rows=P: pars[0:rows, PCOL[n] + i:PCOL[n] + i + 1]
        C.update(ones=ones[:], minus=minus[:], eps=eps[:, 0:1], lnx_eps=eps[0:NH, 1:2])
        gain = lambda n: pars[:, PCOL[n]:PCOL[n] + DK]
        started = nc.alloc_semaphore(name="t_started")
        with nc.Block() as block:
            @block.vector
            def _(dve):
                nc.vector.memset(ones[:], 1.0)
                nc.vector.memset(minus[:], -1.0)
                nc.vector.memset(eps[:, 0:1], NORM_EPS)
                nc.vector.memset(eps[:, 1:2], LNX_EPS)

            @block.sync
            def _(sp):
                dense.seed(sp)
                sp.dma_start(pars[:], a["params"]).then_inc(started, 16)
                sp.dma_start(x[:], a["x"]).then_inc(started, 16)
                sp.dma_start(cc[:], a["c1"]).then_inc(started, 16)
                sp.wait_ge(started, 48)

        with Semaphores(nc) as sems:
            ffn(sems, nc, dense, "_1", x, gain("n1"), C, a["up1"], [a["down1a"], a["down1b"]])

        gates = nc.dram_tensor("gates_saved", [N_GATE, P, TOK], F32, kind="Internal").ap()
        later = nc.dram_tensor("later_saved", [NB * NH, PAST], F32, kind="Internal").ap()
        x_saved = nc.dram_tensor("x_saved", [P, DK, TOK], F32, kind="Internal").ap()
        with ExitStack() as mid:
            pb = mid.enter_context(nc.sbuf_tensor("t_pb", [P, N_P, TOK], F32))
            past = mid.enter_context(nc.sbuf_tensor("t_past", [P, PAST + 64], F32))
            with Semaphores(nc) as sems:
                project(sems, nc, dense, x, gain("n2"), C, a["w_in"], pb, gates, x_saved, past, a["table"], a["logf"])
            with ExitStack() as kept:
                kb = lambda n, s: kept.enter_context(nc.sbuf_tensor("k_" + n, s, F32))
                keep = {n: kb(n, s) for n, s in dict(
                    cum=[P, FT, TOK], kk=[P, FT, TOK], kka=[P, FT, TOK], newb=[P, NCH, 64],
                    mid=[P, FT, NCH], mexp=[P, 3, FT, NCH], vn=[64, FT * P]
                    ).items()}
                with Semaphores(nc) as sems:
                    prepare(sems, nc, pb, C, keep, past, dict(later=later, lora=a["lora"], shift_in=a["shift"], c2=a["c2"], v_out=o["v"],
                                                        k_out=o["k"], shift_out=o["shift"], logf_out=o["logf"]))
                mix(nc, pb, C, keep, past, x, dict(later=later, table=a["table"], keys=a["keys"], values=a["values"], state_in=a["state"],
                                             state_prompt=o["state_prompt"], state_sample=o["state_sample"]))
            fb = lambda n: mid.enter_context(nc.sbuf_tensor(n, [P, FT, TOK], F32R))
            ya, yb = (fb("t_ya_hi"), fb("t_ya_lo")), (fb("t_yb_hi"), fb("t_yb_lo"))
            with Semaphores(nc) as sems:
                finish_mixers(sems, nc, pb, C, dict(g2=a["g2"]), ya, yb)
            with Semaphores(nc) as sems:
                merge(sems, nc, dense, x, pb, dict(gates=gates, x_saved=x_saved), ya, yb, a["w_o"], a["w_out"])
        with Semaphores(nc) as sems:
            ffn(sems, nc, dense, "_2", x, gain("n3"), C, a["up2"], [a["down2a"], a["down2b"]],
                store=lambda sp, s: (sp.dma_start(o["x"], x[:]).then_inc(s, 16), sp.wait_ge(s, 16)))


def constants():
    s, t = np.arange(P)[:, None], np.arange(P)[None, :]
    f = lambda m: np.asarray(m, np.float32)
    c = {"ident": f(s == t), "low": f(np.concatenate([s < t, s <= t], 1))}
    same = (s // NT == t // NT)[:64, :64]
    lows = np.concatenate([same & (s < t)[:64, :64], same & (s <= t)[:64, :64]], 1)
    c["lows"] = np.concatenate([f(lows), np.zeros((64, P), np.float32)])
    c["lev"] = f(np.concatenate([(s // (2 * b) == t // (2 * b)) & (s // b % 2 == 1) & (t // b % 2 == 0)
                                 for b in (1, 2, 4, 8, 16, 32, 64)], 1))
    c["causal"] = np.where(t > s, np.float32(NEG), np.float32(0))
    k, h, step = s // 64, s // NT % NH, s % NT
    key = np.arange(64)[None, :]
    seen = [(key // NT == 2 * turn + k) & (key % NT <= step) for turn in range(NCH)]
    c["bmask"] = f(s // NT == np.arange(NB)[None, :])
    head = lambda ft, n, at: f(np.arange(n)[None, :] == at + 2 * ft + s // DH)
    c["sel8"] = np.concatenate([head(ft, NH, 0) for ft in range(FT)], 1)
    pad = lambda m: np.concatenate([m, np.zeros((P - m.shape[0], m.shape[1]), np.float32)])
    c["selt8"] = np.concatenate([pad(head(ft, NH, 0).T) for ft in range(FT)], 1)
    col = np.arange(TOK)[None, :]
    start = (col - SEQ) % NT == 0
    c2 = {"sel24": np.concatenate([head(i % FT, 24, 8 * (i // FT)) for i in range(12)], 1),
          "selt": np.concatenate([pad(head(i % FT, 24, 8 * (i // FT)).T) for i in range(12)], 1),
          "reset": np.tile(f(~np.where(col < SEQ, col % CH == 0, start)), (P, 1)),
          "fresh": np.tile(f(~np.where(col < SEQ, col == 0, start)), (P, 1)),
          "mnew": np.where(np.concatenate(seen, 1), np.float32(0), np.float32(NEG)),
          "nsel": pad(-f(h == np.arange(NH)[None, :]).T)}
    pack = lambda d, widths: np.ascontiguousarray(np.concatenate([d[n] for n in widths], 1))
    return pack(c, CC_COLS), pack(c2, CC2_COLS)


def weight_tiles(w):
    k, n = w.shape
    return w.reshape(k // P, P, n // P, P).transpose(2, 1, 0, 3)


def columns_of(v):
    return v.reshape(-1, P).T


def kernel(x_prompt, x_sample, cache_k, cache_v, cache_logf, state_wkv, state_shift, page_table,
           ffn1_norm, ffn1_wg, ffn1_wu, ffn1_wd, mix_norm, w_in, shift_mu,
           rwkv_w0, rwkv_w2, rwkv_a0, rwkv_a2, rwkv_g2, rwkv_k_k, rwkv_k_a, rwkv_r_k, rwkv_lnx_w, rwkv_lnx_b,
           fox_b_f, fox_q_norm, fox_k_norm, w_o_a, w_o_b, w_out,
           ffn2_norm, ffn2_wg, ffn2_wu, ffn2_wd):
    import concourse.bacc as bacc
    from concourse.bass_utils import run_bass_kernel_spmd

    A = lambda v: np.asarray(v)
    arrays = {}

    def put(name, v):
        arrays[name] = np.ascontiguousarray(v)

    x = np.concatenate([A(x_prompt)[0], A(x_sample).reshape(NB * NT, D)])
    put("x", x.T.reshape(DK, P, TOK).transpose(1, 0, 2))
    for n, wg, wu, wd in (("1", ffn1_wg, ffn1_wu, ffn1_wd), ("2", ffn2_wg, ffn2_wu, ffn2_wd)):
        up = np.stack([weight_tiles(A(wg)[0]), weight_tiles(A(wu)[0])], 1)
        put("up" + n, up.reshape(2 * sum(UP), P, DK, P))
        put(f"down{n}a", weight_tiles(A(wd)[0][:UP[0] * P]))
        put(f"down{n}b", weight_tiles(A(wd)[0][UP[0] * P:]))
    w = A(w_in)[0]
    f0 = (N_P - 1) * P
    w = np.concatenate([w[:, :f0 + NH], np.zeros((D, P - NH), w.dtype), w[:, f0 + NH:]], 1)
    put("w_in", weight_tiles(w))
    put("w_o", np.stack([weight_tiles(A(w_o_a)[0]), weight_tiles(A(w_o_b)[0])], 1).reshape(2 * DK, P, FT, P))
    put("w_out", weight_tiles(A(w_out)[0]))
    put("lora", np.concatenate([A(rwkv_w2)[0], A(rwkv_a2)[0]]))
    put("g2", A(rwkv_g2)[0])
    put("shift", A(state_shift)[0].T.reshape(N_SH, P, NB).transpose(1, 0, 2))
    put("state", A(state_wkv)[0].transpose(1, 3, 0, 2).reshape(FT, P, NB, DH).transpose(1, 0, 2, 3))
    put("table", A(page_table).reshape(1, -1))
    back = lambda v: A(v)[0][:, ::-1]
    put("keys", back(cache_k).reshape(NPOOL, PAGE, FT, 2 * DH).transpose(0, 3, 2, 1).reshape(NPOOL, P, FT * PAGE))
    put("values", back(cache_v).reshape(NPOOL, PAGE, NH * DH))
    put("logf", back(cache_logf).transpose(0, 2, 1))
    fill = lambda v, n: np.concatenate([v, np.zeros(P - n, np.float32)])
    stat = lambda p, q: np.concatenate([np.full(16, p, np.float32), np.full(8, q, np.float32)])
    cols = dict(n1=A(ffn1_norm)[0], n2=A(mix_norm)[0], n3=A(ffn2_norm)[0], mu=A(shift_mu)[0], w0=A(rwkv_w0)[0],
                a0=A(rwkv_a0)[0], kk=A(rwkv_k_k)[0], ka=A(rwkv_k_a)[0], rk=A(rwkv_r_k)[0].reshape(-1),
                lnw=A(rwkv_lnx_w)[0], lnb=A(rwkv_lnx_b)[0], qn=np.tile(A(fox_q_norm)[0], 2), kn=np.tile(A(fox_k_norm)[0], 2),
                bf=fill(A(fox_b_f)[0], NH), sc=fill(stat(1 / DH, 1), 24), ad=fill(stat(NORM_EPS, 0), 24))
    put("params", np.concatenate([columns_of(cols[n]) for n in PC_COLS], 1))
    c1, c2 = constants()
    put("c1", c1)
    put("c2", c2)

    outs = dict(x=(P, DK, TOK), k=(P, FT, TOK), v=(P, FT, TOK), logf=(NH, TOK), shift=(P, N_SH, 1 + NB),
                state_prompt=(P, FT, DH), state_sample=(P, FT, NB, DH))
    nc = bacc.Bacc("TRN2", target_bir_lowering=False, num_devices=1)
    a = {n: nc.dram_tensor("in_" + n, v.shape, mybir.dt.from_np(v.dtype), kind="ExternalInput").ap() for n, v in arrays.items()}
    o = {n: nc.dram_tensor("out_" + n, s, F32, kind="ExternalOutput").ap() for n, s in outs.items()}
    build(nc, a, o)
    r = run_bass_kernel_spmd(nc, [{"in_" + n: v for n, v in arrays.items()}], core_ids=[0]).results[0]
    r = {n: np.asarray(r["out_" + n]) for n in outs}

    rows = lambda v: v.transpose(2, 1, 0).reshape(v.shape[2], -1)
    xo, ko, vo, sh = rows(r["x"]), rows(r["k"]), rows(r["v"]), rows(r["shift"])
    lf = r["logf"].T
    p = lambda v, *s: np.ascontiguousarray(v[:SEQ]).reshape(1, 1, SEQ, *s)
    q = lambda v, *s: np.ascontiguousarray(v[SEQ:]).reshape(1, NB, NT, *s)
    sp = r["state_prompt"].reshape(2, DH, FT, 1, DH).transpose(3, 2, 0, 4, 1).reshape(1, 1, NH, DH, DH)
    ss = r["state_sample"].reshape(2, DH, FT, NB, DH).transpose(3, 2, 0, 4, 1).reshape(1, NB, NH, DH, DH)
    return (np.ascontiguousarray(xo[:SEQ])[None], np.ascontiguousarray(xo[SEQ:]).reshape(NB, NT, D),
            p(ko, NH, DH), p(vo, NH, DH), p(lf, NH), np.ascontiguousarray(sp), np.ascontiguousarray(sh[:1])[None],
            q(ko, NH, DH), q(vo, NH, DH), q(lf, NH), np.ascontiguousarray(ss), np.ascontiguousarray(sh[1:])[None])
```

```python
from contextlib import ExitStack

import numpy as np

import concourse.bass as bass
from concourse import mybir

F32 = mybir.dt.float32
F32R = mybir.dt.float32r
I32 = mybir.dt.int32
ACT = mybir.ActivationFunctionType
ALU = mybir.AluOpType
AX = mybir.AxisListType

P = 128
D = 1024
DK = D // P
SEQ = 512
NB, NT = 8, 8
TOK = SEQ + NB * NT
HALF = TOK // 2
DH = 64
NH = 8
FT = NH * DH // P
D_FF = 2816
UP = (12, 10)
N_SH = 14
N_P = 27
N_GATE = 16
CH = 128
NCH = SEQ // CH
PAGES = 16
PAGE = 128
NPOOL = 160
KAPPA = float(np.exp(-0.5))
NORM_EPS, LNX_EPS = 1e-6, 64e-5
NEG = -1e30
PAST = PAGES * PAGE
SLOTK = 12

PC_COLS = dict(n1=8, n2=8, n3=8, mu=14, w0=4, a0=4, kk=4, ka=4, rk=4, lnw=4, lnb=4, qn=1, kn=1, bf=1, sc=1, ad=1)
CC_COLS = dict(ident=P, low=2 * P, lows=P, lev=7 * P, causal=P, bmask=NB, sel8=FT * NH, selt8=FT * P)
CC2_COLS = dict(sel24=12 * 24, selt=12 * P, reset=TOK, fresh=TOK, mnew=NCH * 64, nsel=P)


def columns(widths):
    at, out = 0, {}
    for name, n in widths.items():
        out[name] = at
        at += n
    return out, at


CCOL, N_CCOL = columns(CC_COLS)
CCOL2, N_CCOL2 = columns(CC2_COLS)
PCOL, N_PCOL = columns(PC_COLS)


class Tile:

    def __init__(self, first, i, j):
        self.n = 4 * i + j
        self.t = first + self.n
        self.slot = (first + j) % 4
        self.pair = (first + j) % 2
        self.use = i + (first + j) // 4
        self.couple = 2 * i + j // 2
        self.twin = j // 2 % 2
        self.odd = j % 2
        self.turn = i


def tiles(eng, first, count):
    turns = count // 4
    if turns > 1:
        with eng.Fori(0, turns) as i:
            for j in range(4):
                yield Tile(first, i, j)
    elif turns:
        for j in range(4):
            yield Tile(first, 0, j)
    for j in range(count % 4):
        yield Tile(first, turns, j)


class Chain:

    def __init__(self, eng, sem):
        self.eng, self.sem, self.n, self.turn, self.inside = eng, sem, 0, None, 0

    def __call__(self, ins):
        self.n += 1
        ins.then_inc(self.sem, 1)
        self.eng.wait_ge(self.sem, self.n if self.turn is None else self.turn + self.n)

    def loop(self, i, per):
        self.before, self.per, self.n, self.turn = self.n, per, 0, i * per + self.n

    def end(self, turns):
        assert self.n == self.per, (self.sem, self.n, self.per)
        self.n, self.turn = self.before + turns * self.per, None


class Semaphores:

    def __init__(self, nc):
        self.nc, self.held = nc, []

    def __call__(self, name):
        self.held.append(self.nc.alloc_semaphore(name=name))
        return self.held[-1]

    def __enter__(self):
        return self

    def __exit__(self, kind, error, trace):
        if kind is None:
            self.nc.clear_and_free_semaphores(self.held)
            self.nc.all_engine_barrier()


class Dense:

    def __init__(self, sems, nc):
        self.nc = nc
        sem = sems
        self.landed = [sem(f"w_landed{s}") for s in range(4)]
        self.rounded = sem("w_rounded")
        self.split_done = sem("w_split")
        self.mm_done = sem("w_multiplied")
        self.evacuated = sem("w_evacuated")
        self.t = 0

    def buffers(self, ctx, tag, k=SLOTK):
        nc = self.nc
        sb = lambda n, s, d: ctx.enter_context(nc.sbuf_tensor(n, s, d))
        self.raw = sb("w_raw" + tag, [P, 4, k, P], F32)
        self.wh = sb("w_hi" + tag, [P, 2, k, P], F32R)
        self.wl = sb("w_lo" + tag, [P, 2, k, P], F32R)
        self.ps = ctx.enter_context(nc.psum_tensor("ps" + tag, [P, 4, 2, 512], F32))

    def stage(self, count):
        first, self.t = self.t, self.t + count
        return first, count

    def seed(self, sp):
        sp.nop().then_inc(self.split_done, 4)
        sp.nop().then_inc(self.mm_done, 4)
        sp.nop().then_inc(self.evacuated, 4)

    def load(self, sp, st, kn, src):
        for x in tiles(sp, *st):
            sp.wait_ge(self.split_done, x.t + 1)
            sp.dma_start(self.raw[:, x.slot, 0:kn], src(x.n)).then_inc(self.landed[x.slot], 16)

    def split(self, dve, st, kn):
        for x in tiles(dve, *st):
            self.split_tile(dve, x, kn)

    def split_tile(self, dve, x, kn):
        dve.wait_ge(self.landed[x.slot], 16 * x.use + 16)
        dve.wait_ge(self.mm_done, x.t + 3)
        hi, lo, raw = self.wh[:, x.pair, 0:kn], self.wl[:, x.pair, 0:kn], self.raw[:, x.slot, 0:kn]
        self.nc.vector.tensor_copy(hi, raw).then_inc(self.rounded, 1)
        dve.wait_ge(self.rounded, x.t + 1)
        self.nc.vector.tensor_tensor(lo, raw, hi.bitcast(F32), ALU.subtract).then_inc(self.split_done, 1)

    def multiply(self, pe, st, operands, lead=0, ready=None):
        ahead = [Tile(st[0], 0, j) for j in range(lead)]
        for x in ahead:
            pe.wait_ge(self.split_done, x.t + 5)
            pe.wait_ge(self.evacuated, x.t + 1)
        if lead:
            kn = len(operands(ahead[0]))
            for k in range(kn):
                ready(k)
                for x in ahead:
                    for half in range(2):
                        last = self.products(x, half, k, kn, operands(x)[k])
                    if k == kn - 1:
                        last.then_inc(self.mm_done, 1)
        for x in tiles(pe, st[0] + lead, st[1] - lead):
            pe.wait_ge(self.split_done, x.t + 5)
            pe.wait_ge(self.evacuated, x.t + 1)
            ops = operands(x)
            for half in range(2):
                for k, pair in enumerate(ops):
                    last = self.products(x, half, k, len(ops), pair)
            last.then_inc(self.mm_done, 1)

    def products(self, x, half, k, kn, pair):
        hi, lo = (a[:, half * HALF:(half + 1) * HALF] for a in pair)
        wh, wl, out = self.wh[:, x.pair, k], self.wl[:, x.pair, k], self.ps[:, x.slot, half, 0:HALF]
        self.nc.tensor.matmul(out, wh, hi, start=k == 0, stop=False)
        self.nc.tensor.matmul(out, wh, lo, start=False, stop=False)
        return self.nc.tensor.matmul(out, wl, hi, start=False, stop=k == kn - 1)

    def whole(self, hi, lo, kn):
        return lambda x: [(hi[:, k], lo[:, k]) for k in range(kn)]

    def out(self, x):
        return self.ps[:, x.slot, :, 0:HALF]


def halves(ap):
    return ap.rearrange("p (h n) -> p h n", h=2)


class Norm:

    BLOCKS = [(j * P, j * P, j * P + P) for j in range(SEQ // P)] + [(TOK - P, SEQ, TOK)]

    def __init__(self, ctx, sems, nc, tag, x, gain, consts, nh, nl, dense, loaded=None):
        self.loaded = loaded
        sb = lambda n, s, d=F32: ctx.enter_context(nc.sbuf_tensor(n + tag, s, d))
        sem = lambda n: sems(n + tag)
        self.nc, self.x, self.gain, self.consts, self.nh, self.nl = nc, x, gain, consts, nh, nl
        self.row, self.means = dense.ps[:, (dense.t + 2) % 4], dense.ps[:, (dense.t + 3) % 4, 0]
        self.sq = sb("n_sq", [P, 2, TOK])
        self.sum = sb("n_sum", [P, TOK])
        self.rs = sb("n_rs", [P, 8])
        self.y = sb("n_y", [P, 3, TOK])
        self.squared, self.added, self.summed, self.meaned = sem("n_squared"), sem("n_added"), sem("n_summed"), sem("n_meaned")
        self.rooted, self.inverted, self.spread = sem("n_rooted"), sem("n_inverted"), sem("n_spread")
        self.scaled, self.high = sem("n_scaled"), sem("n_high")
        self.split = [sem("n_split_even"), sem("n_split_odd")]

    def act(self, act):
        nc = self.nc
        for k in range(DK):
            if k >= 2:
                act.wait_ge(self.added, k - 1)
            if self.loaded is not None and k % 4 == 0:
                act.wait_ge(self.loaded["x"][k // 4], 16)
            nc.scalar.activation(self.sq[:, k % 2], self.x[:, k], ACT.Square).then_inc(self.squared, 1)
        act.wait_ge(self.meaned, 1)
        nc.scalar.activation(self.rs[:, 0:5], self.means[:, 0:5], ACT.Sqrt, scale=1.0 / D,
                             bias=self.consts["eps"]).then_inc(self.rooted, 1)
        for k in range(DK):
            act.wait_ge(self.scaled, k + 1)
            nc.scalar.activation(self.nh[:, k], self.y[:, k % 3], ACT.Copy).then_inc(self.high, 1)

    def pe(self, pe):
        nc = self.nc
        if self.loaded is not None:
            pe.wait_ge(self.loaded["rest"], 32)
        pe.wait_ge(self.summed, 1)
        for j, (a, _, _) in enumerate(self.BLOCKS):
            mm = nc.tensor.matmul(self.means[:, j:j + 1], self.sum[:, a:a + P],
                                  self.consts["ones"][:, 0:1], start=True, stop=True)
        mm.then_inc(self.meaned, 1)
        pe.wait_ge(self.inverted, 1)
        for j, (at, lo, hi) in enumerate(self.BLOCKS):
            for a, b in ((lo, min(hi, HALF)), (max(lo, HALF), hi)):
                if b > a:
                    h, o = divmod(a, HALF)
                    mm = nc.tensor.matmul(self.row[:, h, o:o + b - a], self.rs[:, j:j + 1].broadcast_to([P, P]),
                                          self.consts["ident"][:, a - at:b - at], start=True, stop=True)
        mm.then_inc(self.spread, 1)

    def dve(self, dve, dense, st):
        nc = self.nc
        for k in range(DK):
            dve.wait_ge(self.squared, k + 1)
            if k:
                dve.wait_ge(self.added, k)
                nc.vector.tensor_tensor(self.sum[:], self.sum[:], self.sq[:, k % 2], ALU.add).then_inc(self.added, 1)
            else:
                nc.vector.tensor_copy(self.sum[:], self.sq[:, 0]).then_inc(self.added, 1)
        dve.wait_ge(self.added, DK)
        dve.nop().then_inc(self.summed, 1)
        dense.split(dve, (st[0], 1), DK)
        dve.wait_ge(self.rooted, 1)
        nc.vector.reciprocal(self.rs[:, 0:5], self.rs[:, 0:5]).then_inc(self.inverted, 1)
        dense.split(dve, (st[0] + 1, 1), DK)
        if self.loaded is not None:
            dve.wait_ge(self.loaded["rest"], 32)
        dve.wait_ge(self.spread, 1)
        for k in range(DK):
            if k >= 3:
                self.wait_split(dve, k - 3)
            nc.vector.scalar_tensor_tensor(halves(self.y[:, k % 3]), halves(self.x[:, k]), self.gain[:, k:k + 1],
                                           self.row[:, :, 0:HALF], ALU.mult, ALU.mult).then_inc(self.scaled, 1)
            if k % 2:
                self.low(dve, nc.vector, k - 1)

    def pool(self, pool):
        for k in range(1, DK, 2):
            self.low(pool, self.nc.gpsimd, k)

    def wait_split(self, eng, k):
        eng.wait_ge(self.split[k % 2], k // 2 + 1)

    def wait(self, pe):
        return lambda k: self.wait_split(pe, k)

    def low(self, eng, ops, k):
        eng.wait_ge(self.high, k + 1)
        ops.tensor_tensor(self.nl[:, k], self.y[:, k % 3], self.nh[:, k].bitcast(F32), ALU.subtract)\
           .then_inc(self.split[k % 2], 1)


def ffn(sems, nc, dense, tag, x, gain, consts, w_up, w_down, loaded=None, out=None):
    with ExitStack() as ctx:
        sb = lambda n, s, d=F32: ctx.enter_context(nc.sbuf_tensor(n + tag, s, d))
        sem = lambda n: sems(n + tag)
        dense.buffers(ctx, tag)
        nh, nl = sb("f_nh", [P, DK, TOK], F32R), sb("f_nl", [P, DK, TOK], F32R)
        hh, hl = sb("f_hh", [P, UP[0], TOK], F32R), sb("f_hl", [P, UP[0], TOK], F32R)
        gate, up, y = sb("f_gate", [P, 2, TOK]), sb("f_up", [P, 2, TOK]), sb("f_y", [P, 2, TOK])
        norm = Norm(ctx, sems, nc, tag, x, gain, consts, nh, nl, dense, loaded)
        hid_link, hid_split, y_added = sem("hid_link"), sem("hid_split"), sem("y_added")
        x_stored = sem("x_stored")
        stages = []
        for n in UP:
            stages += [dense.stage(2 * n), dense.stage(DK)]
        before = [0, UP[0]]

        block = ctx.enter_context(nc.Block())

        @block.sync
        def _(sp):
            for half, n in enumerate(UP):
                src = w_up[2 * before[half]:2 * before[half] + 2 * n]
                dense.load(sp, stages[2 * half], DK, lambda t: src[bass.ds(t, 1)].rearrange("a p k n -> p (a k) n"))
                down = w_down[half]
                dense.load(sp, stages[2 * half + 1], n, lambda t: down[bass.ds(t, 1)].rearrange("a p k n -> p (a k) n"))
            if out is not None:
                for k in range(DK):
                    sp.wait_ge(y_added, 2 + DK + k + 1)
                    sp.dma_start(out[:, k], x[:, k]).then_inc(x_stored, 16)
                sp.wait_ge(x_stored, 16 * DK)

        @block.vector
        def _(dve):
            norm.dve(dve, dense, stages[0])
            for half, n in enumerate(UP):
                first, count = stages[2 * half]
                dense.split(dve, (first, count) if half else (first + 2, count - 2), DK)
                dense.split(dve, stages[2 * half + 1], n)

        @block.scalar
        def _(act):
            norm.act(act)
            for half, n in enumerate(UP):
                for t in tiles(act, *stages[2 * half]):
                    act.wait_ge(dense.mm_done, t.t + 5)
                    if not t.odd:
                        act.wait_ge(hid_split, before[half] + t.couple + 1)
                    buf, func = ((gate, ACT.Silu), (up, ACT.Copy))[t.odd]
                    nc.scalar.activation(halves(buf[:, t.twin]), dense.out(t), func).then_inc(dense.evacuated, 1)
                for t in tiles(act, *stages[2 * half + 1]):
                    act.wait_ge(dense.mm_done, t.t + 5)
                    act.wait_ge(y_added, DK * half + t.n + 1)
                    nc.scalar.activation(halves(y[:, t.odd]), dense.out(t), ACT.Copy, scale=0.5)\
                        .then_inc(dense.evacuated, 1)

        @block.gpsimd
        def _(pool):
            pool.nop().then_inc(hid_split, 2)
            pool.nop().then_inc(y_added, 2)
            norm.pool(pool)
            for half, n in enumerate(UP):
                if half:
                    pool.wait_ge(dense.mm_done, stages[2][0] + 4)
                for t in tiles(pool, *stages[2 * half]):
                    if not t.odd:
                        continue
                    pool.wait_ge(dense.evacuated, t.t + 5)
                    c = before[half] + t.couple
                    k, b = bass.ds(t.couple, 1), slice(t.twin, t.twin + 1)
                    nc.gpsimd.tensor_tensor(up[:, b], gate[:, b], up[:, b], ALU.mult).then_inc(hid_link, 1)
                    pool.wait_ge(hid_link, 2 * c + 1)
                    nc.gpsimd.tensor_copy(hh[:, k], up[:, b]).then_inc(hid_link, 1)
                    pool.wait_ge(hid_link, 2 * c + 2)
                    nc.gpsimd.tensor_tensor(hl[:, k], up[:, b], hh[:, k].bitcast(F32), ALU.subtract)\
                        .then_inc(hid_split, 1)
                for t in tiles(pool, *stages[2 * half + 1]):
                    pool.wait_ge(dense.evacuated, t.t + 5)
                    xn = x[:, bass.ds(t.n, 1)]
                    nc.gpsimd.tensor_tensor(xn, y[:, t.odd:t.odd + 1], xn, ALU.add).then_inc(y_added, 1)

        @block.tensor
        def _(pe):
            norm.pe(pe)
            for half, n in enumerate(UP):
                dense.multiply(pe, stages[2 * half], dense.whole(nh, nl, DK), 0 if half else 2, norm.wait(pe))
                dense.multiply(pe, stages[2 * half + 1], dense.whole(hh, hl, n), 1,
                               lambda k: pe.wait_ge(hid_split, 2 + before[half] + k + 1))


def project(sems, nc, dense, x, gain, consts, w_in, pb, gates_dram, x_dram, past, table_dram, logf_dram):
    with ExitStack() as ctx:
        sb = lambda n, s, d=F32: ctx.enter_context(nc.sbuf_tensor(n, s, d))
        sem = sems
        dense.buffers(ctx, "_p")
        nh, nl = sb("p_nh", [P, DK, TOK], F32R), sb("p_nl", [P, DK, TOK], F32R)
        gate = sb("p_gate", [P, 2, TOK])
        norm = Norm(ctx, sems, nc, "_p", x, gain, consts, nh, nl, dense)
        gate_stored = [sem("gate_stored0"), sem("gate_stored1")]
        table = sb("p_table", [1, NB * PAGES], I32)
        x_saved, table_in, past_in = sem("x_saved"), sem("p_table_in"), sem("p_past_in")
        plain, gates = dense.stage(N_P), dense.stage(N_GATE)
        block = ctx.enter_context(nc.Block())

        @block.sync
        def _(sp):
            sp.dma_start(x_dram, x[:]).then_inc(x_saved, 16)
            dense.load(sp, plain, DK, lambda n: w_in[bass.ds(n, 1)].rearrange("a p k n -> p (a k) n"))
            dense.load(sp, gates, DK, lambda n: w_in[N_P:][bass.ds(n, 1)].rearrange("a p k n -> p (a k) n"))
            sp.wait_ge(x_saved, 16)

        @block.gpsimd
        def _(pool):
            for s in gate_stored:
                pool.nop().then_inc(s, 16)
            norm.pool(pool)
            pool.dma_start(table[:], table_dram).then_inc(table_in, 16)
            nc.gpsimd.memset(past[0:64, 0:1], 0.0)
            pool.wait_ge(table_in, 16)
            for b in range(NB):
                with pool.Fori(0, PAGES) as j:
                    page = pool.value_load(table[0:1, bass.ds(PAGES * b + PAGES - 1 - j, 1)], min_val=0, max_val=NPOOL - 1)
                    pool.dma_start(past[NH * b:NH * b + NH, bass.ds(1 + j * PAGE, PAGE)],
                                   logf_dram[bass.ds(page, 1)].rearrange("a h n -> (a h) n")).then_inc(past_in, 16)
            pool.wait_ge(past_in, 16 * NB * PAGES)

        @block.vector
        def _(dve):
            norm.dve(dve, dense, plain)
            dense.split(dve, (plain[0] + 2, plain[1] - 2), DK)
            dense.split(dve, gates, DK)

        @block.scalar
        def _(act):
            norm.act(act)
            for t in tiles(act, *plain):
                act.wait_ge(dense.mm_done, t.t + 5)
                out = pb[:, bass.ds(t.n, 1)].rearrange("p a (h n) -> p (a h) n", h=2)
                nc.scalar.activation(out, dense.out(t), ACT.Copy).then_inc(dense.evacuated, 1)
            for t in tiles(act, *gates):
                act.wait_ge(dense.mm_done, t.t + 5)
                act.wait_ge(gate_stored[t.odd], 16 * t.couple + 16)
                nc.scalar.activation(halves(gate[:, t.odd]), dense.out(t), ACT.Sigmoid).then_inc(dense.evacuated, 1)
                act.wait_ge(dense.evacuated, t.t + 5)
                act.dma_start(gates_dram[bass.ds(t.n, 1)].rearrange("a p n -> p (a n)"), gate[:, t.odd])\
                   .then_inc(gate_stored[t.odd], 16)
            for s in gate_stored:
                act.wait_ge(s, 16 * (N_GATE // 2) + 16)

        @block.tensor
        def _(pe):
            norm.pe(pe)
            dense.multiply(pe, plain, dense.whole(nh, nl, DK), 2, norm.wait(pe))
            dense.multiply(pe, gates, dense.whole(nh, nl, DK))


RK0 = 12
R0, K0, V0, LW0, LG0, FQ0, FK0, FV0, FF0 = 0, 4, 8, 12, 13, 14, 18, 22, 26


def prepare(sems, nc, pb, C, keep, past, dram):
    with ExitStack() as ctx:
        sb = lambda n, s, d=F32: ctx.enter_context(nc.sbuf_tensor(n, s, d))
        sem = sems
        ps = ctx.enter_context(nc.psum_tensor("c_ps", [P, 4, 2, 512], F32))
        c2 = sb("c_c2", [P, N_CCOL2])
        K = lambda name, rows=P: c2[0:rows, CCOL2[name]:CCOL2[name] + CC2_COLS[name]]
        lora = sb("c_lora", [P, 2, 512])
        shift = sb("c_shift", [P, N_SH, NB])
        newshift = sb("c_newshift", [P, N_SH, 1 + NB])
        diff = sb("c_diff", [P, 4, TOK])
        lw = sb("c_lw", [P, FT, TOK])
        sq = sb("c_sq", [P, 2, TOK])
        stats = sb("c_st", [P, TOK])
        st = stats[0:24]
        gq = sb("c_gq", [P, 1])
        tmp = sb("c_tmp", [P, 2, TOK])
        f_z, f_m, f_a, f_e = sb("c_fz", [NH, TOK]), sb("c_fm", [NH, TOK]), sb("c_fa", [NH, TOK]), sb("c_fe", [NH, TOK])
        cum, kk, kka = keep["cum"], keep["kk"], keep["kka"]
        rk8, cn = pb[0:NH, RK0], pb[0:NH, FF0]
        par = C["par"]

        loaded, mixed, shifted, lora_act = sem("c_loaded"), sem("c_mixed"), sem("c_shifted"), sem("c_lora_act")
        lora_mm, lora_out, squares = sem("c_lora_mm"), sem("c_lora_out"), sem("c_squares")
        sq_used, kraw, biased, rooted, inverted = sem("c_sq_used"), sem("c_kraw"), sem("c_biased"), sem("c_rooted"), sem("c_inverted")
        spread, normed, scanned = sem("c_spread"), sem("c_normed"), sem("c_scanned")
        f_abs, f_exp, f_log, f_done = sem("c_f_abs"), sem("c_f_exp"), sem("c_f_log"), sem("c_f_done")
        rkprod, rksum, tp, mids = sem("c_rkprod"), sem("c_rksum"), sem("c_tp"), sem("c_mids")
        summed, c2_in, cleared = sem("c_summed"), sem("c_c2_in"), sem("c_cleared")
        v_link, a_link, stored = sem("c_v_link"), sem("c_a_link"), sem("c_stored")
        block = ctx.enter_context(nc.Block())

        @block.sync
        def _(sp):
            sp.dma_start(lora[:], dram["lora"]).then_inc(loaded, 16)
            sp.dma_start(shift[:], dram["shift_in"]).then_inc(loaded, 16)
            sp.wait_ge(summed, 1)
            sp.dma_start(dram["later"], past[0:64, 0:PAST]).then_inc(stored, 16)
            sp.dma_start(dram["v_out"], pb[:, FV0:FV0 + FT]).then_inc(stored, 16)
            sp.wait_ge(shifted, 1)
            sp.dma_start(dram["shift_out"], newshift[:]).then_inc(stored, 16)
            sp.wait_ge(f_done, 1)
            sp.dma_start(dram["logf_out"], f_z[:]).then_inc(stored, 16)
            sp.wait_ge(normed, 8)
            sp.dma_start(dram["k_out"], pb[:, FK0:FK0 + FT]).then_inc(stored, 16)
            sp.wait_ge(stored, 80)

        @block.vector
        def _(dve):
            link = Chain(dve, v_link)
            nc.vector.memset(stats[:], 0.0).then_inc(cleared, 1)
            nc.vector.tensor_tensor_scan(past[0:64, 0:PAST], C["ones"][0:64, 0:1].broadcast_to([64, PAST]), past[0:64, 0:PAST],
                                         0.0, ALU.mult, ALU.add).then_inc(summed, 1)
            tail = lambda a: a[:, :, SEQ:TOK].rearrange("p i (b t) -> p i b t", b=NB)
            dve.wait_ge(loaded, 32)
            nc.vector.tensor_copy(newshift[:, :, 0:1], pb[:, 0:N_SH, SEQ - 1:SEQ])
            link(nc.vector.tensor_copy(newshift[:, :, 1:1 + NB], tail(pb)[:, 0:N_SH, :, NT - 1]))
            dve.nop().then_inc(shifted, 1)
            def shift_tokens(a, n):
                p, d = pb[:, a:a + n], diff[:, 0:n]
                nc.vector.tensor_tensor(d[:, :, 1:SEQ], p[:, :, 0:SEQ - 1], p[:, :, 1:SEQ], ALU.subtract)
                nc.vector.tensor_scalar(d[:, :, 0:1], p[:, :, 0:1], -1.0, None, ALU.mult)
                ps_, ds_ = tail(p), tail(d)
                for i in range(n):
                    nc.vector.tensor_tensor(ds_[:, i, :, 1:NT], ps_[:, i, :, 0:NT - 1], ps_[:, i, :, 1:NT], ALU.subtract)
                link(nc.vector.tensor_tensor(ds_[:, :, :, 0], shift[:, a:a + n], ps_[:, :, :, 0], ALU.subtract))
                for i in range(n):
                    last = nc.vector.scalar_tensor_tensor(p[:, i], d[:, i], par("mu", a + i), p[:, i], ALU.mult, ALU.add)
                link(last)
                dve.nop().then_inc(mixed, 1)
            shift_tokens(LW0, 2)
            shift_tokens(K0, 4)
            for ft in range(FT):
                last = nc.vector.tensor_scalar(kk[:, ft], pb[:, K0 + ft], par("kk", ft), -1.0, ALU.mult, ALU.mult)
            link(last)
            dve.nop().then_inc(kraw, 1)
            z = pb[0:NH, FF0]
            link(nc.vector.tensor_scalar(f_z[:], z, par("bf", 0, NH), None, ALU.add))
            nc.vector.tensor_scalar(f_m[:], f_z[:], 0.0, None, ALU.min)
            nc.vector.scalar_tensor_tensor(f_a[:], f_z[:], -1.0, f_z[:], ALU.mult, ALU.max).then_inc(f_abs, 1)
            shift_tokens(R0, 4)
            dve.wait_ge(c2_in, 16)
            for ft in range(FT):
                dve.wait_ge(lora_out, ft + 1)
                nc.vector.tensor_tensor_scan(cum[:, ft], K("reset"), lw[:, ft], 0.0, ALU.mult, ALU.add)\
                    .then_inc(scanned, 1)
            dve.wait_ge(scanned, FT)
            dve.wait_ge(f_abs, 1)
            m, e = keep["mid"], keep["mexp"]
            nc.vector.tensor_copy(m[:], cum[:, :, CH // 2 - 1:SEQ:CH])
            link(nc.vector.tensor_copy(e[:, 1], cum[:, :, CH - 1:SEQ:CH]))
            link(nc.vector.tensor_tensor(e[:, 1], e[:, 1], m[:], ALU.subtract))
            dve.nop().then_inc(mids, 1)
            dve.wait_ge(f_log, 1)
            link(nc.vector.tensor_tensor(f_z[:], f_m[:], f_e[:], ALU.subtract))
            dve.nop().then_inc(f_done, 1)
            link(nc.vector.tensor_tensor_scan(cn, K("fresh", NH), f_z[:], 0.0, ALU.mult, ALU.add))
            dve.nop().then_inc(f_done, 1)
            dve.wait_ge(sq_used, 12)
            link(nc.vector.tensor_scalar(halves(st), ps[0:24, 0, :, 0:HALF], par("sc", 0, 24), par("ad", 0, 24),
                                         ALU.mult, ALU.add))
            nc.vector.tensor_scalar(st, st, 1e-24, None, ALU.max).then_inc(biased, 1)
            link(nc.vector.tensor_scalar(gq[:], par("qn", 0), float(DH) ** -0.5, None, ALU.mult))
            dve.wait_ge(rooted, 1)
            nc.vector.reciprocal(st, st).then_inc(inverted, 1)
            shift_tokens(V0, 4)
            for i in range(12):
                dve.wait_ge(spread, i + 1)
                src = ps[:, i % 4, :, 0:HALF]
                if i < 8:
                    t = pb[:, FQ0 + i]
                    g = gq[:] if i < 4 else par("kn", 0)
                    nc.vector.scalar_tensor_tensor(halves(t), halves(t), g, src, ALU.mult, ALU.mult).then_inc(normed, 1)
                else:
                    t = kk[:, i - 8]
                    nc.vector.tensor_tensor(halves(t), halves(t), src, ALU.mult).then_inc(normed, 1)
            for ft in range(FT):
                dve.wait_ge(lora_out, FT + ft + 1)
                k, r = pb[:, K0 + ft], pb[:, R0 + ft]
                link(nc.vector.tensor_scalar(tmp[:, 0], kka[:, ft], 1.0, par("ka", ft), ALU.subtract, ALU.mult))
                link(nc.vector.scalar_tensor_tensor(k, tmp[:, 0], 1.0, k, ALU.add, ALU.mult))
                if ft:
                    dve.wait_ge(rksum, ft)
                nc.vector.scalar_tensor_tensor(tmp[:, 1], r, par("rk", ft), k, ALU.mult, ALU.mult).then_inc(rkprod, 1)
                dve.wait_ge(normed, 9 + ft)
                link(nc.vector.scalar_tensor_tensor(kka[:, ft], kk[:, ft], -1.0, kka[:, ft], ALU.mult, ALU.mult))
            dve.wait_ge(rksum, FT)
            nc.vector.tensor_copy(halves(rk8), ps[0:NH, 0, :, 0:HALF])
            dve.wait_ge(tp, 1)
            nc.vector.tensor_copy(keep["vn"][:], ps[0:64, 1, 0, :])
            new = ps[:, None, 2, 0, 0:64].broadcast_to([P, NCH, 64])
            nc.vector.tensor_tensor(keep["newb"][:], K("mnew").rearrange("p (c n) -> p c n", c=NCH), new, ALU.add)

        @block.scalar
        def _(act):
            act.dma_start(c2[:], dram["c2"]).then_inc(c2_in, 16)

            def squared(i):
                if i >= 2:
                    act.wait_ge(sq_used, i - 1)
                src = pb[:, FQ0 + i] if i < 8 else kk[:, i - 8]
                nc.scalar.activation(sq[:, i % 2], src, ACT.Square).then_inc(squares, 1)
            for i in range(8):
                squared(i)
            act.wait_ge(mixed, 1)
            nc.scalar.activation(pb[0:64, LW0], pb[0:64, LW0], ACT.Tanh).then_inc(lora_act, 1)
            nc.scalar.activation(pb[:, LG0], pb[:, LG0], ACT.Sigmoid)
            for i in range(2 * FT):
                act.wait_ge(lora_mm, i + 1)
                out = lw[:, i] if i < FT else kka[:, i - FT]
                nc.scalar.activation(halves(out), ps[:, 1 + i % 3, :, 0:HALF], ACT.Sigmoid,
                                     bias=par("w0" if i < FT else "a0", i % FT)).then_inc(lora_out, 1)
            act.wait_ge(kraw, 1)
            for i in range(8, 12):
                squared(i)
            act.wait_ge(f_abs, 1)
            nc.scalar.activation(f_e[:], f_a[:], ACT.Exp, scale=-1.0).then_inc(f_exp, 1)
            act.wait_ge(f_exp, 1)
            nc.scalar.activation(f_e[:], f_e[:], ACT.Ln, bias=1.0).then_inc(f_log, 1)
            act.wait_ge(biased, 1)
            nc.scalar.activation(st, st, ACT.Sqrt).then_inc(rooted, 1)
            act.wait_ge(mids, 1)
            e = keep["mexp"]
            nc.scalar.activation(e[:, 0], keep["mid"][:], ACT.Exp, scale=-KAPPA)
            nc.scalar.activation(e[:, 2], keep["mid"][:], ACT.Exp, scale=KAPPA)
            nc.scalar.activation(e[:, 1], e[:, 1], ACT.Exp, scale=-KAPPA)

        @block.tensor
        def _(pe):
            pe.wait_ge(c2_in, 16)
            pe.wait_ge(cleared, 1)
            sel = K("sel24").rearrange("p (i m) -> p i m", i=12)

            def sum_squares(i):
                pe.wait_ge(squares, i + 1)
                for half in range(2):
                    mm = nc.tensor.matmul(ps[0:24, 0, half, 0:HALF], sel[:, i], sq[:, i % 2, half * HALF:half * HALF + HALF],
                                          start=i == 0, stop=i == 11)
                mm.then_inc(sq_used, 1)
            for i in range(8):
                sum_squares(i)
            pe.wait_ge(loaded, 32)
            pe.wait_ge(lora_act, 1)
            for i in range(2 * FT):
                if i >= 3:
                    pe.wait_ge(lora_out, i - 2)
                for half in range(2):
                    mm = nc.tensor.matmul(ps[:, 1 + i % 3, half, 0:HALF], lora[:, i // FT, (i % FT) * P:(i % FT) * P + P],
                                          pb[:, LW0, half * HALF:half * HALF + HALF], start=True, stop=True)
                mm.then_inc(lora_mm, 1)
            for i in range(8, 12):
                sum_squares(i)
            pe.wait_ge(inverted, 1)
            selt = K("selt").rearrange("p (i m) -> p i m", i=12)
            pe.wait_ge(lora_out, 2 * FT)
            for i in range(12):
                if i >= 4:
                    pe.wait_ge(normed, i - 3)
                for half in range(2):
                    mm = nc.tensor.matmul(ps[:, i % 4, half, 0:HALF], selt[:, i], stats[:, half * HALF:half * HALF + HALF],
                                          start=True, stop=True)
                mm.then_inc(spread, 1)
            pe.wait_ge(normed, 12)
            for ft in range(FT):
                pe.wait_ge(rkprod, ft + 1)
                for half in range(2):
                    mm = nc.tensor.matmul(ps[0:NH, 0, half, 0:HALF], sel[:, 8 + ft, 16:24],
                                          tmp[:, 1, half * HALF:half * HALF + HALF], start=ft == 0, stop=ft == FT - 1)
                mm.then_inc(rksum, 1)
            pe.wait_ge(f_done, 2)
            for i in range(FT):
                nc.tensor.transpose(ps[0:64, 1, 0, i * P:(i + 1) * P], pb[:, FV0 + i, SEQ:TOK], C["ident"])
            nc.tensor.matmul(ps[:, 2, 0, 0:64], K("nsel", NH), cn[:, SEQ:TOK], start=True, stop=True).then_inc(tp, 1)


class Rwkv:

    TR, BANKS = 3, 2

    def __init__(self, ctx, sems, nc, tag, T, levels, pb, C, keep, buf, sample):
        self.nc, self.T, self.levels, self.pb, self.C, self.keep, self.sample = nc, T, levels, pb, C, keep, sample
        self.bank, self.cc, self.e1, self.e3, self.ar = buf["bank"], buf["cc"], buf["e1"], buf["e3"], buf["ar"]
        self.bf, self.kf, self.vf, self.bt, self.kt, self.vt = (buf[n] for n in ("bf", "kf", "vf", "bt", "kt", "vt"))
        self.ntg, self.nkg, self.x, self.xt, self.tt = (buf[n] for n in ("ntg", "nkg", "x", "xt", "tt"))
        self.rs, self.us = buf["rs"], buf["us"]
        if sample:
            self.s0, self.sa, self.ux, self.vx = buf["s0"], buf["sa"], buf["ux"], buf["vx"]
            self.s_loaded, self.x_part, self.v_part, self.y_taken, self.s_added = (
                buf[n] for n in ("s_loaded", "x_part", "v_part", "y_taken", "s_added"))
        else:
            self.s, self.s_mid = buf["s"], buf["s_mid"]
        sem = lambda n: sems(n + tag)
        self.gram_heads = 512 // (2 * T)
        self.rounds = 3 + 2 * (NH // self.gram_heads)
        self.centred, self.exped, self.shifted, self.ready = sem("rw_centred"), sem("rw_exped"), sem("rw_shifted"), sem("rw_ready")
        self.v_copied, self.mm, self.ev = sem("rw_v_copied"), sem("rw_mm"), sem("rw_evacuated")
        self.t_mm, self.t_ev = [sem("rw_t_mm0"), sem("rw_t_mm1")], [sem("rw_t_ev0"), sem("rw_t_ev1")]
        self.xt_mm, self.xt_ev = [sem("rw_xt_mm0"), sem("rw_xt_mm1")], [sem("rw_xt_ev0"), sem("rw_xt_ev1")]
        self.x_mm, self.x_ev = [sem("rw_x_mm0"), sem("rw_x_mm1")], [sem("rw_x_ev0"), sem("rw_x_ev1")]
        self.sm, self.r_mm, self.r_ev, self.u_mm, self.u_ev = sem("rw_sm"), sem("rw_r_mm"), sem("rw_r_ev"), sem("rw_u_mm"), sem("rw_u_ev")
        self.y_mm, self.d_mm, self.d_part, self.done = sem("rw_y_mm"), sem("rw_d_mm"), sem("rw_d_part"), sem("rw_done")

    def seed(self, dve):
        dve.nop().then_inc(self.done, 1)

    def cols(self, c):
        return slice(SEQ, TOK) if self.sample else bass.ds(c * CH, CH)

    def heads(self, g):
        first = g % (NH // self.gram_heads)
        return [first % 2 + 2 * (first // 2 * self.gram_heads + j) for j in range(self.gram_heads)]

    def act_exps(self, act, c):
        T = self.T
        act.wait_ge(self.centred, c + 1)
        self.nc.scalar.activation(self.e1[:, :, 0:T], self.cc[:, :, 0:T], ACT.Exp, scale=-KAPPA).then_inc(self.exped, 1)
        self.nc.scalar.activation(self.e3[:, :, 0:T], self.cc[:, :, 0:T], ACT.Exp, scale=KAPPA).then_inc(self.exped, 1)

    def pool_v(self, pool, c):
        pool.wait_ge(self.done, c + 1)
        self.nc.gpsimd.tensor_copy(self.vf[:, :, 0:self.T], self.pb[:, V0:V0 + FT, self.cols(c)]).then_inc(self.v_copied, 1)

    def dve_operands(self, dve, c):
        nc, T, t, pb, keep = self.nc, self.T, self.cols(c), self.pb, self.keep
        if self.sample:
            nc.vector.tensor_copy(self.cc[:, :, 0:T], keep["cum"][:, :, t]).then_inc(self.centred, 1)
        else:
            mid = keep["mid"][:, :, bass.ds(c, 1)].broadcast_to([P, FT, T])
            nc.vector.tensor_tensor(self.cc[:, :, 0:T], keep["cum"][:, :, t], mid, ALU.subtract).then_inc(self.centred, 1)
        dve.wait_ge(self.exped, 2 * c + 1)
        nc.vector.tensor_tensor(self.ar[:, :, 1, 0:T], pb[:, R0:R0 + FT, t], self.e1[:, :, 0:T], ALU.mult)
        if self.sample:
            g = lambda a: a.rearrange("p f (b t) -> p f b t", t=NT)
            for f in range(FT):
                a, k, e = (g(x)[:, f] for x in (self.ar[:, :, 0, 0:T], keep["kk"][:, :, t], self.e1[:, :, 0:T]))
                nc.vector.tensor_tensor(a[:, :, 1:NT], k[:, :, 1:NT], e[:, :, 0:NT - 1], ALU.mult)
                nc.vector.tensor_copy(a[:, :, 0:1], k[:, :, 0:1])
        else:
            first = keep["mexp"][:, 2, :, bass.ds(c, 1)]
            nc.vector.tensor_tensor(self.ar[:, :, 0, 1:T], keep["kk"][:, :, bass.ds(c * CH + 1, CH - 1)],
                                    self.e1[:, :, 0:T - 1], ALU.mult)
            nc.vector.tensor_tensor(self.ar[:, :, 0, 0:1], keep["kk"][:, :, bass.ds(c * CH, 1)], first, ALU.mult)
        dve.wait_ge(self.exped, 2 * c + 2)
        nc.vector.tensor_tensor(self.bf[:, :, 0:T], keep["kka"][:, :, t], self.e3[:, :, 0:T], ALU.mult)
        nc.vector.tensor_tensor(self.kf[:, :, 0:T], pb[:, K0:K0 + FT, t], self.e3[:, :, 0:T], ALU.mult).then_inc(self.ready, 1)

    def pe_gram(self, pe, c, n):
        nc, T, gh = self.nc, self.T, self.gram_heads
        if n == 0:
            pe.wait_ge(self.ready, c + 1)
            pe.wait_ge(self.done, c + 1)
        if n == 2:
            pe.wait_ge(self.v_copied, c + 1)
        if n >= self.BANKS:
            pe.wait_ge(self.ev, c * self.rounds + n - self.BANKS + 1)
        bank = self.bank[n % 2]
        if n < self.TR:
            src = (self.bf, self.kf, self.vf)[n]
            for f in range(FT):
                mm = nc.tensor.transpose(bank[0:T, f * P:f * P + P], src[:, f, 0:T], self.C["ident"])
        else:
            g = n - self.TR
            src = self.bf if g < NH // gh else self.kf
            for j in range(gh):
                h = self.heads(g)[j]
                po, f = h % 2 * DH, h // 2
                out = bank[0:T, j * 2 * T:j * 2 * T + 2 * T]
                mm = nc.tensor.matmul(out.rearrange("p (a t) -> p a t", a=2), src[po:po + DH, f, 0:T],
                                      self.ar[po:po + DH, f, :, 0:T], start=True, stop=True)
        mm.then_inc(self.mm, 1)

    def dve_gram(self, dve, c, n):
        nc, T, gh = self.nc, self.T, self.gram_heads
        mask = self.C["lows"][0:T, 0:2 * T] if self.sample else self.C["low"]
        mask = mask[:, None, :].broadcast_to([T, gh, 2 * T])
        dve.wait_ge(self.mm, c * self.rounds + n + 1)
        bank = self.bank[n % 2]
        if n < self.TR:
            nc.vector.tensor_copy((self.bt, self.kt, self.vt)[n][0:T], bank[0:T, 0:512]).then_inc(self.ev, 1)
        else:
            g = n - self.TR
            dst, h = (self.ntg if g < NH // gh else self.nkg), self.heads(g)
            nc.vector.tensor_tensor(dst[0:T, h[0]:h[-1] + 1:2, 0:2 * T], bank[0:T].rearrange("p (h m) -> p h m", h=gh),
                                    mask, ALU.mult).then_inc(self.ev, 1)

    def view(self, buf, bt):
        return buf[0:self.T, 4 * bt:4 * bt + 4, 0:self.T]

    def pe_level(self, pe, c, level, bt):
        nc, T, L, ident = self.nc, self.T, self.levels, self.C["ident"]
        out = self.bank[bt].rearrange("p (h m) -> p h m", h=4)
        if level == 0 and bt == 0:
            pe.wait_ge(self.ev, (c + 1) * self.rounds)
        if level:
            pe.wait_ge(self.x_ev[bt], c * (L - 1) + level)
        for j in range(4):
            h = 4 * bt + j
            if level == 0:
                mm = nc.tensor.transpose(out[0:T, j, 0:T], self.ntg[0:T, h, 0:T], ident[0:T, 0:T])
            else:
                mm = nc.tensor.matmul(out[0:T, j, 0:T], self.ntg[0:T, h, 0:T], self.x[0:T, h, 0:T], start=True, stop=True)
        mm.then_inc(self.t_mm[bt], 1)

    def pe_level_xt(self, pe, c, level, bt):
        nc, T, L, ident = self.nc, self.T, self.levels, self.C["ident"]
        out = self.bank[bt].rearrange("p (h m) -> p h m", h=4)
        pe.wait_ge(self.t_ev[bt], c * L + level + 1)
        for j in range(4):
            h = 4 * bt + j
            if level == 0:
                mm = nc.tensor.transpose(out[0:T, j, 0:T], self.tt[0:T, h, 0:T], ident[0:T, 0:T])
            else:
                mm = nc.tensor.matmul(out[0:T, j, 0:T], self.tt[0:T, h, 0:T], self.xt[0:T, h, 0:T], start=True, stop=True)
        mm.then_inc(self.xt_mm[bt], 1)

    def pe_level_x(self, pe, c, level, bt):
        nc, T, L = self.nc, self.T, self.levels
        out = self.bank[bt].rearrange("p (h m) -> p h m", h=4)
        pe.wait_ge(self.xt_ev[bt], c * L + level + 1)
        for j in range(4):
            mm = nc.tensor.transpose(out[0:T, j, 0:T], self.xt[0:T, 4 * bt + j, 0:T], self.C["ident"][0:T, 0:T])
        mm.then_inc(self.x_mm[bt], 1)

    def dve_t(self, dve, c, level, bt):
        T = self.T
        mask = self.C["lev"][0:T, level * P:level * P + T][:, None, :].broadcast_to([T, 4, T])
        src = self.bank[bt].rearrange("p (h m) -> p h m", h=4)[0:T, :, 0:T]
        dve.wait_ge(self.t_mm[bt], c * self.levels + level + 1)
        self.nc.vector.tensor_tensor(self.view(self.tt, bt), src, mask, ALU.mult).then_inc(self.t_ev[bt], 1)

    def dve_xt(self, dve, c, level, bt):
        T, L = self.T, self.levels
        src = self.bank[bt].rearrange("p (h m) -> p h m", h=4)[0:T, :, 0:T]
        dve.wait_ge(self.xt_mm[bt], c * L + level + 1)
        if level:
            dve.wait_ge(self.xt_ev[bt], c * L + level)
            add = self.view(self.xt, bt)
        else:
            add = self.C["ident"][0:T, None, 0:T].broadcast_to([T, 4, T])
        self.nc.vector.tensor_tensor(self.view(self.xt, bt), src, add, ALU.add).then_inc(self.xt_ev[bt], 1)

    def act_x(self, act, c, level, bt):
        src = self.bank[bt].rearrange("p (h m) -> p h m", h=4)[0:self.T, :, 0:self.T]
        act.wait_ge(self.x_mm[bt], c * (self.levels - 1) + level + 1)
        self.nc.scalar.activation(self.view(self.x, bt), src, ACT.Copy).then_inc(self.x_ev[bt], 1)


    def pe_r(self, pe, c):
        nc, L = self.nc, self.levels
        for bt in range(2):
            pe.wait_ge(self.xt_ev[bt], (c + 1) * L)
        pe.wait_ge(self.sm, c + 1)
        for h in range(NH):
            po, f, hs = h % 2 * DH, h // 2, slice(h * DH, h * DH + DH)
            out = self.bank[h % 2][:, f * DH:f * DH + DH]
            nc.tensor.matmul(out, self.ar[po:po + DH, f, 0], self.s_mid[po:po + DH, f], start=True, stop=False)
            mm = nc.tensor.matmul(out, self.nkg[:, h, 0:CH], self.vt[:, hs], start=False, stop=True)
        mm.then_inc(self.r_mm, 1)

    def pe_u(self, pe, c):
        nc, b0 = self.nc, self.bank[0]
        pe.wait_ge(self.r_ev, 2 * c + 2)
        for h in range(NH):
            hs = slice(h * DH, h * DH + DH)
            mm = nc.tensor.matmul(b0[:, hs], self.xt[:, h], self.rs[:, hs], start=True, stop=True)
        mm.then_inc(self.u_mm, 1)

    def pe_y(self, pe, c):
        nc, b1 = self.nc, self.bank[1]
        pe.wait_ge(self.u_ev, c + 1)
        for h in range(NH):
            po, f, hs = h % 2 * DH, h // 2, slice(h * DH, h * DH + DH)
            out = b1[po:po + DH, f * CH:f * CH + CH]
            nc.tensor.matmul(out, self.us[:, hs], self.ntg[:, h, CH:2 * CH], start=True, stop=False)
            nc.tensor.matmul(out, self.vt[:, hs], self.nkg[:, h, CH:2 * CH], start=False, stop=False)
            mm = nc.tensor.matmul(out, self.s_mid[po:po + DH, f], self.ar[po:po + DH, f, 1], start=False, stop=True)
        mm.then_inc(self.y_mm, 1)

    def pe_d(self, pe, c):
        nc, b0 = self.nc, self.bank[0]
        for h in range(NH):
            po, f, hs = h % 2 * DH, h // 2, slice(h * DH, h * DH + DH)
            out = b0[po:po + DH, f * DH:f * DH + DH]
            nc.tensor.matmul(out, self.bt[:, hs], self.us[:, hs], start=True, stop=False)
            mm = nc.tensor.matmul(out, self.kt[:, hs], self.vt[:, hs], start=False, stop=True)
        mm.then_inc(self.d_mm, 1)

    def act_r(self, act, c):
        act.wait_ge(self.r_mm, c + 1)
        for u in range(2):
            dst = self.rs.rearrange("p (f u v) -> p f u v", f=FT, u=2)[:, :, u]
            src = self.bank[u][:, 0:FT * DH].rearrange("p (f v) -> p f v", f=FT)
            self.nc.scalar.activation(dst, src, ACT.Copy).then_inc(self.r_ev, 1)

    def dve_state_in(self, dve, c):
        e = self.keep["mexp"][:, 0, :, bass.ds(c, 1)].broadcast_to([P, FT, DH])
        dve.wait_ge(self.done, c + 1)
        self.nc.vector.tensor_tensor(self.s_mid[:], self.s[:], e, ALU.mult).then_inc(self.sm, 1)

    def dve_u(self, dve, c):
        dve.wait_ge(self.u_mm, c + 1)
        self.nc.vector.tensor_copy(self.us[:], self.bank[0]).then_inc(self.u_ev, 1)

    def dve_yd(self, dve, c):
        nc = self.nc
        dve.wait_ge(self.y_mm, c + 1)
        nc.vector.tensor_scalar(self.pb[:, R0:R0 + FT, self.cols(c)], self.bank[1].rearrange("p (f t) -> p f t", f=FT),
                                1.0, None, ALU.mult)
        dve.wait_ge(self.d_mm, c + 1)
        src = self.bank[0][:, 0:FT * DH].rearrange("p (f v) -> p f v", f=FT)
        e = self.keep["mexp"][:, 1, :, bass.ds(c, 1)].broadcast_to([P, FT, DH])
        nc.vector.tensor_tensor(self.s[:], src, self.s_mid[:], ALU.add).then_inc(self.d_part, 1)
        dve.wait_ge(self.d_part, c + 1)
        nc.vector.tensor_tensor(self.s[:], self.s[:], e, ALU.mult).then_inc(self.done, 1)


    def pe_sample(self, pe):
        nc, T, L = self.nc, self.T, self.levels
        b0, b1 = self.bank
        for bt in range(2):
            pe.wait_ge(self.xt_ev[bt], L)
        pe.wait_ge(self.s_loaded, 16)
        view = b0.rearrange("p (f a t) -> p f a t", f=FT, a=2)
        for f in range(FT):
            for b in range(NB):
                for po in (0, DH):
                    mm = nc.tensor.matmul(view[po:po + DH, f, :, NT * b:NT * b + NT], self.s0[po:po + DH, f, b],
                                          self.ar[po:po + DH, f, :, NT * b:NT * b + NT], start=True, stop=True)
        mm.then_inc(self.sm, 1)
        pe.wait_ge(self.d_part, 1)
        for f in range(FT):
            for u in range(2):
                h = 2 * f + u
                hs = slice(h * DH, h * DH + DH)
                nc.tensor.matmul(b1[0:T, hs], self.sa[:, f, 0], self.C["ident"][:, u * DH:u * DH + DH], start=True, stop=False)
                mm = nc.tensor.matmul(b1[0:T, hs], self.nkg[0:T, h, 0:T], self.vt[0:T, hs], start=False, stop=True)
        mm.then_inc(self.r_mm, 1)
        pe.wait_ge(self.r_ev, 1)
        for h in range(NH):
            hs = slice(h * DH, h * DH + DH)
            mm = nc.tensor.matmul(b0[0:T, hs], self.xt[0:T, h, 0:T], self.rs[0:T, hs], start=True, stop=True)
        mm.then_inc(self.u_mm, 1)
        pe.wait_ge(self.u_ev, 1)
        for h in range(NH):
            po, f, hs = h % 2 * DH, h // 2, slice(h * DH, h * DH + DH)
            out = b1[po:po + DH, f * T:f * T + T]
            nc.tensor.matmul(out, self.us[0:T, hs], self.ntg[0:T, h, T:2 * T], start=True, stop=False)
            mm = nc.tensor.matmul(out, self.vt[0:T, hs], self.nkg[0:T, h, T:2 * T], start=False, stop=True)
        mm.then_inc(self.y_mm, 1)
        for f in range(FT):
            pe.wait_ge(self.x_part, f + 1)
            pe.wait_ge(self.v_part, f + 1)
            if f >= 2:
                pe.wait_ge(self.done, f)
            if f == 1:
                pe.wait_ge(self.y_taken, 1)
            for po in (0, DH):
                h = 2 * f + po // DH
                hs = slice(h * DH, h * DH + DH)
                ux, vx = self.ux[0:T, f % 2, po // DH], self.vx[0:T, f % 2, po // DH]
                nc.tensor.matmul(self.bank[f % 2][po:po + DH], self.bt[0:T, hs], ux, start=True, stop=False)
                mm = nc.tensor.matmul(self.bank[f % 2][po:po + DH], self.kt[0:T, hs], vx, start=False, stop=True)
            mm.then_inc(self.d_mm, 1)

    def act_sample(self, act):
        act.wait_ge(self.r_mm, 1)
        self.nc.scalar.activation(self.rs[0:self.T], self.bank[1][0:self.T], ACT.Copy).then_inc(self.r_ev, 1)

    def dve_sample(self, dve):
        nc, T = self.nc, self.T
        b0, b1 = self.bank
        dve.wait_ge(self.sm, 1)
        nc.vector.tensor_copy(self.sa[:], b0.rearrange("p (f a t) -> p f a t", f=FT, a=2)).then_inc(self.d_part, 1)
        dve.wait_ge(self.u_mm, 1)
        nc.vector.tensor_copy(self.us[0:T], b0[0:T]).then_inc(self.u_ev, 1)
        dve.wait_ge(self.u_ev, 1)
        dve.wait_ge(self.y_mm, 1)
        nc.vector.tensor_tensor(self.pb[:, R0:R0 + FT, SEQ:TOK], b1[:, 0:FT * T].rearrange("p (f t) -> p f t", f=FT),
                                self.sa[:, :, 1], ALU.add).then_inc(self.y_taken, 1)
        bm = self.C["bmask"][0:T, :, None].broadcast_to([T, NB, DH])
        for f in range(FT):
            if f >= 2:
                dve.wait_ge(self.d_mm, f - 1)
            for u in range(2):
                h = 2 * f + u
                v = self.us[0:T, h * DH:h * DH + DH][:, None, :].broadcast_to([T, NB, DH])
                last = nc.vector.tensor_tensor(self.ux[0:T, f % 2, u].rearrange("p (b v) -> p b v", b=NB), v, bm, ALU.mult)
            last.then_inc(self.x_part, 1)
            if f >= 1:
                self.dve_state_out(dve, f - 1)
        self.dve_state_out(dve, FT - 1)

    def pool_sample(self, pool):
        T, bm = self.T, self.C["bmask"][0:self.T, :, None].broadcast_to([self.T, NB, DH])
        pool.wait_ge(self.ev, 3)
        for f in range(FT):
            if f >= 2:
                pool.wait_ge(self.d_mm, f - 1)
            for u in range(2):
                h = 2 * f + u
                v = self.vt[0:T, h * DH:h * DH + DH][:, None, :].broadcast_to([T, NB, DH])
                last = self.nc.gpsimd.tensor_tensor(self.vx[0:T, f % 2, u].rearrange("p (b v) -> p b v", b=NB), v, bm, ALU.mult)
            last.then_inc(self.v_part, 1)

    def dve_state_out(self, dve, f):
        nc = self.nc
        dve.wait_ge(self.d_mm, f + 1)
        src = self.bank[f % 2].rearrange("p (b v) -> p b v", b=NB)
        nc.vector.tensor_tensor(self.s0[:, f], src, self.s0[:, f], ALU.add).then_inc(self.s_added, 1)
        dve.wait_ge(self.s_added, f + 1)
        e = self.e1[:, f, NT - 1:NB * NT:NT][:, :, None].broadcast_to([P, NB, DH])
        nc.vector.tensor_tensor(self.s0[:, f], self.s0[:, f], e, ALU.mult).then_inc(self.done, 1)


class FoxPrompt:

    UNITS = [(u, i) for i in range(SEQ // P) for u in range(2)]

    def __init__(self, ctx, sems, nc, pb, C, keep, banks):
        self.nc, self.pb, self.C, self.keep = nc, pb, C, keep
        sb = lambda n, s, d=F32: ctx.enter_context(nc.sbuf_tensor(n, s, d))
        sem = sems
        self.b_s, self.b_t, self.b_o = banks
        self.q, self.k, self.v = sb("fp_q", [P, SEQ], F32), sb("fp_k", [P, SEQ]), sb("fp_v", [P, SEQ])
        self.sel, self.bias, self.vt = sb("fp_sel", [NH, 2, P]), sb("fp_bias", [P, 2, SEQ]), sb("fp_vt", [P, 4, P])
        self.s, self.p, self.pt = sb("fp_s", [P, 2, SEQ]), sb("fp_p", [P, 2, SEQ]), sb("fp_pt", [P, 2, 4, P])
        self.nm, self.rsum = sb("fp_nm", [P, 8]), sb("fp_rsum", [P, 8])
        self.copied, self.masked, self.bias_mm, self.bias_ev = sem("fp_copied"), sem("fp_masked"), sem("fp_bias_mm"), sem("fp_bias_ev")
        self.causal, self.vt_mm, self.vt_ev = sem("fp_causal"), sem("fp_vt_mm"), sem("fp_vt_ev")
        self.s_mm, self.s_ev, self.maxed, self.exped = sem("fp_s_mm"), sem("fp_s_ev"), sem("fp_maxed"), sem("fp_exped")
        self.inverted, self.p_done, self.t_mm, self.t_ev, self.o_mm, self.o_ev = (
            sem("fp_inverted"), sem("fp_p_done"), sem("fp_t_mm"), sem("fp_t_ev"), sem("fp_o_mm"), sem("fp_o_ev"))

    def seed(self, dve):
        dve.nop().then_inc(self.s_ev, 1)
        dve.nop().then_inc(self.o_ev, 1)
        dve.nop().then_inc(self.o_mm, 1)

    def pool(self, pool, c):
        pool.wait_ge(self.o_mm, 8 * c + 1)
        for dst, a in ((self.k, FK0), (self.q, FQ0), (self.v, FV0)):
            src = self.pb[:, a:a + FT][:, bass.ds(c, 1), 0:SEQ].rearrange("p a n -> p (a n)")
            self.nc.gpsimd.tensor_copy(dst[:], src).then_inc(self.copied, 1)

    def pe_in(self, pe, c):
        nc = self.nc
        pe.wait_ge(self.copied, 3 * c + 3)
        for u in range(2):
            pe.wait_ge(self.masked, 2 * c + u + 1)
            if u == 0:
                pe.wait_ge(self.s_ev, 8 * c + 1)
            else:
                pe.wait_ge(self.bias_ev, 2 * c + 1)
            nc.tensor.matmul(self.b_s[:], self.sel[:, u], self.pb[0:NH, FF0, 0:SEQ], start=True, stop=True).then_inc(self.bias_mm, 1)
        for j in range(4):
            mm = nc.tensor.transpose(self.b_t[:, j * P:j * P + P], self.v[:, j * P:j * P + P], self.C["ident"])
        mm.then_inc(self.vt_mm, 1)

    def pe_turn(self, pe, c, n):
        nc, (u, i) = self.nc, self.UNITS[n]
        pe.wait_ge(self.p_done, 8 * c + n + 1)
        if n:
            pe.wait_ge(self.t_ev, 8 * c + n)
        for j in range(i + 1):
            mm = nc.tensor.transpose(self.b_t[:, j * P:j * P + P], self.p[:, n % 2, j * P:j * P + P], self.C["ident"])
        mm.then_inc(self.t_mm, 1)

    def pe_values(self, pe, c, n):
        nc, (u, i) = self.nc, self.UNITS[n]
        pe.wait_ge(self.t_ev, 8 * c + n + 1)
        if n == 0:
            pe.wait_ge(self.o_ev, c + 1)
        po = u * DH
        for j in range(i + 1):
            mm = nc.tensor.matmul(self.b_o[po:po + DH, i * P:i * P + P], self.vt[:, j, po:po + DH],
                                  self.pt[:, n % 2, j], start=j == 0, stop=j == i)
        mm.then_inc(self.o_mm, 1)

    def pe_scores(self, pe, c, n):
        u, i = self.UNITS[n]
        if n == 0:
            pe.wait_ge(self.bias_ev, 2 * c + 2)
            pe.wait_ge(self.vt_ev, c + 1)
        if n:
            pe.wait_ge(self.s_ev, 8 * c + n + 1)
        r = slice(u * DH, u * DH + DH)
        self.nc.tensor.matmul(self.b_s[:, 0:i * P + P], self.q[r, i * P:i * P + P], self.k[r, 0:i * P + P],
                              start=True, stop=True).then_inc(self.s_mm, 1)

    def dve_in(self, dve, c):
        nc = self.nc
        for u in range(2):
            nc.vector.tensor_scalar(self.sel[:, u], self.C["minus"][0:NH], self.C["ident"][0:NH, bass.ds(2 * c + u, 1)],
                                    None, ALU.mult).then_inc(self.masked, 1)

    def dve_normalise(self, dve, c, n):
        nc, (u, i) = self.nc, self.UNITS[n]
        w = i * P + P
        dve.wait_ge(self.exped, 8 * c + n + 1)
        nc.vector.reciprocal(self.rsum[:, n:n + 1], self.rsum[:, n:n + 1]).then_inc(self.inverted, 1)
        dve.wait_ge(self.inverted, 8 * c + n + 1)
        nc.vector.tensor_scalar(self.p[:, n % 2, 0:w], self.p[:, n % 2, 0:w], self.rsum[:, n:n + 1], None,
                                ALU.mult).then_inc(self.p_done, 1)

    def dve_scores(self, dve, c, n):
        nc = self.nc
        u, i = self.UNITS[n]
        a, w = i * P, i * P + P
        dve.wait_ge(self.s_mm, 8 * c + n + 1)
        nc.vector.tensor_tensor(self.s[:, n % 2, 0:w], self.b_s[:, 0:w], self.bias[:, u, 0:w], ALU.add).then_inc(self.s_ev, 1)
        dve.wait_ge(self.s_ev, 8 * c + n + 2)
        nc.vector.tensor_tensor(self.s[:, n % 2, a:w], self.s[:, n % 2, a:w], self.C["causal"], ALU.add).then_inc(self.causal, 1)
        dve.wait_ge(self.causal, 8 * c + n + 1)
        nc.vector.tensor_reduce(self.nm[:, n:n + 1], self.s[:, n % 2, 0:w], AX.X, ALU.max, negate=True).then_inc(self.maxed, 1)

    def act_in(self, act, c):
        nc = self.nc
        for u in range(2):
            act.wait_ge(self.bias_mm, 2 * c + u + 1)
            nc.scalar.activation(self.bias[:, u], self.b_s[:], ACT.Copy).then_inc(self.bias_ev, 1)
        act.wait_ge(self.vt_mm, c + 1)
        nc.scalar.activation(self.vt[:].rearrange("p j n -> p (j n)"), self.b_t[:], ACT.Copy).then_inc(self.vt_ev, 1)

    def act_exp(self, act, c, n):
        nc, (u, i) = self.nc, self.UNITS[n]
        w = i * P + P
        act.wait_ge(self.maxed, 8 * c + n + 1)
        if n >= 2:
            act.wait_ge(self.t_mm, 8 * c + n - 1)
        nc.scalar.activation(self.p[:, n % 2, 0:w], self.s[:, n % 2, 0:w], ACT.Exp, bias=self.nm[:, n:n + 1],
                             accum_out=self.rsum[:, n:n + 1]).then_inc(self.exped, 1)

    def act_out(self, act, c):
        nc = self.nc
        act.wait_ge(self.o_mm, 8 * c + 9)
        dst = self.pb[:, FQ0:FQ0 + FT][:, bass.ds(c, 1), 0:SEQ]
        nc.scalar.activation(dst, self.b_o[:][:, None, :], ACT.Copy).then_inc(self.o_ev, 1)

    def act_turned(self, act, c, n):
        u, i = self.UNITS[n]
        act.wait_ge(self.t_mm, 8 * c + n + 1)
        self.nc.scalar.activation(self.pt[:, n % 2, 0:i + 1].rearrange("p j n -> p (j n)"), self.b_t[:, 0:i * P + P],
                                  ACT.Copy).then_inc(self.t_ev, 1)


class FoxSample:

    RING = 4

    def __init__(self, ctx, sems, nc, pb, C, keep, scores, banks, dram):
        self.nc, self.pb, self.C, self.keep, self.dram = nc, pb, C, keep, dram
        sb = lambda n, s, d=F32: ctx.enter_context(nc.sbuf_tensor(n, s, d))
        sem = sems
        self.ring, self.b_o = banks[0:2], banks[2]
        self.table = sb("fs_table", [1, NB * PAGES], I32)
        self.kr, self.vr = sb("fs_keys", [P, self.RING, FT * PAGE]), sb("fs_values", [P, self.RING, FT * P])
        self.s, self.pt = scores, sb("fs_pt", [P, PAGES + 1, P])
        self.o = self.pt[:, 0:FT].rearrange("p j n -> p (j n)")
        self.q = sb("fs_q", [P, FT * (P + 16)])
        self.tops, self.nm = sb("fs_tops", [P, 5]), sb("fs_nm", [P, 1])
        self.parts, self.rsum = sb("fs_parts", [P, 5]), sb("fs_rsum", [P, 1])
        self.k_in = [sem(f"fs_k_in{s}") for s in range(self.RING)]
        self.v_in = [sem(f"fs_v_in{s}") for s in range(self.RING)]
        self.t_in, self.bias_in, self.k_used, self.v_used = sem("fs_table_in"), sem("fs_bias_in"), sem("fs_k_used"), sem("fs_v_used")
        self.q_in, self.s_mm, self.s_ev, self.maxed, self.exped = sem("fs_q_in"), sem("fs_s_mm"), sem("fs_s_ev"), sem("fs_maxed"), sem("fs_exped")
        self.topped, self.summed = sem("fs_topped"), sem("fs_summed")
        self.t_mm, self.t_ev, self.inverted = sem("fs_t_mm"), sem("fs_t_ev"), sem("fs_inverted")
        self.o_mm, self.o_ev, self.ot_mm, self.done, self.zeroed = sem("fs_o_mm"), sem("fs_o_ev"), sem("fs_ot_mm"), sem("fs_done"), sem("fs_zeroed")

    def seed(self, pool):
        pool.nop().then_inc(self.k_used, self.RING)
        pool.nop().then_inc(self.v_used, self.RING)
        pool.nop().then_inc(self.t_mm, 1)
        self.nc.gpsimd.memset(self.q[:], 0.0).then_inc(self.zeroed, 1)

    def seed_done(self, dve):
        dve.nop().then_inc(self.done, 1)

    def load_table(self, sp):
        sp.dma_start(self.table[:], self.dram["table"]).then_inc(self.t_in, 16)
        sp.wait_ge(self.t_in, 16)

    def load(self, sp, c):
        sp.wait_ge(self.t_mm, 5 * c + 1)
        later = self.dram["later"][bass.ds(2 * NH * c, 2 * NH)]
        sp.dma_start(self.s[:, 0:PAST], later[:, None, :].broadcast_to([2 * NH, NT, PAST])).then_inc(self.bias_in, 16)
        for buf, used, landed, src in ((self.kr, self.k_used, self.k_in, "keys"), (self.vr, self.v_used, self.v_in, "values")):
            with sp.Fori(0, 2 * PAGES // self.RING) as i:
                for n in range(self.RING):
                    j, k = n // 2, n % 2
                    at = 2 * PAGES * c + PAGES * k + PAGES - 1 - j - self.RING // 2 * i
                    page = sp.value_load(self.table[0:1, bass.ds(at, 1)], min_val=0, max_val=NPOOL - 1)
                    sp.wait_ge(used, 2 * PAGES * c + self.RING * i + n + 1)
                    sp.dma_start(buf[:, n], self.dram[src][bass.ds(page, 1)].rearrange("a p n -> p (a n)"))\
                      .then_inc(landed[n], 16)

    def landed(self, c, n):
        return 16 * (2 * PAGES // self.RING * c + n // self.RING + 1)

    def act_queries(self, act, c):
        act.wait_ge(self.k_used, 2 * PAGES * c + self.RING)
        for u in range(2):
            r = slice(64 * u, 64 * u + 64)
            src = self.pb[r, FQ0:FQ0 + FT, bass.ds(SEQ + 2 * NT * c, 2 * NT)].rearrange("p i (k t) -> p i k t", k=2)
            blocks = self.q[r].rearrange("p (i m) -> p i m", i=FT)[:, :, NT * u:NT * u + P]
            dst = blocks.rearrange("p i (k m) -> p i k m", k=2)[:, :, :, 0:NT]
            self.nc.scalar.activation(dst, src, ACT.Copy).then_inc(self.q_in, 1)

    def queries(self, i, k):
        return self.q[:, i * P + 64 * k:i * P + 64 * k + 64]

    def pe_new(self, pe, c):
        pe.wait_ge(self.q_in, 2 * c + 2)
        for k in range(2):
            for i in range(FT):
                mm = self.nc.tensor.matmul(self.ring[0][64 * k:64 * k + 64, 0:64], self.queries(i, k), self.pb[:, FK0 + i, SEQ:TOK],
                                           start=i == 0, stop=i == FT - 1)
        mm.then_inc(self.s_mm, 1)

    def pe_keys(self, pe, c, j, k):
        n, g = 2 * j + k, j // 4 + 1
        if n % 8 == 0 and g >= 2:
            pe.wait_ge(self.s_ev, 5 * c + g - 1)
        pe.wait_ge(self.k_in[n % self.RING], self.landed(c, n))
        out = self.ring[g % 2][64 * k:64 * k + 64, j % 4 * PAGE:j % 4 * PAGE + PAGE]
        for i in range(FT):
            mm = self.nc.tensor.matmul(out, self.queries(i, k), self.kr[:, n % self.RING, i * PAGE:i * PAGE + PAGE],
                                       start=i == 0, stop=i == FT - 1)
        mm.then_inc(self.k_used, 1)

    def pages(self, q):
        return range(4 * q, 4 * q + 4) if q < 3 else (12, 13, 14) if q == 3 else (15,)

    def pe_turn(self, pe, c, q):
        bank = self.ring[(5 + q) % 2]
        pe.wait_ge(self.exped, 5 * c + q + 1)
        if q >= 2:
            pe.wait_ge(self.t_ev, 5 * c + q - 1)
        for m, j in enumerate(self.pages(q)):
            mm = self.nc.tensor.transpose(bank[:, m * P:m * P + P], self.s[:, j * PAGE:j * PAGE + PAGE], self.C["ident"])
        if q == 4:
            mm = self.nc.tensor.transpose(bank[0:64, P:2 * P], self.s[:, PAST:PAST + 64], self.C["ident"])
        mm.then_inc(self.t_mm, 1)

    def pe_values(self, pe, c, j, k):
        n = 2 * j + k
        if n == 0:
            pe.wait_ge(self.t_ev, 5 * c + 5)
            pe.wait_ge(self.done, c + 1)
        pe.wait_ge(self.v_in[n % self.RING], self.landed(c, n))
        self.nc.tensor.matmul(self.b_o[64 * k:64 * k + 64], self.pt[:, j, 64 * k:64 * k + 64], self.vr[:, n % self.RING],
                              start=j == 0, stop=False).then_inc(self.v_used, 1)

    def pe_new_values(self, pe):
        for k in range(2):
            mm = self.nc.tensor.matmul(self.b_o[64 * k:64 * k + 64], self.pt[0:64, PAGES, 64 * k:64 * k + 64],
                                       self.keep["vn"][:], start=False, stop=True)
        mm.then_inc(self.o_mm, 1)

    def pe_out(self, pe, c):
        pe.wait_ge(self.o_ev, c + 1)
        for i in range(FT):
            mm = self.nc.tensor.transpose(self.b_o[:, i * P:i * P + P], self.o[:, i * P:i * P + P], self.C["ident"])
        mm.then_inc(self.ot_mm, 1)

    def dve_scores(self, dve, c, g):
        bank = self.ring[g % 2]
        if g == 0:
            dve.wait_ge(self.s_mm, c + 1)
            new = self.keep["newb"][:, bass.ds(c, 1)].rearrange("p a n -> p (a n)")
            self.nc.vector.tensor_tensor(self.s[:, PAST:PAST + 64], bank[:, 0:64], new, ALU.add).then_inc(self.s_ev, 1)
        else:
            dve.wait_ge(self.k_used, 2 * PAGES * c + self.RING + 8 * g)
            if g == 1:
                dve.wait_ge(self.bias_in, 16 * c + 16)
            s = self.s[:, 512 * (g - 1):512 * g]
            self.nc.vector.tensor_tensor(s, bank[:], s, ALU.add).then_inc(self.s_ev, 1)
        dve.wait_ge(self.s_ev, 5 * c + g + 1)
        s = self.s[:, PAST:PAST + 64] if g == 0 else self.s[:, 512 * (g - 1):512 * g]
        self.nc.vector.tensor_reduce(self.tops[:, g:g + 1], s, AX.X, ALU.max).then_inc(self.topped, 1)

    def dve_max(self, dve, c):
        dve.wait_ge(self.topped, 5 * c + 5)
        self.nc.vector.tensor_reduce(self.nm[:], self.tops[:], AX.X, ALU.max, negate=True).then_inc(self.maxed, 1)

    def columns(self, q):
        pages = self.pages(q)
        return slice(pages[0] * PAGE, PAST + 64 if q == 4 else pages[-1] * PAGE + PAGE)

    def act_exp(self, act, c):
        act.wait_ge(self.maxed, c + 1)
        for q in range(5):
            s = self.s[:, self.columns(q)]
            self.nc.scalar.activation(s, s, ACT.Exp, bias=self.nm[:], accum_out=self.parts[:, q:q + 1]).then_inc(self.exped, 1)

    def act_turned(self, act, c, q):
        nc, bank, pages = self.nc, self.ring[(5 + q) % 2], self.pages(q)
        act.wait_ge(self.t_mm, 5 * c + q + 2)
        w = len(pages) * P
        if q == 4:
            nc.scalar.activation(self.pt[0:64, PAGES], bank[0:64, P:2 * P], ACT.Copy)
        dst = self.pt[:, pages[0]:pages[-1] + 1].rearrange("p j n -> p (j n)")
        nc.scalar.activation(dst, bank[:, 0:w], ACT.Copy).then_inc(self.t_ev, 1)

    def dve_inverse(self, dve, c):
        dve.wait_ge(self.exped, 5 * c + 5)
        self.nc.vector.tensor_reduce(self.rsum[:], self.parts[:], AX.X, ALU.add).then_inc(self.summed, 1)
        dve.wait_ge(self.summed, c + 1)
        self.nc.vector.reciprocal(self.rsum[:], self.rsum[:]).then_inc(self.inverted, 1)

    def dve_normalise(self, dve, c):
        dve.wait_ge(self.inverted, c + 1)
        dve.wait_ge(self.o_mm, c + 1)
        self.nc.vector.tensor_scalar(self.o, self.b_o[:], self.rsum[:], None, ALU.mult).then_inc(self.o_ev, 1)

    def dve_out(self, dve, c):
        dve.wait_ge(self.ot_mm, c + 1)
        for u in range(2):
            r = slice(64 * u, 64 * u + 64)
            for i in range(FT):
                src = self.b_o[r, i * P:i * P + P].rearrange("p (k n) -> p k n", k=2)[:, :, 16 * i + NT * u:16 * i + NT * u + NT]
                dst = self.pb[r, FQ0 + i, bass.ds(SEQ + 2 * NT * c, 2 * NT)].rearrange("p (k t) -> p k t", k=2)
                last = self.nc.vector.tensor_scalar(dst, src, 1.0, None, ALU.mult)
        last.then_inc(self.done, 1)


def turn_steps():
    rw = [("operands", None, 4.0)] + [("gram", n, 0.9) for n in range(3 + 8)]
    for level in range(7):
        for kind, time in (("t", 0.8), ("xt", 0.8), ("x", 1.0)):
            if kind != "x" or level < 6:
                rw += [(kind, (level, bt), time) for bt in range(2)]
    rw += [("r", None, 2.6), ("u", None, 0.9), ("yd", None, 7.0)]
    units = FoxPrompt.UNITS
    fp = [("fp_copy", None, 8.0), ("fp_in", None, 0.5), ("scores", 0, 0.6), ("exp", 0, 0.5)]
    for n in range(8):
        w = units[n][1] + 1
        if n < 7:
            fp += [("scores", n + 1, 0.2 * w)]
        fp += [("normalise", n, 0.2)]
        if n < 7:
            fp += [("exp", n + 1, 0.2)]
        fp += [("turn", n, 0.2 * w)]
        fp += [("values", n, 0.3 * w)]
    fp += [("fp_out", None, 2.0)]
    fs = [("fs_in", None, 0.5), ("fs_new", None, 0.5), ("fs_scores", 0, 0.1)]
    for j in range(PAGES):
        fs += [("keys", (j, k), 0.85) for k in range(2)]
        if j % 4 == 3:
            fs += [("fs_scores", j // 4 + 1, 0.1)]
    fs += [("fs_max", None, 3.0), ("fs_exp", None, 3.0)] + [("fs_turn", q, 0.6) for q in range(5)]
    fs += [("cached", (j, k), 0.85) for j in range(PAGES) for k in range(2)]
    fs += [("fs_new_values", None, 2.5), ("fs_out", None, 1.0), ("fs_done", None, 1.0)]
    woven = []
    for order, chain in enumerate((fs, rw, fp)):
        total, at = sum(s[2] for s in chain), 0.0
        for step, n, time in chain:
            woven.append((at / total, order, len(woven), step, n))
            at += time
    return [(step, n) for _, _, _, step, n in sorted(woven, key=lambda s: s[:3])]


TURN = turn_steps()


def mix(nc, pb, C, keep, past, spare, dram):
    with Semaphores(nc) as sems, ExitStack() as ctx:
        sb = lambda n, s, d=F32: ctx.enter_context(nc.sbuf_tensor(n, s, d))
        sem = sems
        bank = [ctx.enter_context(nc.psum_tensor(f"m_bank{i}", [P, 512], F32)) for i in range(8)]
        room = spare[:].rearrange("p k n -> p (k n)")[:, 0:4 * NH * CH].rearrange("p (a h n) -> p a h n", a=2, h=NH)
        early = [sb(n, [P, 2, FT, CH]) for n in ("rw_exps", "rw_bk", "rw_cc_v")]
        late = [e[:].rearrange("p a f n -> p (a f) n") for e in early]
        buf = dict(bank=[bank[0][:], bank[1][:]], e1=early[0][:, 0], e3=early[0][:, 1], bf=early[1][:, 0], kf=early[1][:, 1],
                   cc=early[2][:, 0], vf=early[2][:, 1], tt=late[0], xt=late[1], x=late[2],
                   ar=sb("rw_ar", [P, FT, 2, CH]), ntg=room[:, 0], nkg=room[:, 1], rs=spare[:, DK - 1, TOK - 512:TOK],
                   bt=sb("rw_bt", [P, 512]), kt=sb("rw_kt", [P, 512]), vt=sb("rw_vt", [P, 512]), us=sb("rw_us", [P, 512]),
                   s_mid=sb("rw_s_mid", [P, FT, DH]), s=sb("rw_s", [P, FT, DH]))
        chunk = Rwkv(ctx, sems, nc, "", CH, 7, pb, C, keep, buf, False)
        zeroed, out = sem("m_zeroed"), sem("m_out")
        fp = FoxPrompt(ctx, sems, nc, pb, C, keep, [b[:] for b in bank[2:5]])
        fs = FoxSample(ctx, sems, nc, pb, C, keep, past, [b[:] for b in bank[5:8]], dram)
        block = ctx.enter_context(nc.Block())

        @block.sync
        def _(sp):
            fs.load_table(sp)
            with sp.Fori(0, NCH) as c:
                fs.load(sp, c)
            sp.wait_ge(chunk.done, 1 + NCH)
            sp.dma_start(dram["state_prompt"], buf["s"][:]).then_inc(out, 16)
            sp.wait_ge(out, 16)

        @block.gpsimd
        def _(pool):
            fs.seed(pool)
            with pool.Fori(0, NCH) as c:
                for step, n in TURN:
                    if step == "operands":
                        chunk.pool_v(pool, c)
                    if step == "fp_copy":
                        fp.pool(pool, c)

        @block.vector
        def _(dve):
            nc.vector.memset(buf["s"][:], 0.0).then_inc(zeroed, 1)
            chunk.seed(dve)
            fp.seed(dve)
            fs.seed_done(dve)
            dve.wait_ge(zeroed, 1)
            with dve.Fori(0, NCH) as c:
                for step, n in TURN:
                    if step == "operands":
                        chunk.dve_operands(dve, c)
                        chunk.dve_state_in(dve, c)
                    if step == "gram":
                        chunk.dve_gram(dve, c, n)
                    if step == "t":
                        chunk.dve_t(dve, c, *n)
                    if step == "xt":
                        chunk.dve_xt(dve, c, *n)
                    if step == "u":
                        chunk.dve_u(dve, c)
                    if step == "yd":
                        chunk.dve_yd(dve, c)
                    if step == "fp_in":
                        fp.dve_in(dve, c)
                    if step == "scores":
                        fp.dve_scores(dve, c, n)
                    if step == "normalise":
                        fp.dve_normalise(dve, c, n)
                    if step == "fs_scores":
                        fs.dve_scores(dve, c, n)
                    if step == "fs_max":
                        fs.dve_max(dve, c)
                    if step == "fs_turn" and n == 4:
                        fs.dve_inverse(dve, c)
                    if step == "fs_out":
                        fs.dve_normalise(dve, c)
                    if step == "fs_done":
                        fs.dve_out(dve, c)

        @block.scalar
        def _(act):
            act.wait_ge(fs.zeroed, 1)
            with act.Fori(0, NCH) as c:
                for step, n in TURN:
                    if step == "operands":
                        chunk.act_exps(act, c)
                    if step == "x":
                        chunk.act_x(act, c, *n)
                    if step == "r":
                        chunk.act_r(act, c)
                    if step == "fp_in":
                        fp.act_in(act, c)
                    if step == "exp":
                        fp.act_exp(act, c, n)
                    if step == "turn":
                        fp.act_turned(act, c, n)
                    if step == "fp_out":
                        fp.act_out(act, c)
                    if step == "fs_in":
                        fs.act_queries(act, c)
                    if step == "fs_exp":
                        fs.act_exp(act, c)
                    if step == "fs_turn":
                        fs.act_turned(act, c, n)

        @block.tensor
        def _(pe):
            with pe.Fori(0, NCH) as c:
                for step, n in TURN:
                    if step == "gram":
                        chunk.pe_gram(pe, c, n)
                    if step == "t":
                        chunk.pe_level(pe, c, *n)
                    if step == "xt":
                        chunk.pe_level_xt(pe, c, *n)
                    if step == "x":
                        chunk.pe_level_x(pe, c, *n)
                    if step == "r":
                        chunk.pe_r(pe, c)
                    if step == "u":
                        chunk.pe_u(pe, c)
                    if step == "yd":
                        chunk.pe_y(pe, c)
                        chunk.pe_d(pe, c)
                    if step == "fp_in":
                        fp.pe_in(pe, c)
                    if step == "scores":
                        fp.pe_scores(pe, c, n)
                    if step == "turn":
                        fp.pe_turn(pe, c, n)
                    if step == "values":
                        fp.pe_values(pe, c, n)
                    if step == "fs_new":
                        fs.pe_new(pe, c)
                    if step == "keys":
                        fs.pe_keys(pe, c, *n)
                    if step == "fs_turn":
                        fs.pe_turn(pe, c, n)
                    if step == "cached":
                        fs.pe_values(pe, c, *n)
                    if step == "fs_new_values":
                        fs.pe_new_values(pe)
                    if step == "fs_done":
                        fs.pe_out(pe, c)
    with Semaphores(nc) as sems, ExitStack() as ctx:
        sb = lambda n, s, d=F32: ctx.enter_context(nc.sbuf_tensor(n, s, d))
        sem = sems
        bank = [ctx.enter_context(nc.psum_tensor(f"s_bank{i}", [P, 512], F32)) for i in range(2)]
        T = NB * NT
        buf = dict(bank=[bank[0][:], bank[1][:]],
                   cc=sb("sw_cc", [P, FT, T]), e1=sb("sw_e1", [P, FT, T]), e3=sb("sw_e3", [P, FT, T]),
                   ar=sb("sw_ar", [P, FT, 2, T]), bf=sb("sw_bf", [P, FT, T]), kf=sb("sw_kf", [P, FT, T]),
                   vf=sb("sw_vf", [P, FT, T]), bt=sb("sw_bt", [P, 512]), kt=sb("sw_kt", [P, 512]), vt=sb("sw_vt", [P, 512]),
                   ntg=sb("sw_ntg", [P, NH, 2 * T]), nkg=sb("sw_nkg", [P, NH, 2 * T]),
                   x=sb("sw_x", [P, NH, T]), xt=sb("sw_xt", [P, NH, T]), tt=sb("sw_tt", [P, NH, T]),
                   rs=sb("sw_rs", [P, 512]), us=sb("sw_us", [P, 512]), s0=sb("sw_s0", [P, FT, NB, DH]),
                   sa=sb("sw_sa", [P, FT, 2, T]), ux=sb("sw_ux", [P, 2, 2, 512]), vx=sb("sw_vx", [P, 2, 2, 512]),
                   s_loaded=sem("sw_s_loaded"), x_part=sem("sw_x_part"), v_part=sem("sw_v_part"), y_taken=sem("sw_y_taken"), s_added=sem("sw_s_added"))
        sample = Rwkv(ctx, sems, nc, "_s", T, 3, pb, C, keep, buf, True)
        out = sem("s_out")
        block = ctx.enter_context(nc.Block())

        @block.sync
        def _(sp):
            sp.dma_start(buf["s0"][:], dram["state_in"]).then_inc(sample.s_loaded, 16)
            for f in range(FT):
                sp.wait_ge(sample.done, 2 + f)
                sp.dma_start(dram["state_sample"][:, f], buf["s0"][:, f]).then_inc(out, 16)
            sp.wait_ge(out, 16 * FT)

        @block.gpsimd
        def _(pool):
            sample.pool_v(pool, 0)
            sample.pool_sample(pool)

        @block.vector
        def _(dve):
            sample.seed(dve)
            sample.dve_operands(dve, 0)
            for n in range(sample.rounds):
                sample.dve_gram(dve, 0, n)
            for level in range(3):
                for bt in range(2):
                    sample.dve_t(dve, 0, level, bt)
                for bt in range(2):
                    sample.dve_xt(dve, 0, level, bt)
            dve.wait_ge(sample.s_loaded, 16)
            sample.dve_sample(dve)

        @block.scalar
        def _(act):
            sample.act_exps(act, 0)
            for level in range(2):
                for bt in range(2):
                    sample.act_x(act, 0, level, bt)
            sample.act_sample(act)

        @block.tensor
        def _(pe):
            for n in range(sample.rounds):
                sample.pe_gram(pe, 0, n)
            for level in range(3):
                for bt in range(2):
                    sample.pe_level(pe, 0, level, bt)
                for bt in range(2):
                    sample.pe_level_xt(pe, 0, level, bt)
                if level < 2:
                    for bt in range(2):
                        sample.pe_level_x(pe, 0, level, bt)
            sample.pe_sample(pe)


def finish_mixers(sems, nc, dense, outs, x, pb, C, dram, w_o, ya, yb):
    with ExitStack() as ctx:
        sb = lambda n, s, d=F32: ctx.enter_context(nc.sbuf_tensor(n, s, d))
        sem = sems
        ps = dense.ps
        par, rk8 = C["par"], pb[:, RK0]
        g2, sq, bonus = sb("d_g2", [P, 512]), sb("d_sq", [P, 2, TOK]), sb("d_bonus", [P, FT, TOK])
        mean, rstd = sb("d_mean", [P, TOK]), sb("d_rstd", [P, TOK])
        loaded, cleared, sum_mm, mean_ev, mean_mm, centred = (
            sem("d_loaded"), sem("d_cleared"), sem("d_sum_mm"), sem("d_mean_ev"), sem("d_mean_mm"), sem("d_centred"))
        squared, sq_mm, rooted, inverted = sem("d_squared"), sem("d_sq_mm"), sem("d_rooted"), sem("d_inverted")
        bonus_mm, bonus_ev, gate_mm, rstd_mm = sem("d_bonus_mm"), sem("d_bonus_ev"), sem("d_gate_mm"), sem("d_rstd_mm")
        scaled, shifted, gated, high, x_in = sem("d_scaled"), sem("d_shifted"), sem("d_gated"), sem("d_high"), sem("d_x_in")
        sel8 = C["sel8"].rearrange("p (f h) -> p f h", f=FT)
        selt8 = C["selt8"].rearrange("p (f n) -> p f n", f=FT)
        cut = lambda half: slice(half * HALF, half * HALF + HALF)
        y = lambda f: pb[:, R0 + f]
        block = ctx.enter_context(nc.Block())

        @block.sync
        def _(sp):
            sp.dma_start(g2[:], dram["g2"]).then_inc(loaded, 16)
            dense.load(sp, (outs[0], 4), FT, lambda n: w_o[n:n + 1].rearrange("a p k n -> p (a k) n"))
            sp.dma_start(x[:], dram["x_saved"]).then_inc(x_in, 16)
            sp.wait_ge(x_in, 16)

        @block.tensor
        def _(pe):
            def product(slot, weights, moving, rows=P, start=True, stop=True):
                for half in range(2):
                    mm = nc.tensor.matmul(ps[0:rows, slot, half, 0:HALF], weights, moving[:, cut(half)], start=start, stop=stop)
                return mm
            for f in range(FT):
                mm = product(3, sel8[:, f], y(f), NH, f == 0, f == FT - 1)
            mm.then_inc(sum_mm, 1)
            pe.wait_ge(mean_ev, 1)
            for f in range(FT):
                product(f, selt8[:, f], mean).then_inc(mean_mm, 1)
            for f in range(FT):
                pe.wait_ge(centred, f + 1)
                if f == 3:
                    pe.wait_ge(bonus_ev, 1)
                product(f % 3, selt8[:, f], rk8).then_inc(bonus_mm, 1)
            for f in range(FT):
                pe.wait_ge(squared, f + 1)
                product(3, sel8[:, f], sq[:, f % 2], NH, f == 0, f == FT - 1).then_inc(sq_mm, 1)
            pe.wait_ge(loaded, 16)
            pe.wait_ge(bonus_ev, FT)
            for f in range(FT):
                if f >= 2:
                    pe.wait_ge(gated, f - 1)
                product(2 * f % 4, g2[:, f * P:f * P + P], pb[:, LG0]).then_inc(gate_mm, 1)
                if f == 0:
                    pe.wait_ge(inverted, 1)
                if f >= 2:
                    pe.wait_ge(scaled, f - 1)
                product((2 * f + 1) % 4, selt8[:, f], rstd).then_inc(rstd_mm, 1)

        @block.scalar
        def _(act):
            for f in range(FT):
                nc.scalar.activation(yb[0][:, f], pb[:, FQ0 + f], ACT.Copy).then_inc(high, 1)
            act.wait_ge(cleared, 1)
            act.wait_ge(sum_mm, 1)
            nc.scalar.activation(halves(mean[0:NH]), ps[0:NH, 3, :, 0:HALF], ACT.Copy, scale=1.0 / DH).then_inc(mean_ev, 1)
            for f in range(FT):
                act.wait_ge(centred, f + 1)
                if f >= 2:
                    act.wait_ge(sq_mm, f - 1)
                nc.scalar.activation(sq[:, f % 2], y(f), ACT.Square).then_inc(squared, 1)
            act.wait_ge(sq_mm, FT)
            nc.scalar.activation(halves(rstd[0:NH]), ps[0:NH, 3, :, 0:HALF], ACT.Sqrt, scale=1.0 / DH,
                                 bias=C["lnx_eps"]).then_inc(rooted, 1)
            for f in range(FT):
                act.wait_ge(gated, f + 1)
                nc.scalar.activation(ya[0][:, f], y(f), ACT.Copy).then_inc(high, 1)

        @block.gpsimd
        def _(pool):
            for f in range(FT):
                pool.wait_ge(high, f + 1)
                nc.gpsimd.tensor_tensor(yb[1][:, f], pb[:, FQ0 + f], yb[0][:, f].bitcast(F32), ALU.subtract)
            for f in range(FT):
                pool.wait_ge(high, FT + f + 1)
                nc.gpsimd.tensor_tensor(ya[1][:, f], y(f), ya[0][:, f].bitcast(F32), ALU.subtract)

        @block.vector
        def _(dve):
            nc.vector.memset(mean[:], 0.0)
            nc.vector.memset(rstd[:], 0.0).then_inc(cleared, 1)
            for f in range(FT):
                dve.wait_ge(mean_mm, f + 1)
                nc.vector.tensor_tensor(halves(y(f)), halves(y(f)), ps[:, f, :, 0:HALF], ALU.subtract).then_inc(centred, 1)
            for f in range(FT):
                dve.wait_ge(bonus_mm, f + 1)
                nc.vector.tensor_tensor(halves(bonus[:, f]), halves(pb[:, V0 + f]), ps[:, f % 3, :, 0:HALF],
                                        ALU.mult).then_inc(bonus_ev, 1)
            dense.split(dve, (outs[0], 2), FT)
            dve.wait_ge(rooted, 1)
            nc.vector.reciprocal(rstd[0:NH], rstd[0:NH]).then_inc(inverted, 1)
            dve.wait_ge(bonus_ev, FT)
            for f in range(FT):
                dve.wait_ge(rstd_mm, f + 1)
                nc.vector.scalar_tensor_tensor(halves(y(f)), halves(y(f)), par("lnw", f), ps[:, (2 * f + 1) % 4, :, 0:HALF],
                                               ALU.mult, ALU.mult).then_inc(scaled, 1)
                dve.wait_ge(scaled, f + 1)
                nc.vector.scalar_tensor_tensor(y(f), y(f), par("lnb", f), bonus[:, f], ALU.add, ALU.add).then_inc(shifted, 1)
                dve.wait_ge(shifted, f + 1)
                dve.wait_ge(gate_mm, f + 1)
                nc.vector.tensor_tensor(halves(y(f)), halves(y(f)), ps[:, 2 * f % 4, :, 0:HALF], ALU.mult).then_inc(gated, 1)


def merge(sems, nc, dense, outs, x, pb, dram, ya, yb, w_o, w_out):
    with ExitStack() as ctx:
        sb = lambda n, s, d=F32: ctx.enter_context(nc.sbuf_tensor(n, s, d))
        sem = sems
        gates = pb[:, 8:12].rearrange("p (b a) n -> p b a n", b=2)
        prod = pb[:, 12:16].rearrange("p (b a) n -> p b a n", b=2)
        y = pb[:, 16:18]
        mh, ml = sb("e_mh", [P, DK, TOK], F32R), sb("e_ml", [P, DK, TOK], F32R)
        gate_in = [sem("e_gate_in0"), sem("e_gate_in1")]
        added, merged, high, y_added = sem("e_added"), sem("e_merged"), sem("e_high"), sem("e_y_added")
        proj = dense.stage(DK)
        block = ctx.enter_context(nc.Block())

        @block.sync
        def _(sp):
            dense.load(sp, (outs[0] + 4, outs[1] - 4), FT, lambda n: w_o[4:][bass.ds(n, 1)].rearrange("a p k n -> p (a k) n"))
            dense.load(sp, proj, DK, lambda n: w_out[bass.ds(n, 1)].rearrange("a p k n -> p (a k) n"))

        @block.vector
        def _(dve):
            def product(slot, i, twin, odd):
                dve.wait_ge(gate_in[twin], 16 * i + 16)
                nc.vector.tensor_tensor(halves(prod[:, twin, odd]), dense.ps[:, slot, :, 0:HALF],
                                        halves(gates[:, twin, odd]), ALU.mult).then_inc(dense.evacuated, 1)
            turns = DK // 2 - 1
            with dve.Fori(0, turns) as i:
                for j in range(4):
                    t = Tile(outs[0] + 2, i, j)
                    dense.split_tile(dve, t, FT)
                    product((t.slot + 2) % 4, i, j // 2, j % 2)
            for j in range(4):
                t = Tile(outs[0] + 2, turns, j)
                dense.split_tile(dve, t, FT if j < 2 else DK)
                product((t.slot + 2) % 4, turns, j // 2, j % 2)
            dense.split(dve, (proj[0] + 2, proj[1] - 2), DK)

        @block.scalar
        def _(act):
            src = dram["gates"].rearrange("(a n) p m -> n p a m", a=2)
            for n in range(DK + 2):
                if n >= 2:
                    act.wait_ge(added, n - 1)
                    nc.scalar.activation(mh[:, n - 2], prod[:, n % 2, 0], ACT.Copy).then_inc(high, 1)
                if 2 <= n < DK:
                    act.wait_ge(merged, n - 1)
                if n < DK:
                    act.dma_start(gates[:, n % 2], src[n]).then_inc(gate_in[n % 2], 16)
            for t in tiles(act, *proj):
                act.wait_ge(dense.mm_done, t.t + 5)
                act.wait_ge(y_added, t.n + 1)
                nc.scalar.activation(halves(y[:, t.odd]), dense.out(t), ACT.Copy).then_inc(dense.evacuated, 1)

        @block.gpsimd
        def _(pool):
            pool.nop().then_inc(y_added, 2)
            with pool.Fori(0, DK // 2) as i:
                for b in range(2):
                    n = 2 * i + b
                    pool.wait_ge(dense.evacuated, outs[0] + 2 * n + 6)
                    one = prod[:, b, 0:1]
                    nc.gpsimd.tensor_tensor(one, one, prod[:, b, 1:2], ALU.add).then_inc(added, 1)
                    pool.wait_ge(high, n + 1)
                    nc.gpsimd.tensor_tensor(ml[:, bass.ds(n, 1)], one, mh[:, bass.ds(n, 1)].bitcast(F32), ALU.subtract)\
                        .then_inc(merged, 1)
            for t in tiles(pool, *proj):
                pool.wait_ge(dense.evacuated, t.t + 5)
                xn = x[:, bass.ds(t.n, 1)]
                nc.gpsimd.tensor_tensor(xn, y[:, t.odd:t.odd + 1], xn, ALU.add).then_inc(y_added, 1)

        @block.tensor
        def _(pe):
            def branch(t):
                hi, lo = yb if t.odd else ya
                return dense.whole(hi, lo, FT)(t)
            dense.multiply(pe, outs, branch)
            dense.multiply(pe, proj, dense.whole(mh, ml, DK), 1, lambda k: pe.wait_ge(merged, k + 1))


def build(nc, a, o):
    with ExitStack() as top:
        sb = lambda n, s, d=F32: top.enter_context(nc.sbuf_tensor(n, s, d))
        dense = Dense(Semaphores(nc), nc)
        cc, pars = sb("t_consts", [P, N_CCOL]), sb("t_params", [P, N_PCOL])
        ones, minus, eps = sb("t_ones", [P, P]), sb("t_minus", [P, P]), sb("t_eps", [P, 2])
        x = sb("t_x", [P, DK, TOK])
        C = {n: cc[:, CCOL[n]:CCOL[n] + w] for n, w in CC_COLS.items()}
        C["par"] = lambda n, i=0, rows=P: pars[0:rows, PCOL[n] + i:PCOL[n] + i + 1]
        C.update(ones=ones[:], minus=minus[:], eps=eps[:, 0:1], lnx_eps=eps[0:NH, 1:2])
        gain = lambda n: pars[:, PCOL[n]:PCOL[n] + DK]
        loaded = dict(x=[nc.alloc_semaphore(name="t_x0_in"), nc.alloc_semaphore(name="t_x1_in")],
                      rest=nc.alloc_semaphore(name="t_rest_in"))
        with nc.Block() as block:
            @block.vector
            def _(dve):
                nc.vector.memset(ones[:], 1.0)
                nc.vector.memset(minus[:], -1.0)
                nc.vector.memset(eps[:, 0:1], NORM_EPS)
                nc.vector.memset(eps[:, 1:2], LNX_EPS)

            @block.sync
            def _(sp):
                dense.seed(sp)
                for part in range(2):
                    k = slice(DK // 2 * part, DK // 2 * part + DK // 2)
                    sp.dma_start(x[:, k], a["x"][:, k]).then_inc(loaded["x"][part], 16)

            @block.scalar
            def _(act):
                act.dma_start(pars[:], a["params"]).then_inc(loaded["rest"], 16)
                act.dma_start(cc[:], a["c1"]).then_inc(loaded["rest"], 16)

        with Semaphores(nc) as sems:
            ffn(sems, nc, dense, "_1", x, gain("n1"), C, a["up1"], [a["down1a"], a["down1b"]], loaded)

        gates = nc.dram_tensor("gates_saved", [N_GATE, P, TOK], F32, kind="Internal").ap()
        later = nc.dram_tensor("later_saved", [NB * NH, PAST], F32, kind="Internal").ap()
        x_saved = nc.dram_tensor("x_saved", [P, DK, TOK], F32, kind="Internal").ap()
        with ExitStack() as mid:
            pb = mid.enter_context(nc.sbuf_tensor("t_pb", [P, N_P, TOK], F32))
            past = mid.enter_context(nc.sbuf_tensor("t_past", [P, PAST + 64], F32))
            with Semaphores(nc) as sems:
                project(sems, nc, dense, x, gain("n2"), C, a["w_in"], pb, gates, x_saved, past, a["table"], a["logf"])
            with ExitStack() as kept:
                kb = lambda n, s: kept.enter_context(nc.sbuf_tensor("k_" + n, s, F32))
                keep = {n: kb(n, s) for n, s in dict(
                    cum=[P, FT, TOK], kk=[P, FT, TOK], kka=[P, FT, TOK], newb=[P, NCH, 64],
                    mid=[P, FT, NCH], mexp=[P, 3, FT, NCH], vn=[64, FT * P]
                    ).items()}
                with Semaphores(nc) as sems:
                    prepare(sems, nc, pb, C, keep, past, dict(later=later, lora=a["lora"], shift_in=a["shift"], c2=a["c2"], v_out=o["v"],
                                                        k_out=o["k"], shift_out=o["shift"], logf_out=o["logf"]))
                mix(nc, pb, C, keep, past, x, dict(later=later, table=a["table"], keys=a["keys"], values=a["values"], state_in=a["state"],
                                             state_prompt=o["state_prompt"], state_sample=o["state_sample"]))
            fb = lambda n: mid.enter_context(nc.sbuf_tensor(n, [P, FT, TOK], F32R))
            ya, yb = (fb("t_ya_hi"), fb("t_ya_lo")), (fb("t_yb_hi"), fb("t_yb_lo"))
            dense.buffers(mid, "_m", DK)
            outs = dense.stage(2 * DK)
            with Semaphores(nc) as sems:
                finish_mixers(sems, nc, dense, outs, x, pb, C, dict(g2=a["g2"], x_saved=x_saved), a["w_o"], ya, yb)
            with Semaphores(nc) as sems:
                merge(sems, nc, dense, outs, x, pb, dict(gates=gates), ya, yb, a["w_o"], a["w_out"])
        with Semaphores(nc) as sems:
            ffn(sems, nc, dense, "_2", x, gain("n3"), C, a["up2"], [a["down2a"], a["down2b"]],
                out=o["x"])


def constants():
    s, t = np.arange(P)[:, None], np.arange(P)[None, :]
    f = lambda m: np.asarray(m, np.float32)
    c = {"ident": f(s == t), "low": f(np.concatenate([s < t, s <= t], 1))}
    same = (s // NT == t // NT)[:64, :64]
    lows = np.concatenate([same & (s < t)[:64, :64], same & (s <= t)[:64, :64]], 1)
    c["lows"] = np.concatenate([f(lows), np.zeros((64, P), np.float32)])
    c["lev"] = f(np.concatenate([(s // (2 * b) == t // (2 * b)) & (s // b % 2 == 1) & (t // b % 2 == 0)
                                 for b in (1, 2, 4, 8, 16, 32, 64)], 1))
    c["causal"] = np.where(t > s, np.float32(NEG), np.float32(0))
    k, h, step = s // 64, s // NT % NH, s % NT
    key = np.arange(64)[None, :]
    seen = [(key // NT == 2 * turn + k) & (key % NT <= step) for turn in range(NCH)]
    c["bmask"] = f(s // NT == np.arange(NB)[None, :])
    head = lambda ft, n, at: f(np.arange(n)[None, :] == at + 2 * ft + s // DH)
    c["sel8"] = np.concatenate([head(ft, NH, 0) for ft in range(FT)], 1)
    pad = lambda m: np.concatenate([m, np.zeros((P - m.shape[0], m.shape[1]), np.float32)])
    c["selt8"] = np.concatenate([pad(head(ft, NH, 0).T) for ft in range(FT)], 1)
    col = np.arange(TOK)[None, :]
    start = (col - SEQ) % NT == 0
    c2 = {"sel24": np.concatenate([head(i % FT, 24, 8 * (i // FT)) for i in range(12)], 1),
          "selt": np.concatenate([pad(head(i % FT, 24, 8 * (i // FT)).T) for i in range(12)], 1),
          "reset": np.tile(f(~np.where(col < SEQ, col % CH == 0, start)), (P, 1)),
          "fresh": np.tile(f(~np.where(col < SEQ, col == 0, start)), (P, 1)),
          "mnew": np.where(np.concatenate(seen, 1), np.float32(0), np.float32(NEG)),
          "nsel": pad(-f(h == np.arange(NH)[None, :]).T)}
    pack = lambda d, widths: np.ascontiguousarray(np.concatenate([d[n] for n in widths], 1))
    return pack(c, CC_COLS), pack(c2, CC2_COLS)


def weight_tiles(w):
    k, n = w.shape
    return w.reshape(k // P, P, n // P, P).transpose(2, 1, 0, 3)


def columns_of(v):
    return v.reshape(-1, P).T


def kernel(x_prompt, x_sample, cache_k, cache_v, cache_logf, state_wkv, state_shift, page_table,
           ffn1_norm, ffn1_wg, ffn1_wu, ffn1_wd, mix_norm, w_in, shift_mu,
           rwkv_w0, rwkv_w2, rwkv_a0, rwkv_a2, rwkv_g2, rwkv_k_k, rwkv_k_a, rwkv_r_k, rwkv_lnx_w, rwkv_lnx_b,
           fox_b_f, fox_q_norm, fox_k_norm, w_o_a, w_o_b, w_out,
           ffn2_norm, ffn2_wg, ffn2_wu, ffn2_wd):
    import concourse.bacc as bacc
    from concourse.bass_utils import run_bass_kernel_spmd

    A = lambda v: np.asarray(v)
    arrays = {}

    def put(name, v):
        arrays[name] = np.ascontiguousarray(v)

    x = np.concatenate([A(x_prompt)[0], A(x_sample).reshape(NB * NT, D)])
    put("x", x.T.reshape(DK, P, TOK).transpose(1, 0, 2))
    for n, wg, wu, wd in (("1", ffn1_wg, ffn1_wu, ffn1_wd), ("2", ffn2_wg, ffn2_wu, ffn2_wd)):
        up = np.stack([weight_tiles(A(wg)[0]), weight_tiles(A(wu)[0])], 1)
        put("up" + n, up.reshape(2 * sum(UP), P, DK, P))
        put(f"down{n}a", weight_tiles(A(wd)[0][:UP[0] * P]))
        put(f"down{n}b", weight_tiles(A(wd)[0][UP[0] * P:]))
    w = A(w_in)[0]
    f0 = (N_P - 1) * P
    w = np.concatenate([w[:, :f0 + NH], np.zeros((D, P - NH), w.dtype), w[:, f0 + NH:]], 1)
    put("w_in", weight_tiles(w))
    put("w_o", np.stack([weight_tiles(A(w_o_a)[0]), weight_tiles(A(w_o_b)[0])], 1).reshape(2 * DK, P, FT, P))
    put("w_out", weight_tiles(A(w_out)[0]))
    zero = np.zeros_like(A(rwkv_w2)[0])
    put("lora", np.stack([np.concatenate([A(rwkv_w2)[0], zero]), np.concatenate([zero, A(rwkv_a2)[0]])], 1))
    put("g2", A(rwkv_g2)[0])
    put("shift", A(state_shift)[0].T.reshape(N_SH, P, NB).transpose(1, 0, 2))
    put("state", A(state_wkv)[0].transpose(1, 3, 0, 2).reshape(FT, P, NB, DH).transpose(1, 0, 2, 3))
    put("table", A(page_table).reshape(1, -1))
    back = lambda v: A(v)[0][:, ::-1]
    put("keys", back(cache_k).reshape(NPOOL, PAGE, FT, 2 * DH).transpose(0, 3, 2, 1).reshape(NPOOL, P, FT * PAGE))
    put("values", back(cache_v).reshape(NPOOL, PAGE, NH * DH))
    put("logf", back(cache_logf).transpose(0, 2, 1))
    fill = lambda v, n: np.concatenate([v, np.zeros(P - n, np.float32)])
    stat = lambda p, q: np.concatenate([np.full(16, p, np.float32), np.full(8, q, np.float32)])
    cols = dict(n1=A(ffn1_norm)[0], n2=A(mix_norm)[0], n3=A(ffn2_norm)[0], mu=A(shift_mu)[0], w0=A(rwkv_w0)[0],
                a0=A(rwkv_a0)[0], kk=A(rwkv_k_k)[0], ka=A(rwkv_k_a)[0], rk=A(rwkv_r_k)[0].reshape(-1),
                lnw=A(rwkv_lnx_w)[0], lnb=A(rwkv_lnx_b)[0], qn=np.tile(A(fox_q_norm)[0], 2), kn=np.tile(A(fox_k_norm)[0], 2),
                bf=fill(A(fox_b_f)[0], NH), sc=fill(stat(1 / DH, 1), 24), ad=fill(stat(NORM_EPS, 0), 24))
    put("params", np.concatenate([columns_of(cols[n]) for n in PC_COLS], 1))
    c1, c2 = constants()
    put("c1", c1)
    put("c2", c2)

    outs = dict(x=(P, DK, TOK), k=(P, FT, TOK), v=(P, FT, TOK), logf=(NH, TOK), shift=(P, N_SH, 1 + NB),
                state_prompt=(P, FT, DH), state_sample=(P, FT, NB, DH))
    nc = bacc.Bacc("TRN2", target_bir_lowering=False, num_devices=1)
    a = {n: nc.dram_tensor("in_" + n, v.shape, mybir.dt.from_np(v.dtype), kind="ExternalInput").ap() for n, v in arrays.items()}
    o = {n: nc.dram_tensor("out_" + n, s, F32, kind="ExternalOutput").ap() for n, s in outs.items()}
    build(nc, a, o)
    r = run_bass_kernel_spmd(nc, [{"in_" + n: v for n, v in arrays.items()}], core_ids=[0]).results[0]
    r = {n: np.asarray(r["out_" + n]) for n in outs}

    rows = lambda v: v.transpose(2, 1, 0).reshape(v.shape[2], -1)
    xo, ko, vo, sh = rows(r["x"]), rows(r["k"]), rows(r["v"]), rows(r["shift"])
    lf = r["logf"].T
    p = lambda v, *s: np.ascontiguousarray(v[:SEQ]).reshape(1, 1, SEQ, *s)
    q = lambda v, *s: np.ascontiguousarray(v[SEQ:]).reshape(1, NB, NT, *s)
    sp = r["state_prompt"].reshape(2, DH, FT, 1, DH).transpose(3, 2, 0, 4, 1).reshape(1, 1, NH, DH, DH)
    ss = r["state_sample"].reshape(2, DH, FT, NB, DH).transpose(3, 2, 0, 4, 1).reshape(1, NB, NH, DH, DH)
    return (np.ascontiguousarray(xo[:SEQ])[None], np.ascontiguousarray(xo[SEQ:]).reshape(NB, NT, D),
            p(ko, NH, DH), p(vo, NH, DH), p(lf, NH), np.ascontiguousarray(sp), np.ascontiguousarray(sh[:1])[None],
            q(ko, NH, DH), q(vo, NH, DH), q(lf, NH), np.ascontiguousarray(ss), np.ascontiguousarray(sh[1:])[None])
```
